# Optimizing a Trainium2 kernel written in Bass

```python
import math
import jax, jax.numpy as jnp
from jax import lax
import numpy as np

D_MODEL = 1024
BATCH = 1
SEQ = 256
DEPTH = 2

D_MIX = D_MODEL
HG_HEADS = 4
HG_WIDTH = D_MIX // 4
HG_HEAD_DIM = HG_WIDTH // HG_HEADS
HG_KEY_DIM = 64
HG_CHUNK = 16
LRU_WIDTH = D_MIX // 4
LRU_BLOCKS = 4
LRU_BLOCK_DIM = LRU_WIDTH // LRU_BLOCKS
CONV_WIDTH = 4
LRU_C = 8.0
DA_WIDTH = D_MIX - HG_WIDTH - LRU_WIDTH
DA_HEADS = 4
DA_HEAD_DIM = DA_WIDTH // (2 * DA_HEADS)
Q_BLOCK = 128
D_FF = 3584
N_EXPERTS = 8
TOP_K = 2
N_DENSE = (DEPTH + 1) // 2
N_MOE = DEPTH // 2
DN_ALPHA = (2.0 * DEPTH) ** 0.25
DN_BETA = (8.0 * DEPTH) ** -0.25
EPS = 1e-5
PROJ_SIZES = (HG_HEADS * HG_KEY_DIM, HG_HEADS * HG_KEY_DIM, HG_WIDTH, HG_WIDTH,
              LRU_WIDTH, LRU_WIDTH, DA_WIDTH, DA_WIDTH, DA_WIDTH)
PROJ_SPLITS = tuple(sum(PROJ_SIZES[:i + 1]) for i in range(len(PROJ_SIZES) - 1))
D_PROJ = sum(PROJ_SIZES)

kernel_name = 'hybrid_hgrn2_rglru_diffattn_moe_deepnorm'

def _layer_norm(x, g, b):
    xf = x.astype(jnp.float32)
    mu = jnp.mean(xf, axis=-1, keepdims=True)
    var = jnp.mean(jnp.square(xf - mu), axis=-1, keepdims=True)
    y = (xf - mu) * lax.rsqrt(var + EPS) * g.astype(jnp.float32) + b.astype(jnp.float32)
    return y.astype(x.dtype)

def _rms_heads(x, g, n_heads):
    B, S, W = x.shape
    xf = x.astype(jnp.float32).reshape(B, S, n_heads, W // n_heads)
    xf = xf * lax.rsqrt(jnp.mean(jnp.square(xf), axis=-1, keepdims=True) + EPS)
    return xf.reshape(B, S, W) * g.astype(jnp.float32)

def _hgrn2(q_raw, f_raw, i_raw, g_raw, lb, norm_g):
    B, S, _ = q_raw.shape
    H, DK, DV, C = HG_HEADS, HG_KEY_DIM, HG_HEAD_DIM, HG_CHUNK
    N = S // C
    z = f_raw.astype(jnp.float32)
    lbv = lb.astype(jnp.float32)
    logf = jnp.log(lbv + (1.0 - lbv) * jax.nn.sigmoid(z))
    k = (1.0 - lbv) * jax.nn.sigmoid(-z)
    q = jax.nn.silu(q_raw.astype(jnp.float32))
    v = i_raw.astype(jnp.float32)

    def to_chunks(t, d):
        return t.reshape(B, N, C, H, d).transpose(0, 3, 1, 2, 4)

    q, logf, k, v = to_chunks(q, DK), to_chunks(logf, DK), to_chunks(k, DK), to_chunks(v, DV)
    b = jnp.cumsum(logf, axis=3)
    causal = jnp.tril(jnp.ones((C, C), dtype=bool))[:, :, None]
    rel = b[:, :, :, :, None, :] - b[:, :, :, None, :, :]
    decay = jnp.exp(jnp.where(causal, rel, -jnp.inf))
    scores = jnp.einsum('bhntk,bhnsk,bhntsk->bhnts', q, k, decay)
    o_intra = jnp.einsum('bhnts,bhnsv->bhntv', scores, v)
    b_last = b[:, :, :, -1:, :]
    u = jnp.einsum('bhnsk,bhnsv->bhnkv', k * jnp.exp(b_last - b), v)
    chunk_decay = jnp.exp(b_last[:, :, :, 0, :])

    def step(state, inp):
        d_n, u_n = inp
        return d_n[..., None] * state + u_n, state

    _, s_in = lax.scan(step, jnp.zeros((B, H, DK, DV), jnp.float32),
                       (jnp.moveaxis(chunk_decay, 2, 0), jnp.moveaxis(u, 2, 0)))
    s_in = jnp.moveaxis(s_in, 0, 2)
    o_inter = jnp.einsum('bhntk,bhnkv->bhntv', q * jnp.exp(b), s_in)
    o = (o_intra + o_inter).transpose(0, 2, 3, 1, 4).reshape(B, S, H * DV)
    return _rms_heads(o, norm_g, H) * jax.nn.silu(g_raw.astype(jnp.float32))

def _linear_combine(c1, c2):
    a1, b1 = c1
    a2, b2 = c2
    return a1 * a2, a2 * b1 + b2

def _rglru_block(x_raw, gate_raw, conv_w, conv_b, wa, ba, wx, bx, lam):
    B, S, W = x_raw.shape
    xc = lax.conv_general_dilated(x_raw, conv_w[:, None, :], window_strides=(1,),
                                  padding=[(CONV_WIDTH - 1, 0)],
                                  dimension_numbers=('NWC', 'WIO', 'NWC'),
                                  feature_group_count=W) + conv_b
    xb = xc.reshape(B, S, LRU_BLOCKS, LRU_BLOCK_DIM)
    r = jax.nn.sigmoid((jnp.einsum('bsgi,gij->bsgj', xb, wa).reshape(B, S, W) + ba).astype(jnp.float32))
    i = jax.nn.sigmoid((jnp.einsum('bsgi,gij->bsgj', xb, wx).reshape(B, S, W) + bx).astype(jnp.float32))
    log_a = LRU_C * r * jax.nn.log_sigmoid(lam.astype(jnp.float32))
    a = jnp.exp(log_a)
    u = jnp.sqrt(-jnp.expm1(2.0 * log_a)) * i * xc.astype(jnp.float32)
    _, h = lax.associative_scan(_linear_combine, (a, u), axis=1)
    return h * jax.nn.gelu(gate_raw.astype(jnp.float32))

def _diff_attention(q_raw, k_raw, v_raw, lq1, lk1, lq2, lk2, norm_g, layer):
    B, S, _ = q_raw.shape
    H, d = DA_HEADS, DA_HEAD_DIM
    lam_init = 0.8 - 0.6 * math.exp(-0.3 * layer)
    lam = (jnp.exp(jnp.sum(lq1.astype(jnp.float32) * lk1.astype(jnp.float32)))
           - jnp.exp(jnp.sum(lq2.astype(jnp.float32) * lk2.astype(jnp.float32))) + lam_init)
    q = q_raw.reshape(B, S, H, 2, d).transpose(0, 2, 3, 1, 4)
    k = k_raw.reshape(B, S, H, 2, d).transpose(0, 2, 3, 1, 4)
    v = v_raw.reshape(B, S, H, 2 * d).transpose(0, 2, 1, 3)
    scale = d ** -0.5
    outs = []
    for blk in range(S // Q_BLOCK):
        s0 = blk * Q_BLOCK
        s1 = s0 + Q_BLOCK
        sc = jnp.einsum('bhcqd,bhckd->bhcqk', q[:, :, :, s0:s1], k[:, :, :, :s1]).astype(jnp.float32) * scale
        mask = jnp.arange(s1)[None, :] <= (s0 + jnp.arange(Q_BLOCK))[:, None]
        p = jax.nn.softmax(jnp.where(mask, sc, -jnp.inf), axis=-1)
        w = p[:, :, 0] - lam * p[:, :, 1]
        outs.append(jnp.einsum('bhqk,bhkv->bhqv', w.astype(v.dtype), v[:, :, :s1]))
    o = jnp.concatenate(outs, axis=2).transpose(0, 2, 1, 3).reshape(B, S, H * 2 * d)
    return _rms_heads(o, norm_g, H) * (1.0 - lam_init)

def _mixer(x, w_in, w_out, lb, hg_norm_g, conv_w, conv_b, wa, ba, wx, bx, lru_lambda,
           lq1, lk1, lq2, lk2, da_norm_g, layer):
    proj = x @ w_in
    hq, hf, hi, hg, lx, lg, dq, dk, dv = jnp.split(proj, PROJ_SPLITS, axis=-1)
    o_hg = _hgrn2(hq, hf, hi, hg, lb, hg_norm_g)
    o_lru = _rglru_block(lx, lg, conv_w, conv_b, wa, ba, wx, bx, lru_lambda)
    o_da = _diff_attention(dq, dk, dv, lq1, lk1, lq2, lk2, da_norm_g, layer)
    o = jnp.concatenate([o_hg, o_lru, o_da], axis=-1).astype(x.dtype)
    return o @ w_out

def _swiglu(x, wg, wu, wd):
    return (jax.nn.silu(x @ wg) * (x @ wu)) @ wd

def _moe(x, router_w, wg, wu, wd):
    B, S, D = x.shape
    xf = x.reshape(B * S, D)
    logits = (xf @ router_w).astype(jnp.float32)
    top_v, top_i = lax.top_k(logits, TOP_K)
    gates = jax.nn.softmax(top_v, axis=-1)
    combine = jnp.sum(jax.nn.one_hot(top_i, N_EXPERTS, dtype=jnp.float32) * gates[..., None], axis=1)
    y = jnp.zeros_like(xf)
    for e in range(N_EXPERTS):
        y = y + combine[:, e:e + 1].astype(x.dtype) * _swiglu(xf, wg[e], wu[e], wd[e])
    return y.reshape(B, S, D)

def setup_inputs(seed: int = 0) -> dict:
    key = jax.random.key(seed)
    ks = jax.random.split(key, 28)

    def nrm(k, shape, scale):
        return jax.random.normal(k, shape, jnp.float32) * scale

    u = jax.random.uniform(ks[11], (DEPTH, LRU_WIDTH), jnp.float32, 0.9, 0.999)
    s = u ** (1.0 / LRU_C)
    return {
        'x': nrm(ks[0], (BATCH, SEQ, D_MODEL), 1.0),
        'w_in': nrm(ks[1], (DEPTH, D_MODEL, D_PROJ), D_MODEL ** -0.5),
        'w_out': nrm(ks[2], (DEPTH, D_MIX, D_MODEL), DN_BETA * D_MIX ** -0.5),
        'hg_lb_logits': nrm(ks[3], (DEPTH, HG_HEADS * HG_KEY_DIM), 0.5),
        'hg_norm_g': 1.0 + nrm(ks[4], (DEPTH, HG_WIDTH), 0.02),
        'lru_conv_w': nrm(ks[5], (DEPTH, CONV_WIDTH, LRU_WIDTH), CONV_WIDTH ** -0.5),
        'lru_conv_b': nrm(ks[6], (DEPTH, LRU_WIDTH), 0.01),
        'lru_wa': nrm(ks[7], (DEPTH, LRU_BLOCKS, LRU_BLOCK_DIM, LRU_BLOCK_DIM), LRU_BLOCK_DIM ** -0.5),
        'lru_ba': nrm(ks[8], (DEPTH, LRU_WIDTH), 0.01),
        'lru_wx': nrm(ks[9], (DEPTH, LRU_BLOCKS, LRU_BLOCK_DIM, LRU_BLOCK_DIM), LRU_BLOCK_DIM ** -0.5),
        'lru_bx': nrm(ks[10], (DEPTH, LRU_WIDTH), 0.01),
        'lru_lambda': jnp.log(s) - jnp.log1p(-s),
        'da_lq1': nrm(ks[12], (DEPTH, DA_HEAD_DIM), 0.1),
        'da_lk1': nrm(ks[13], (DEPTH, DA_HEAD_DIM), 0.1),
        'da_lq2': nrm(ks[14], (DEPTH, DA_HEAD_DIM), 0.1),
        'da_lk2': nrm(ks[15], (DEPTH, DA_HEAD_DIM), 0.1),
        'da_norm_g': 1.0 + nrm(ks[16], (DEPTH, DA_WIDTH), 0.02),
        'ln1_g': 1.0 + nrm(ks[17], (DEPTH, D_MODEL), 0.02),
        'ln1_b': nrm(ks[18], (DEPTH, D_MODEL), 0.02),
        'ln2_g': 1.0 + nrm(ks[19], (DEPTH, D_MODEL), 0.02),
        'ln2_b': nrm(ks[20], (DEPTH, D_MODEL), 0.02),
        'ffn_wg': nrm(ks[21], (N_DENSE, D_MODEL, D_FF), D_MODEL ** -0.5),
        'ffn_wu': nrm(ks[22], (N_DENSE, D_MODEL, D_FF), D_MODEL ** -0.5),
        'ffn_wd': nrm(ks[23], (N_DENSE, D_FF, D_MODEL), DN_BETA * D_FF ** -0.5),
        'router_w': nrm(ks[24], (N_MOE, D_MODEL, N_EXPERTS), D_MODEL ** -0.5),
        'moe_wg': nrm(ks[25], (N_MOE, N_EXPERTS, D_MODEL, D_FF), D_MODEL ** -0.5),
        'moe_wu': nrm(ks[26], (N_MOE, N_EXPERTS, D_MODEL, D_FF), D_MODEL ** -0.5),
        'moe_wd': nrm(ks[27], (N_MOE, N_EXPERTS, D_FF, D_MODEL), DN_BETA * D_FF ** -0.5),
    }

def reference(x, w_in, w_out, hg_lb_logits, hg_norm_g, lru_conv_w, lru_conv_b, lru_wa, lru_ba,
              lru_wx, lru_bx, lru_lambda, da_lq1, da_lk1, da_lq2, da_lk2, da_norm_g,
              ln1_g, ln1_b, ln2_g, ln2_b, ffn_wg, ffn_wu, ffn_wd, router_w, moe_wg, moe_wu, moe_wd):
    lb_p = jax.nn.softmax(hg_lb_logits.astype(jnp.float32), axis=0)
    lb_all = jnp.cumsum(lb_p, axis=0) - lb_p[0:1]
    for l in range(DEPTH):
        h = _mixer(x, w_in[l], w_out[l], lb_all[l], hg_norm_g[l], lru_conv_w[l], lru_conv_b[l],
                   lru_wa[l], lru_ba[l], lru_wx[l], lru_bx[l], lru_lambda[l],
                   da_lq1[l], da_lk1[l], da_lq2[l], da_lk2[l], da_norm_g[l], l)
        x = _layer_norm(DN_ALPHA * x + h, ln1_g[l], ln1_b[l])
        j = l // 2
        if l % 2 == 0:
            f = _swiglu(x, ffn_wg[j], ffn_wu[j], ffn_wd[j])
        else:
            f = _moe(x, router_w[j], moe_wg[j], moe_wu[j], moe_wd[j])
        x = _layer_norm(DN_ALPHA * x + f, ln2_g[l], ln2_b[l])
    return x


_drawn_inputs = setup_inputs


def setup_inputs(seed=0):
    import zlib

    import numpy as np

    out = dict(_drawn_inputs(seed))
    spreads = {}
    factors = {'hg_lb_logits': 3.98,
     'hg_norm_g': 22.731,
     'lru_conv_b': 6.298,
     'lru_ba': 200.0,
     'lru_bx': 176.546,
     'da_norm_g': 6.408}
    for name, (base, spread) in spreads.items():
        noise = np.random.default_rng([zlib.crc32(name.encode()), seed]).standard_normal(out[name].shape)
        drawn = base * np.exp(spread * noise) if base else spread * noise
        out[name] = __import__('jax').numpy.asarray(drawn.astype(out[name].dtype))
    for name, factor in factors.items():
        out[name] = (out[name] * factor).astype(out[name].dtype)
    return out
```

```python
import math
from contextlib import ExitStack

import concourse.bass as bass
from concourse import mybir

P = 128
SLOT_RAW = 6
SLOT_SPLIT = 3
PIECE = 2048
FAR = -3.0e38


def decoder_trunk(nc, x, w_in, w_out, hg_lb_logits, hg_norm_g, lru_conv_w, lru_conv_b, lru_wa, lru_ba,
                  lru_wx, lru_bx, lru_lambda, da_lq1, da_lk1, da_lq2, da_lk2, da_norm_g,
                  ln1_g, ln1_b, ln2_g, ln2_b, ffn_wg, ffn_wu, ffn_wd, router_w, moe_wg, moe_wu, moe_wd, out):
    f32, f32r, bf16 = mybir.dt.float32, mybir.dt.float32r, mybir.dt.bfloat16
    i8, i32, u32 = mybir.dt.int8, mybir.dt.int32, mybir.dt.uint32
    ALU, ACT, AX = mybir.AluOpType, mybir.ActivationFunctionType, mybir.AxisListType.X

    _, SEQ, D = x.shape
    DEPTH = w_in.shape[0]
    TB = SEQ // P
    DC = D // P
    NCOL = w_in.shape[2] // 256
    F = ffn_wg.shape[2]
    FB = F // 512
    E = moe_wg.shape[1]
    TOP_K = 2
    ITEMS = E + (TOP_K * SEQ - 1) // (P + 1)
    ALPHA = (2.0 * DEPTH) ** 0.25
    EPS = 1e-5
    DA_HEADS, DA_DIM, HG_DIM = 4, 64, 64
    HG_LEVELS = 9
    assert (SEQ, D, DEPTH, NCOL, FB * 512, E) == (256, 1024, 2, 12, F, 8)

    HQ, HF, HI, HG, LX, LG, DQ, DK, DV = 0, 1, 2, 3, 4, 5, 6, 8, 10
    ORDER = [HQ, HF, LX, LG, HI, DQ, DQ + 1, DK, DK + 1, DV, DV + 1, HG]
    TOKEN_MAJOR = (HI, HG, DV, DV + 1)
    OUT_ORDER = [1, 0, 2, 3]
    N_MIX = NCOL + len(OUT_ORDER)
    N_FFN = 6 * FB
    MIX0 = [l * (N_MIX + N_FFN) for l in range(DEPTH)]
    DENSE0 = MIX0[0] + N_MIX
    MOE0 = MIX0[1] + N_MIX
    assert N_FFN % SLOT_RAW == 0 and SLOT_RAW % SLOT_SPLIT == 0

    C_LB, C_HGN, C_CW, C_CB, C_BA, C_BX, C_LAM, C_DAN, N_VEC = 0, 4, 8, 24, 28, 32, 36, 40, 48

    ctx = ExitStack()
    with ctx:
        def sb(name, shape, dt=f32, where=ctx):
            return where.enter_context(nc.sbuf_tensor(name, shape, dt))

        def sem(name):
            return ctx.enter_context(nc.semaphore(name))

        raw = [sb(f"raw{k}", [P, PIECE]) for k in range(SLOT_RAW)]
        w_hi = [sb(f"w_hi{k}", [P, PIECE], f32r) for k in range(SLOT_SPLIT)]
        w_lo = [sb(f"w_lo{k}", [P, PIECE], f32r) for k in range(SLOT_SPLIT)]
        xres = sb("xres", [P, TB, D])
        actT_hi = sb("actT_hi", [P, DC * SEQ], f32r)
        actT_lo = sb("actT_lo", [P, DC * SEQ], f32r)
        mixT_hi = sb("mixT_hi", [P, DC * SEQ], f32r)
        mixT_lo = sb("mixT_lo", [P, DC * SEQ], f32r)
        norm_gb = sb("norm_gb", [P, 2, D])
        ident = sb("ident", [P, P])
        iota_row = sb("iota_row", [P, P])
        before = sb("before", [P, P])
        ones = sb("ones", [P, P])
        zeros = sb("zeros", [P, P], bf16)
        far_mask = sb("far_mask", [P, 2 * P])
        pair = sb("pair", [P, 7, P], i8)
        keep = [sb(f"keep{n}", [P, 2 * SEQ], bf16) for n in range(3)]
        eps = sb("eps", [P, 1])
        vec_rows = sb("vec_rows", [N_VEC, P])
        vec = sb("vec", [P, N_VEC])
        gate_a = sb("gate_a", [P, DEPTH, 2, P])
        gate_x = sb("gate_x", [P, DEPTH, 2, P])
        lam_rows = sb("lam_rows", [1, 4, DEPTH * DA_DIM])
        lam_prod = sb("lam_prod", [1, 2, DEPTH * DA_DIM])
        lam_sum = sb("lam_sum", [1, 2 * DEPTH])
        lam_one = sb("lam_one", [1, DEPTH])
        lam = sb("lam", [P, DEPTH])
        lb = sb("lb", [P, DEPTH, 2])
        lb_rest = sb("lb_rest", [P, DEPTH, 2])
        lb_tmp = sb("lb_tmp", [P, 8])
        decay = sb("decay", [P, 2 * DEPTH])
        decay_neg = sb("decay_neg", [P, 2 * DEPTH])
        soft = sb("soft", [P, 4, 2 * DEPTH])
        da_g = sb("da_g", [P, DEPTH * 4])
        stats = sb("stats", [P, TB, 2, 6])
        mean_var = sb("mean_var", [P, TB, 2])
        std = sb("std", [P, TB])
        rstd = sb("rstd", [P, TB])
        with ExitStack() as mixer_only:
            def mb(name, shape, dt=f32):
                return sb(name, shape, dt, mixer_only)

            sig = mb("sig", [P, 2 * SEQ])
            hq = mb("hq", [P, 2 * SEQ])
            hk = mb("hk", [P, 2 * SEQ])
            logf = mb("logf", [P, 2 * SEQ])
            run = [mb(f"run{n}", [P, 2 * SEQ]) for n in range(3)]
            rel = [mb(f"rel{n}", [P, 2 * SEQ]) for n in range(2)]
            sides_t = mb("sides_t", [P, 2, 2 * SEQ])
            side = [sides_t[:, n, :] for n in range(2)]
            pairT = mb("pairT", [P, 3, 4, P])
            hv = mb("hv", [P, TB, 256])
            lx = mb("lx", [P, 2, 3 + SEQ])
            shared = mb("shared", [P, 4, 2 * SEQ])
            dq = mb("dq", [P, DA_HEADS, SEQ])
            dk = mb("dk", [P, DA_HEADS, SEQ])
            row_max = mb("row_max", [P, 16])
            row_sum = mb("row_sum", [P, 16])
            row_inv = mb("row_inv", [P, 16])
            head_ms = mb("head_ms", [P, 8])
            head_r = mb("head_r", [P, 8])
            pair_f = shared[:, 0:2, :].rearrange("p a n -> p (a n)")[:, 0:7 * P].rearrange("p (m t) -> p m t", m=7)
            xc = shared[:, 0, :].rearrange("p (c t) -> p c t", c=2)
            lgate, lgelu, lt = shared[:, 1, :], shared[:, 2, :], shared[:, 3, :]
            lr, li, la = run[0], run[1], logf
            hgate = logf[:, :].rearrange("p (t n) -> p t n", t=TB)
            hgate_sig = sig[:, :].rearrange("p (t n) -> p t n", t=TB)
            dv = [run[n][:, :].rearrange("p (t n) -> p t n", t=TB) for n in (2, 1)]
            prob1 = shared[:, :, :].rearrange("p a n -> p (a n)").rearrange(
                "p (m h k) -> p m h k", m=2, h=DA_HEADS)
            prob0 = sides_t[:, :, :].rearrange("p m (h k) -> p m h k", h=DA_HEADS)
            hsq, hout = rel
            dsq = shared[:, 0:2, :]
            dout = shared[:, 2:4, :]
        xs_hi = sb("xs_hi", [P, TB, D], f32r)
        xs_lo = sb("xs_lo", [P, TB, D], f32r)
        y_hi = sb("y_hi", [P, D], f32r)
        y_lo = sb("y_lo", [P, D], f32r)
        hid_sig = sb("hid_sig", [P, 512])
        hid2 = [sb(f"hid{n}", [P, 512]) for n in range(2)]
        hid = hid2[0]
        rw = sb("rw", [P, DC, E])
        rw_hi = sb("rw_hi", [P, DC, E], f32r)
        rw_lo = sb("rw_lo", [P, DC, E], f32r)
        logit = sb("logit", [P, TB, E])
        best = sb("best", [P, TB, 8])
        best_at = sb("best_at", [P, TB, 8], u32)
        best_f = sb("best_f", [P, TB, 8])
        hot = sb("hot", [P, TOP_K, TB, E])
        gates = sb("gates", [P, 4, TB])
        routed = sb("routed", [P, TB, E])
        combine = sb("combine", [P, TB, ITEMS])
        place = sb("place", [P, TB, ITEMS])
        over = sb("over", [P, 3, E])
        over_sel = sb("over_sel", [P, E])
        over_tmp = sb("over_tmp", [P, TB, E])
        item_f = sb("item_f", [P, 1 + ITEMS])
        item_i = sb("item_i", [P, 1 + ITEMS], i32)
        pick = sb("pick", [P, TB, P], f32r)
        pickT = sb("pickT", [P, SEQ], f32r)
        gate_tok = sb("gate_tok", [P, TB])
        gate_slot = sb("gate_slot", [P, 1])

        bank = [ctx.enter_context(nc.psum_tensor(f"bank{k}", [P, 512], f32)) for k in range(8)]

        full = [sem(f"full{k}") for k in range(SLOT_RAW)]
        hi_ready, lo_ready, used = sem("hi_ready"), sem("lo_ready"), sem("used")
        x_in, vec_in, gate_in, lam_in, norm_in, rw_in, stored = [
            sem(n) for n in "x_in vec_in gate_in lam_in norm_in rw_in stored".split()]
        consts, consts2, lam_taken, vecT_done, vec_done, lam_done, lamB_done, lx_blank = [
            sem(n) for n in "consts consts2 lam_taken vecT_done vec_done lam_done lamB_done lx_blank".split()]
        x_ready, xT_done, xT_hi_ready, xT_lo_ready, norm_used = [
            sem(n) for n in "x_ready xT_done xT_hi_ready xT_lo_ready norm_used".split()]
        taken, f_ready, k_sig, logf_done, qk_ready, rel_done, exp_done, side_done, level_done, level_taken = [
            sem(n) for n in ("taken f_ready k_sig logf_done qk_ready rel_done exp_done side_done "
                             "level_done level_taken").split()]
        xc_ready, gates_done, act_lru, tanh_done, root_in, root_done, gelu_in, gelu_sig, lru_out, lru_hi = [
            sem(n) for n in ("xc_ready gates_done act_lru tanh_done root_in root_done gelu_in gelu_sig "
                             "lru_out lru_hi").split()]
        score_done, score_taken, max_done, prob_done, w_done, wT_done, wT_taken = [
            sem(n) for n in "score_done score_taken max_done prob_done w_done wT_done wT_taken".split()]
        hpv_done, hsq_done, hms_done, hstd_done, hout_done, hT_done, hT_hi_ready, mix_lo = [
            sem(n) for n in "hpv_done hsq_done hms_done hstd_done hout_done hT_done hT_hi_ready mix_lo".split()]
        dpv_done, dsq_done, dms_done, dstd_done, dout_done, dT_done, dT_hi_ready = [
            sem(n) for n in "dpv_done dsq_done dms_done dstd_done dout_done dT_done dT_hi_ready".split()]
        hg_sig, var_done, ln_std = [sem(n) for n in "hg_sig var_done ln_std".split()]
        d_silu, d_h, d_hi, d_lo = [sem(n) for n in "d_silu d_h d_hi d_lo".split()]
        rw_split, logit_done, gap_done, gap_exp, routed_done, rank_done, items_done, xs_hi_done, xs_done = [
            sem(n) for n in ("rw_split logit_done gap_done gap_exp routed_done rank_done items_done "
                             "xs_hi_done xs_done").split()]
        m_pick, m_gath, m_xg_hi, m_xg_lo, m_silu, m_h, m_T, m_T_hi, m_T_lo, m_y_hi, m_y_lo, m_back, m_acc = [
            sem(n) for n in ("m_pick m_gath m_xg_hi m_xg_lo m_silu m_h m_T m_T_hi m_T_lo m_y_hi m_y_lo "
                             "m_back m_acc").split()]
        dve_step, act_step, pool_step = sem("dve_step"), sem("act_step"), sem("pool_step")

        def ring(c, turns=0):
            return c % SLOT_RAW, c % SLOT_SPLIT, 16 * (c // SLOT_RAW + 1) + 16 * turns, c + SLOT_RAW * turns

        actT = [t[:, :].rearrange("p (c t) -> p c t", c=DC) for t in (actT_hi, actT_lo)]
        xg = [t[:, 0:DC * P].rearrange("p (c t) -> p c t", c=DC) for t in (actT_hi, actT_lo)]
        mixT = [t[:, :].rearrange("p (c t) -> p c t", c=DC) for t in (mixT_hi, mixT_lo)]

        in_v = w_in.rearrange("l (c p) (b n) -> l b p c n", p=P, n=256)
        out_v = w_out.rearrange("l (q c p) n -> l q p c n", p=P, c=2)
        up_v = [w[0].rearrange("(c p) (b n) -> b p c n", p=P, n=256) for w in (ffn_wg, ffn_wu)]
        down_v = ffn_wd[0].rearrange("(q c p) n -> q p c n", p=P, c=2)
        moe_up_v = [w[0].rearrange("e (c p) (b n) -> e b p c n", p=P, n=512) for w in (moe_wg, moe_wu)]
        moe_down_v = moe_wd[0].rearrange("e (b q c p) n -> e b q p c n", p=P, c=2, q=2)

        block = ctx.enter_context(nc.Block())

        @block.sync
        def _(sp):
            for t in range(TB):
                sp.dma_start(xres[:, t, :], x[0, t * P:(t + 1) * P, :]).then_inc(x_in, 16)

            def load(c, src, turns=0, reuse=True):
                slot, _, _, n = ring(c, turns)
                if reuse:
                    sp.wait_ge(lo_ready, n - SLOT_RAW + 1)
                dst = raw[slot][:, :].rearrange("p (c n) -> p c n", c=src.shape[1])
                sp.dma_start(dst, src).then_inc(full[slot], 16)

            def load_mixer(l):
                for j in range(NCOL):
                    load(MIX0[l] + j, in_v[l, ORDER[j]], reuse=MIX0[l] + j >= SLOT_RAW)
                for j, q in enumerate(OUT_ORDER):
                    load(MIX0[l] + NCOL + j, out_v[l, q])

            def load_expert(e, i):
                def ups(c, b, turns):
                    for m in range(2):
                        for h in range(2):
                            load(c + 2 * m + h, moe_up_v[m][e, b, :, 4 * h:4 * h + 4, :], turns)

                def downs(c, b, turns):
                    for h in range(2):
                        load(c + h, moe_down_v[e, b, h], turns)

                ups(MOE0, 0, FB * i)
                with sp.Fori(1, FB) as fb:
                    ups(MOE0 + 4, fb, FB * i + fb - 1)
                    downs(MOE0 + 8, fb - 1, FB * i + fb - 1)
                downs(MOE0 + N_FFN - 2, FB - 1, FB * i)

            load_mixer(0)
            with sp.Fori(0, FB) as fb:
                for h in range(2):
                    for m in range(2):
                        load(DENSE0 + 2 * h + m, up_v[m][2 * fb + h], fb)
                for h in range(2):
                    load(DENSE0 + 4 + h, down_v[2 * fb + h], fb)
            load_mixer(1)
            with sp.Fori(0, E) as i:
                load_expert(i, i)
            sp.wait_ge(items_done, 1)
            n_items = sp.value_load(item_i[0:1, 0:1], min_val=E, max_val=ITEMS)
            with sp.If(n_items > E):
                with sp.Fori(E, n_items) as i:
                    e = sp.value_load(item_i[0:1, bass.ds(i + 1, 1)], min_val=0, max_val=E - 1)
                    load_expert(e, i)
            for t in range(TB):
                sp.wait_ge(x_ready, TB * (2 * DEPTH - 1) + t + 1)
                sp.dma_start(out[0, t * P:(t + 1) * P, :], xres[:, t, :]).then_inc(stored, 16)
            sp.wait_ge(stored, 16 * TB)

        @block.gpsimd
        def _(pool):
            count = [0]

            def step(ins):
                count[0] += 1
                ins.then_inc(pool_step, 1)
                pool.wait_ge(pool_step, count[0])

            def select(t, pattern, op, base, mult, fill=0.0):
                step(pool.affine_select(out=t, in_=t, pattern=pattern, compare_op=op, fill=fill,
                                        base=base, channel_multiplier=mult))

            step(pool.memset(ident[:, :], 0.0))
            pool.affine_select(out=ident[:, :], in_=ident[:, :], pattern=[[-1, P]], compare_op=ALU.not_equal,
                               fill=1.0, base=0, channel_multiplier=1).then_inc(consts, 1)
            for g, t in ((lru_wa, gate_a), (lru_wx, gate_x)):
                step(pool.memset(t[:, :, :, :], 0.0))
                view = g.rearrange("l (c h) i j -> h i (l c) j", h=2)
                for h in range(2):
                    rows = slice(64 * h, 64 * h + 64)
                    dst = t[rows, :, :, 64 * h:64 * h + 64].rearrange("p l c j -> p (l c) j")
                    pool.dma_start(dst, view[h]).then_inc(gate_in, 16)
            pool.memset(lx[:, :, 0:3], 0.0).then_inc(lx_blank, 1)
            for n in range(2 * DEPTH):
                g, b = ((ln1_g, ln1_b), (ln2_g, ln2_b))[n % 2]
                if n:
                    pool.wait_ge(norm_used, n)
                pool.dma_start(norm_gb[:, 0, :], g[n // 2:n // 2 + 1, :].to_broadcast((P, D))).then_inc(norm_in, 16)
                pool.dma_start(norm_gb[:, 1, :], b[n // 2:n // 2 + 1, :].to_broadcast((P, D))).then_inc(norm_in, 16)
                if n:
                    continue
                step(pool.memset(eps[:, :], EPS))
                step(pool.memset(ones[:, :], 1.0))
                step(pool.memset(zeros[:, :], 0.0))
                for m, width in enumerate((16, 64, 256)):
                    step(pool.memset(keep[m][:, :], 1.0))
                    step(pool.memset(keep[m][:, :].rearrange("p (b w) -> p b w", w=width)[:, :, 0:1], 0.0))
                step(pool.memset(pair_f[:, :, :], 0.0))
                for m in range(7):
                    h = 1 << m
                    nb = P // (2 * h)
                    odd = pair_f[:, m, :].rearrange("p (b two h) -> p b two h", two=2, h=h)[:, :, 1, :]
                    step(pool.memset(odd, 1.0))
                    select(odd, [[-2 * h, nb], [0, h]], ALU.is_ge, 0, 1)
                    select(odd, [[2 * h, nb], [0, h]], ALU.is_ge, h - 1, -1)
                step(pool.tensor_copy(pair[:, :, :], pair_f[:, :, :]))
                step(pool.memset(far_mask[:, :], 0.0))
                select(far_mask[:, P:2 * P], [[-1, P]], ALU.is_ge, 0, 1, FAR)
                step(pool.memset(before[:, :], 1.0))
                select(before[:, :], [[1, P]], ALU.is_gt, 0, -1)
                pool.iota(iota_row[:, :], pattern=[[1, P]], base=0, channel_multiplier=0,
                          allow_small_or_imprecise_dtypes=True).then_inc(consts2, 1)

        @block.tensor
        def _(pe):
            def product(o, a, b, first, last):
                pe.matmul(o, a[0], b[0], start=first, stop=False, skip_group_check=True)
                pe.matmul(o, a[1], b[0], start=False, stop=False, skip_group_check=True)
                return pe.matmul(o, a[0], b[1], start=False, stop=last, skip_group_check=True)

            def piece(c, width, turns=0):
                _, k, _, n = ring(c, turns)
                pe.wait_ge(lo_ready, n + 1)
                return [t[:, :].rearrange("p (c n) -> p c n", n=width) for t in (w_hi[k], w_lo[k])]

            def transpose_x(n):
                for t in range(TB):
                    if n == 0:
                        pe.wait_ge(x_in, 16 * TB)
                        pe.wait_ge(consts, 1)
                    else:
                        pe.wait_ge(x_ready, TB * (n - 1) + t + 1)
                    for c in range(DC):
                        o = bank[c // 2][:, (c % 2) * SEQ + t * P:(c % 2) * SEQ + (t + 1) * P]
                        last = pe.transpose(o, xres[:, t, c * P:(c + 1) * P], ident[:, :])
                last.then_inc(xT_done, 1)
                pe.wait_ge(xT_lo_ready, 4 * (n + 1))

            def project(l, j):
                w = piece(MIX0[l] + j, 256)
                if j >= 4:
                    pe.wait_ge(taken, NCOL * l + j - 3)
                for g in range(2):
                    for c in range(DC):
                        if ORDER[j] in TOKEN_MAJOR:
                            a = [t[:, c, g * P:(g + 1) * P] for t in actT]
                            b = [t[:, c, :] for t in w]
                        else:
                            a = [t[:, c, g * P:(g + 1) * P] for t in w]
                            b = [t[:, c, :] for t in actT]
                        last = product(bank[j % 4][:, g * 256:(g + 1) * 256], a, b, c == 0, c == DC - 1)
                last.then_inc(used, 1)

            def level(l, m):
                if m == 0:
                    pe.wait_ge(qk_ready, l + 1)
                    a, b = hk[:, :], hq[:, :]
                else:
                    pe.wait_ge(side_done, 8 * l + m)
                    a = b = side[m % 2]
                    pe.wait_ge(level_taken, HG_LEVELS * l + m)
                for h in range(2):
                    r = slice(64 * h, 64 * h + 64)
                    for c in range(2):
                        if m == HG_LEVELS - 1:
                            last = pe.matmul(bank[4 + h][:, c * P:(c + 1) * P], a[r, c * SEQ:c * SEQ + P],
                                             b[r, c * SEQ + P:(c + 1) * SEQ], start=True, stop=True)
                            continue
                        for t in range(TB):
                            s = slice(c * SEQ + t * P, c * SEQ + (t + 1) * P)
                            last = pe.matmul(bank[4 + h][:, t * 256 + c * P:t * 256 + (c + 1) * P],
                                             a[r, s], b[r, s], start=True, stop=True)
                last.then_inc(level_done, 1)

            def lru_gates(l):
                pe.wait_ge(xc_ready, l + 1)
                pe.wait_ge(gate_in, 64)
                for k, g in enumerate((gate_a, gate_x)):
                    for c in range(2):
                        last = pe.matmul(bank[6 + k][:, c * SEQ:(c + 1) * SEQ], g[:, l, c, :], xc[:, c, :],
                                         start=True, stop=True)
                last.then_inc(gates_done, 1)

            def scores(l, r):
                if r == 0:
                    pe.wait_ge(taken, NCOL * l + 9)
                    pe.wait_ge(act_lru, l + 1)
                else:
                    pe.wait_ge(score_taken, 3 * l + r)
                for m in range(2):
                    rows = slice(64 * m, 64 * m + 64)
                    if r < 2:
                        for h in range(2):
                            last = pe.matmul(bank[6 + m][:, h * 256:(h + 1) * 256], dq[rows, 2 * r + h, P:2 * P],
                                             dk[rows, 2 * r + h, :], start=True, stop=True)
                    else:
                        for h in range(DA_HEADS):
                            last = pe.matmul(bank[6 + m][:, h * P:(h + 1) * P], dq[rows, h, 0:P],
                                             dk[rows, h, 0:P], start=True, stop=True)
                last.then_inc(score_done, 1)

            def out_project(l, j):
                w = piece(MIX0[l] + NCOL + j, D)
                for c in range(2):
                    d = 2 * OUT_ORDER[j] + c
                    for t in range(TB):
                        for h in range(2):
                            last = product(bank[2 * t + h][:, :], [m[:, d, t * P:(t + 1) * P] for m in mixT],
                                           [v[:, c, h * 512:(h + 1) * 512] for v in w],
                                           j == 0 and c == 0, j == 3 and c == 1)
                last.then_inc(used, 1)

            pe.wait_ge(consts, 1)
            pe.wait_ge(vec_in, 16 * 8)
            pe.transpose(bank[7][:, 0:N_VEC], vec_rows[:, :], ident[0:N_VEC, 0:N_VEC]).then_inc(vecT_done, 1)

            for l in range(DEPTH):
                transpose_x(2 * l)
                for j in range(NCOL):
                    project(l, j)
                    if j == 4 and l == 0:
                        pe.wait_ge(consts2, 1)
                        pe.wait_ge(lam_done, 1)
                        pe.matmul(bank[7][:, 0:DEPTH], ones[0:1, :], lam_one[:, :], start=True,
                                  stop=True).then_inc(lamB_done, 1)
                    if j >= 3:
                        level(l, j - 3)
                    if j == 5:
                        if l == 0:
                            pe.wait_ge(lam_taken, 1)
                        lru_gates(l)
                    if j >= 9:
                        scores(l, j - 9)
                pe.wait_ge(taken, NCOL * (l + 1))
                pe.wait_ge(mix_lo, 3 * l + 1)
                out_project(l, 0)
                pe.wait_ge(level_taken, HG_LEVELS * (l + 1))
                for t in range(TB):
                    for u in range(4):
                        head = 2 * (u % 2) + u // 2
                        o = bank[4 + t][:, head * 64:(head + 1) * 64]
                        v = [hv[:, b, head * 64:(head + 1) * 64] for b in range(TB)]
                        last = pe.matmul(o, pairT[:, t, u, :], v[t], start=True, stop=t == 0)
                        if t == 1:
                            last = pe.matmul(o, pairT[:, 2, u, :], v[0], start=False, stop=True)
                last.then_inc(hpv_done, 1)
                pe.wait_ge(hout_done, l + 1)
                for c in range(2):
                    for t in range(TB):
                        last = pe.transpose(bank[4][:, c * SEQ + t * P:c * SEQ + (t + 1) * P],
                                            hout[:, :].rearrange("p (t n) -> p t n", t=TB)[:, t, c * P:(c + 1) * P],
                                            ident[:, :])
                last.then_inc(hT_done, 1)
                pe.wait_ge(mix_lo, 3 * l + 2)
                out_project(l, 1)
                pe.wait_ge(w_done, l + 1)
                for b, w in enumerate((prob0[:, 0, :, :], prob1[:, 0, :, P:2 * P], prob1[:, 0, :, 0:P])):
                    for h in range(DA_HEADS):
                        last = pe.transpose(bank[5 + b][:, h * P:(h + 1) * P], w[:, h, :], ident[:, :])
                last.then_inc(wT_done, 1)
                pe.wait_ge(wT_taken, l + 1)
                for t in range(TB):
                    for h in range(DA_HEADS):
                        o = bank[4 + t][:, h * P:(h + 1) * P]
                        last = pe.matmul(o, pairT[:, t, h, :], dv[h // 2][:, t, (h % 2) * P:(h % 2 + 1) * P], start=True, stop=t == 0)
                        if t == 1:
                            last = pe.matmul(o, pairT[:, 2, h, :], dv[h // 2][:, 0, (h % 2) * P:(h % 2 + 1) * P],
                                             start=False, stop=True)
                last.then_inc(dpv_done, 1)
                pe.wait_ge(dout_done, l + 1)
                for h in range(DA_HEADS):
                    for t in range(TB):
                        last = pe.transpose(bank[6 + h // 2][:, (h % 2) * SEQ + t * P:(h % 2) * SEQ + (t + 1) * P],
                                            dout[:, t, h * P:(h + 1) * P], ident[:, :])
                last.then_inc(dT_done, 1)
                pe.wait_ge(mix_lo, 3 * l + 3)
                out_project(l, 2)
                out_project(l, 3)
                transpose_x(2 * l + 1)
                if l:
                    continue
                for k in range(4):
                    pe.matmul(bank[4 + k][:, :], zeros[:, :], keep[0][:, :], start=True, stop=False,
                              skip_group_check=True)
                with pe.Fori(0, FB) as fb:
                    for k in range(4):
                        w = piece(DENSE0 + k, 256, fb)
                        for g in range(2):
                            for c in range(DC):
                                last = product(bank[k][:, g * SEQ:(g + 1) * SEQ],
                                               [t[:, c, g * P:(g + 1) * P] for t in w],
                                               [t[:, c, :] for t in actT], c == 0, c == DC - 1)
                        last.then_inc(used, 1)
                    for h in range(2):
                        w = piece(DENSE0 + 4 + h, D, fb)
                        pe.wait_ge(d_lo, 2 * fb + h + 1)
                        for c in range(2):
                            for t in range(TB):
                                for n in range(2):
                                    last = product(bank[4 + 2 * t + n][:, :],
                                                   [m[:, 2 * h + c, t * P:(t + 1) * P] for m in mixT],
                                                   [v[:, c, n * 512:(n + 1) * 512] for v in w], False, True)
                        last.then_inc(used, 1)

            pe.wait_ge(rw_split, 1)
            for t in range(TB):
                for c in range(DC):
                    last = product(bank[4][:, t * E:(t + 1) * E], [a[:, c, t * P:(t + 1) * P] for a in actT],
                                   [rw_hi[:, c, :], rw_lo[:, c, :]], c == 0, c == DC - 1)
            last.then_inc(logit_done, 1)
            pe.wait_ge(routed_done, 1)
            pe.matmul(bank[5][:, 0:E], before[:, :], routed[:, 0, :], start=True, stop=True)
            pe.matmul(bank[5][:, E:2 * E], before[:, :], routed[:, 1, :], start=True, stop=False)
            pe.matmul(bank[5][:, E:2 * E], ones[:, :], routed[:, 0, :], start=False, stop=True)
            pe.matmul(bank[5][:, 2 * E:3 * E], ones[:, :], routed[:, 0, :], start=True, stop=False)
            pe.matmul(bank[5][:, 2 * E:3 * E], ones[:, :], routed[:, 1, :], start=False,
                      stop=True).then_inc(rank_done, 1)

            pe.wait_ge(items_done, 1)
            pe.wait_ge(xs_done, 1)
            n_items = pe.value_load(item_i[0:1, 0:1], min_val=E, max_val=ITEMS)
            hT = [t[:, 0:4 * P].rearrange("p (c t) -> p c t", c=4) for t in (mixT_hi, mixT_lo)]
            with pe.Fori(0, n_items) as i:
                def up(c, m, turns):
                    for h in range(2):
                        w = piece(c + 2 * m + h, 512, turns)
                        for k in range(4):
                            last = product(bank[m][:, :], [a[:, 4 * h + k, :] for a in xg],
                                           [t[:, k, :] for t in w], h + k == 0, h + k == 4)
                        last.then_inc(used, 1)

                def turn(n):
                    pe.wait_ge(m_h, n)
                    for k in range(4):
                        last = pe.transpose(bank[2][:, k * P:(k + 1) * P], hid[:, k * P:(k + 1) * P], ident[:, :])
                    last.then_inc(m_T, 1)

                def down(c, n, turns, end):
                    pe.wait_ge(m_T_lo, n)
                    for h in range(2):
                        w = piece(c + h, D, turns)
                        for k in range(2):
                            for m in range(2):
                                last = product(bank[4 + m][:, :], [t[:, 2 * h + k, :] for t in hT],
                                               [t[:, k, m * 512:(m + 1) * 512] for t in w],
                                               False, end and h + k == 2)
                        last.then_inc(used, 1)

                pe.wait_ge(m_pick, i + 1)
                for m in range(2):
                    pe.matmul(bank[4 + m][:, :], zeros[:, :], keep[0][:, :], start=True, stop=False,
                              skip_group_check=True)
                for t in range(TB):
                    pe.transpose(bank[3][:, t * P:(t + 1) * P], pick[:, t, :].bitcast(f32), ident[:, :])
                for t in range(TB):
                    pe.matmul(bank[3][:, SEQ:SEQ + 1], pick[:, t, :].bitcast(f32), gate_tok[:, t:t + 1],
                              start=t == 0, stop=t == TB - 1)
                for c in range(DC):
                    for t in range(TB):
                        for n, s in enumerate((xs_hi, xs_lo)):
                            last = pe.matmul(bank[6 + c // 4][:, (c % 4) * P:(c % 4 + 1) * P],
                                             s[:, t, c * P:(c + 1) * P], pick[:, t, :],
                                             start=t + n == 0, stop=t + n == 2)
                last.then_inc(m_gath, 1)
                pe.wait_ge(m_xg_lo, i + 1)
                up(MOE0, 0, FB * i)
                up(MOE0, 1, FB * i)
                with pe.Fori(1, FB) as fb:
                    turns = FB * i + fb - 1
                    pe.wait_ge(m_silu, FB * i + fb)
                    up(MOE0 + 4, 0, turns)
                    turn(FB * i + fb)
                    up(MOE0 + 4, 1, turns)
                    down(MOE0 + 8, FB * i + fb, turns, False)
                turn(FB * i + FB)
                down(MOE0 + N_FFN - 2, FB * i + FB, FB * i, True)
                pe.wait_ge(m_y_lo, i + 1)
                for t in range(TB):
                    for h in range(2):
                        o = bank[(6, 7, 2, 3)[2 * t + h]][:, :]
                        pe.matmul(o, pickT[:, t * P:(t + 1) * P], y_hi[:, h * 512:(h + 1) * 512],
                                  start=True, stop=False)
                        pe.matmul(o, pickT[:, t * P:(t + 1) * P], y_lo[:, h * 512:(h + 1) * 512],
                                  start=False, stop=True).then_inc(m_back, 1)

        @block.scalar
        def _(act):
            count = [0]

            def step(ins):
                count[0] += 1
                ins.then_inc(act_step, 1)
                act.wait_ge(act_step, count[0])

            def hi(c, turns=0):
                slot, k, landed, n = ring(c, turns)
                act.wait_ge(full[slot], landed)
                if c >= SLOT_SPLIT:
                    act.wait_ge(used, n - SLOT_SPLIT + 1)
                act.activation(w_hi[k][:, :], raw[slot][:, :], ACT.Copy).then_inc(hi_ready, 1)

            def xT_hi(n):
                act.wait_ge(xT_done, n + 1)
                for k in range(4):
                    act.activation(actT_hi[:, k * 512:(k + 1) * 512], bank[k][:, :],
                                   ACT.Copy).then_inc(xT_hi_ready, 1)

            rows = [(hg_lb_logits, C_LB, 4), (hg_norm_g, C_HGN, 4), (lru_conv_b, C_CB, 4), (lru_ba, C_BA, 4),
                    (lru_bx, C_BX, 4), (lru_lambda, C_LAM, 4), (da_norm_g, C_DAN, 8)]
            for v, at, n in rows:
                act.dma_start(vec_rows[at:at + n, :], v.rearrange("l (c p) -> (l c) p", p=P)).then_inc(vec_in, 16)
            act.dma_start(vec_rows[C_CW:C_CW + 16, :],
                          lru_conv_w.rearrange("l j (c p) -> (l j c) p", p=P)).then_inc(vec_in, 16)
            for k, v in enumerate((da_lq1, da_lk1, da_lq2, da_lk2)):
                act.dma_start(lam_rows[:, k, :], v.rearrange("(a l) d -> a (l d)", a=1)).then_inc(lam_in, 16)

            def exps(l, m):
                act.wait_ge(rel_done, 8 * l + m)
                act.activation(rel[m % 2][:, :], rel[m % 2][:, :], ACT.Exp).then_inc(exp_done, 1)

            for l in range(DEPTH):
                if l:
                    for c in range(3):
                        hi(MIX0[l] + c)
                xT_hi(2 * l)
                if l == 0:
                    act.wait_ge(vec_done, 1)
                    act.activation(soft[:, 0, :], soft[:, 0, :], ACT.Exp)
                    act.activation(lb_tmp[:, 0:4], lb_tmp[:, 0:4], ACT.Exp)
                    act.activation(lam_sum[:, :], lam_sum[:, :], ACT.Exp).then_inc(lam_done, 1)
                    for c in range(3):
                        hi(MIX0[l] + c)
                for j in range(NCOL):
                    hi(MIX0[l] + j + 3)
                    act.wait_ge(used, MIX0[l] + j + 1)
                    b = bank[j % 4]
                    b3 = b[:, :].rearrange("p (t n) -> p t n", t=2)
                    kind = ORDER[j]
                    if kind == HQ:
                        act.activation(hq[:, :], b[:, :], ACT.Copy)
                        done = act.activation(sig[:, :], b[:, :], ACT.Sigmoid)
                    elif kind == HF:
                        act.activation(logf[:, :], b[:, :], ACT.Sigmoid)
                        done = act.activation(hk[:, :], b[:, :], ACT.Sigmoid, scale=-1.0)
                    elif kind == HI:
                        done = act.activation(hv[:, :, :], b3, ACT.Copy)
                    elif kind == HG:
                        act.activation(hgate, b3, ACT.Copy)
                        done = act.activation(hgate_sig, b3, ACT.Sigmoid)
                    elif kind == LX:
                        if l == 0:
                            act.wait_ge(lx_blank, 1)
                        done = act.activation(lx[:, :, 3:3 + SEQ], b3, ACT.Copy)
                    elif kind == LG:
                        if l == 0:
                            act.wait_ge(consts2, 1)
                        act.activation(lgate, b[:, :], ACT.Copy)
                        done = act.activation(lgelu, b[:, :], ACT.Square)
                    elif kind in (DQ, DQ + 1):
                        h = 2 * (kind - DQ)
                        done = act.activation(dq[:, h:h + 2, :], b3, ACT.Copy)
                    elif kind in (DK, DK + 1):
                        h = 2 * (kind - DK)
                        done = act.activation(dk[:, h:h + 2, :], b3, ACT.Copy)
                    else:
                        done = act.activation(dv[kind - DV], b3, ACT.Copy)
                    done.then_inc(taken, 1)
                    if j == 2:
                        act.wait_ge(f_ready, l + 1)
                        act.activation(logf[:, :], logf[:, :], ACT.Ln).then_inc(logf_done, 1)
                        exps(l, 1)
                        exps(l, 2)
                    if 3 <= j <= 8:
                        exps(l, j)
                    if j == 6:
                        act.wait_ge(gates_done, l + 1)
                        for c in range(2):
                            s = slice(c * SEQ, (c + 1) * SEQ)
                            act.activation(lr[:, s], bank[6][:, s], ACT.Sigmoid,
                                           bias=vec[:, C_BA + 2 * l + c:C_BA + 2 * l + c + 1])
                            last = act.activation(li[:, s], bank[7][:, s], ACT.Sigmoid,
                                                  bias=vec[:, C_BX + 2 * l + c:C_BX + 2 * l + c + 1])
                        last.then_inc(act_lru, 1)
                        act.wait_ge(act_lru, l + 1)
                        act.wait_ge(gelu_in, l + 1)
                        act.activation(lgelu, lgelu, ACT.Sigmoid).then_inc(gelu_sig, 1)
                        for c in range(2):
                            s = slice(c * SEQ, (c + 1) * SEQ)
                            act.activation(lt[:, s], lr[:, s], ACT.Tanh,
                                           scale=decay_neg[:, 2 * l + c:2 * l + c + 1])
                            last = act.activation(la[:, s], lr[:, s], ACT.Exp,
                                                  scale=decay[:, 2 * l + c:2 * l + c + 1])
                        last.then_inc(tanh_done, 1)
                    if j == 9:
                        act.wait_ge(root_in, l + 1)
                        act.activation(lt, lt, ACT.Sqrt).then_inc(root_done, 1)
                        act.wait_ge(lru_out, l + 1)
                        act.activation(mixT_hi[:, 2 * SEQ:4 * SEQ], lr[:, :], ACT.Copy).then_inc(lru_hi, 1)
                act.wait_ge(max_done, l + 1)
                for k in range(16):
                    t = (prob1 if k < 8 else prob0)[:, (k // 4) % 2, k % 4, :]
                    last = act.activation(t, t, ACT.Exp, bias=row_max[:, k:k + 1], scale=DA_DIM ** -0.5,
                                          accum_out=row_sum[:, k:k + 1])
                last.then_inc(prob_done, 1)
                hi(MIX0[l] + N_MIX - 1)
                act.wait_ge(hpv_done, l + 1)
                for t in range(TB):
                    last = act.activation(hsq[:, t * 256:(t + 1) * 256], bank[4 + t][:, 0:256], ACT.Square)
                last.then_inc(hsq_done, 1)
                act.wait_ge(hms_done, l + 1)
                act.activation(head_r[:, :], head_ms[:, :], ACT.Sqrt, bias=eps[:, :],
                               scale=1.0 / HG_DIM).then_inc(hstd_done, 1)
                act.wait_ge(hT_done, l + 1)
                for c in range(2):
                    last = act.activation(mixT_hi[:, c * SEQ:(c + 1) * SEQ], bank[4][:, c * SEQ:(c + 1) * SEQ],
                                          ACT.Copy, scale=vec[:, C_HGN + 2 * l + c:C_HGN + 2 * l + c + 1])
                last.then_inc(hT_hi_ready, 1)
                act.wait_ge(wT_done, l + 1)
                for b in range(3):
                    last = act.activation(pairT[:, b, :, :], bank[5 + b][:, :].rearrange("p (h t) -> p h t", h=4),
                                          ACT.Copy)
                last.then_inc(wT_taken, 1)
                act.wait_ge(dpv_done, l + 1)
                for t in range(TB):
                    last = act.activation(dsq[:, t, :], bank[4 + t][:, :], ACT.Square)
                last.then_inc(dsq_done, 1)
                act.wait_ge(dms_done, l + 1)
                act.activation(head_r[:, :], head_ms[:, :], ACT.Sqrt, bias=eps[:, :],
                               scale=1.0 / (2 * DA_DIM)).then_inc(dstd_done, 1)
                act.wait_ge(dT_done, l + 1)
                for h in range(DA_HEADS):
                    last = act.activation(mixT_hi[:, (4 + h) * SEQ:(5 + h) * SEQ],
                                          bank[6 + h // 2][:, (h % 2) * SEQ:(h % 2 + 1) * SEQ], ACT.Copy,
                                          scale=da_g[:, 4 * l + h:4 * l + h + 1])
                last.then_inc(dT_hi_ready, 1)

                def norm_std(n):
                    act.wait_ge(var_done, n + 1)
                    act.activation(std[:, :], mean_var[:, :, 1], ACT.Sqrt, bias=eps[:, :]).then_inc(ln_std, 1)

                norm_std(2 * l)
                xT_hi(2 * l + 1)
                if l:
                    continue
                with act.Fori(0, FB) as fb:
                    def hidden(h):
                        act.wait_ge(used, DENSE0 + 2 * h + 2 + SLOT_RAW * fb)
                        act.activation(hid_sig[:, :], bank[2 * h][:, :], ACT.Silu).then_inc(d_silu, 1)
                        act.wait_ge(d_h, 2 * fb + h + 1)
                        act.activation(mixT_hi[:, h * 512:(h + 1) * 512], hid2[h][:, :], ACT.Copy).then_inc(d_hi, 1)

                    for k in range(5):
                        hi(DENSE0 + k, fb)
                    hidden(0)
                    hi(DENSE0 + 5, fb)
                    hidden(1)
                norm_std(1)

            act.dma_start(rw[:, :, :], router_w[0].rearrange("(c p) e -> p c e", p=P)).then_inc(rw_in, 16)
            act.wait_ge(rw_in, 16)
            act.activation(rw_hi[:, :, :], rw[:, :, :], ACT.Copy).then_inc(xs_hi_done, 1)
            act.activation(xs_hi[:, :, :], xres[:, :, :], ACT.Copy).then_inc(xs_hi_done, 1)
            act.wait_ge(gap_done, 1)
            act.activation(gates[:, 0, :], gates[:, 3, :], ACT.Exp).then_inc(gap_exp, 1)
            act.wait_ge(items_done, 1)
            n_items = act.value_load(item_i[0:1, 0:1], min_val=E, max_val=ITEMS)
            with act.Fori(0, n_items) as i:
                def silu(n, done):
                    act.wait_ge(used, done)
                    act.activation(hid_sig[:, :], bank[0][:, :], ACT.Silu).then_inc(m_silu, 1)

                def turned(n):
                    act.wait_ge(m_T, n)
                    act.activation(mixT_hi[:, 0:512], bank[2][:, :], ACT.Copy).then_inc(m_T_hi, 1)

                at = N_FFN * i
                for k in range(3):
                    hi(MOE0 + k, FB * i)
                act.wait_ge(m_gath, i + 1)
                for k in range(2):
                    act.activation(actT_hi[:, k * 512:(k + 1) * 512], bank[6 + k][:, :], ACT.Copy)
                act.activation(pickT[:, :], bank[3][:, 0:SEQ], ACT.Copy)
                act.activation(gate_slot[:, :], bank[3][:, SEQ:SEQ + 1], ACT.Copy).then_inc(m_xg_hi, 1)
                hi(MOE0 + 3, FB * i)
                silu(1, at + MOE0 + 4)
                with act.Fori(1, FB) as fb:
                    turns = FB * i + fb - 1
                    for k in range(4):
                        hi(MOE0 + 4 + k, turns)
                    turned(FB * i + fb)
                    hi(MOE0 + 8, turns)
                    hi(MOE0 + 9, turns)
                    silu(0, MOE0 + 8 + SLOT_RAW * turns)
                hi(MOE0 + N_FFN - 2, FB * i)
                hi(MOE0 + N_FFN - 1, FB * i)
                turned(FB * i + FB)
                act.wait_ge(used, MOE0 + N_FFN + at)
                act.wait_ge(m_xg_hi, i + 1)
                act.activation(y_hi[:, 0:512], bank[4][:, :], ACT.Copy, scale=gate_slot[:, :])
                act.activation(y_hi[:, 512:1024], bank[5][:, :], ACT.Copy,
                               scale=gate_slot[:, :]).then_inc(m_y_hi, 1)
            act.wait_ge(var_done, 4)
            act.activation(std[:, :], mean_var[:, :, 1], ACT.Sqrt, bias=eps[:, :]).then_inc(ln_std, 1)

        @block.vector
        def _(dve):
            count = [0]

            def step(ins):
                count[0] += 1
                ins.then_inc(dve_step, 1)
                dve.wait_ge(dve_step, count[0])

            def lo(c, turns=0):
                slot, k, _, n = ring(c, turns)
                dve.wait_ge(hi_ready, n + 1)
                dve.tensor_tensor(w_lo[k][:, :], raw[slot][:, :], w_hi[k][:, :].bitcast(f32),
                                  ALU.subtract).then_inc(lo_ready, 1)

            def xT_lo(n):
                for k in range(4):
                    s = slice(k * 512, (k + 1) * 512)
                    dve.wait_ge(xT_hi_ready, 4 * n + k + 1)
                    dve.tensor_tensor(actT_lo[:, s], bank[k][:, :], actT_hi[:, s].bitcast(f32),
                                      ALU.subtract).then_inc(xT_lo_ready, 1)

            def norm(n):
                for t in range(TB):
                    for h in range(2):
                        step(dve.bn_stats(stats[:, t, h, :], xres[:, t, h * 512:(h + 1) * 512]))
                for t in range(TB):
                    last = dve.bn_aggr(mean_var[:, t, :], stats[:, t, :, :].rearrange("p a b -> p (a b)"))
                last.then_inc(var_done, 1)
                dve.wait_ge(ln_std, n + 1)
                dve.wait_ge(var_done, n + 1)
                step(dve.reciprocal(rstd[:, :], std[:, :]))
                dve.wait_ge(norm_in, 32 * (n + 1))
                for t in range(TB):
                    step(dve.tensor_scalar(xres[:, t, :], xres[:, t, :], mean_var[:, t, 0:1], rstd[:, t:t + 1],
                                           ALU.subtract, ALU.mult))
                    step(dve.tensor_tensor(xres[:, t, :], xres[:, t, :], norm_gb[:, 0, :], ALU.mult))
                    last = dve.tensor_tensor(xres[:, t, :], xres[:, t, :], norm_gb[:, 1, :], ALU.add)
                    last.then_inc(x_ready, 1)
                dve.wait_ge(x_ready, TB * (n + 1))
                dve.sem_inc(norm_used, 1)

            def residual(first):
                for t in range(TB):
                    for h in range(2):
                        s = xres[:, t, h * 512:(h + 1) * 512]
                        step(dve.scalar_tensor_tensor(s, s, ALPHA, bank[first + 2 * t + h][:, :], ALU.mult, ALU.add))

            def relative(l, m):
                h = 1 << (m - 1)
                r = run[0 if h <= 8 else 1 if h <= 32 else 2]
                v, o = [t[:, :].rearrange("p (b two h) -> p b two h", two=2, h=h) for t in (r, rel[m % 2])]
                edge = v[:, :, 0, h - 1:h].to_broadcast((P, 2 * SEQ // (2 * h), h))
                dve.tensor_tensor(o[:, :, 0, :], edge, v[:, :, 0, :], ALU.subtract)
                dve.tensor_tensor(o[:, :, 1, :], v[:, :, 1, :], edge, ALU.subtract).then_inc(rel_done, 1)

            def sides(l, m):
                h = 1 << (m - 1)
                e, o, k, q = [t.rearrange("p (b two h) -> p b two h", two=2, h=h)
                              for t in (rel[m % 2][:, :], side[m % 2], hk[:, :], hq[:, :])]
                dve.wait_ge(exp_done, 8 * l + m)
                if m > 2:
                    dve.wait_ge(level_done, HG_LEVELS * l + m - 1)
                dve.tensor_tensor(o[:, :, 0, :], e[:, :, 0, :], k[:, :, 0, :], ALU.mult)
                dve.tensor_tensor(o[:, :, 1, :], e[:, :, 1, :], q[:, :, 1, :], ALU.mult).then_inc(side_done, 1)
                dve.wait_ge(side_done, 8 * l + m)

            def take_level(l, m):
                dve.wait_ge(level_done, HG_LEVELS * l + m + 1)
                for h in range(2):
                    if m == HG_LEVELS - 1:
                        last = dve.tensor_copy(pairT[:, 2, 2 * h:2 * h + 2, :],
                                               bank[4 + h][:, 0:256].rearrange("p (c t) -> p c t", c=2))
                        continue
                    s = bank[4 + h][:, :].rearrange("p (b c t) -> p b c t", b=2, c=2)
                    o = pairT[:, 0:2, 2 * h:2 * h + 2, :]
                    if m == 0:
                        mask = ident[:, :].unsqueeze(1).unsqueeze(1).to_broadcast((P, 2, 2, P))
                        last = dve.tensor_tensor(o, s, mask, ALU.mult)
                    else:
                        mask = pair[:, m - 1, :].unsqueeze(1).unsqueeze(1).to_broadcast((P, 2, 2, P))
                        last = dve.copy_predicated(o, mask, s)
                last.then_inc(level_taken, 1)
                dve.wait_ge(level_taken, HG_LEVELS * l + m + 1)

            def masked_scores(l, r):
                dve.wait_ge(score_done, 3 * l + r + 1)
                for m in range(2):
                    if r < 2:
                        o = prob1[:, m, 2 * r:2 * r + 2, :]
                        mask = far_mask[:, :].unsqueeze(1).to_broadcast((P, 2, 2 * P))
                        s = bank[6 + m][:, :].rearrange("p (h k) -> p h k", h=2)
                    else:
                        o = prob0[:, m, :, :]
                        mask = far_mask[:, P:2 * P].unsqueeze(1).to_broadcast((P, DA_HEADS, P))
                        s = bank[6 + m][:, :].rearrange("p (h k) -> p h k", h=DA_HEADS)
                    last = dve.tensor_tensor(o, s, mask, ALU.add)
                last.then_inc(score_taken, 1)
                dve.wait_ge(score_taken, 3 * l + r + 1)

            def head_norm(first, heads, width, o, ms_sem, std_sem, l, sq):
                ms = head_ms[:, :]
                dve.reduce_sum(ms, sq.rearrange("p (g w) -> p g w", w=width), axis=AX).then_inc(ms_sem, 1)
                dve.wait_ge(std_sem, l + 1)
                step(dve.reciprocal(head_r[:, :], head_r[:, :]))
                for t in range(TB):
                    s = bank[first + t][:, 0:heads * width].rearrange("p (g w) -> p g w", w=width)
                    r = head_r[:, t * heads:(t + 1) * heads].unsqueeze(2).to_broadcast((P, heads, width))
                    last = dve.tensor_tensor(o[t].rearrange("p (g w) -> p g w", w=width), s, r, ALU.mult)
                return last

            dve.wait_ge(vecT_done, 1)
            step(dve.tensor_copy(vec[:, :], bank[7][:, 0:N_VEC]))
            v = vec[:, C_LAM:C_LAM + 2 * DEPTH]
            step(dve.tensor_scalar(soft[:, 1, :], v, -1.0, None, ALU.mult))
            step(dve.tensor_tensor(soft[:, 0, :], v, soft[:, 1, :], ALU.min))
            l0, l1 = vec[:, C_LB:C_LB + 2], vec[:, C_LB + 2:C_LB + 4]
            step(dve.tensor_tensor(lb_tmp[:, 4:6], l0, l1, ALU.max))
            step(dve.tensor_tensor(lb_tmp[:, 0:2], l0, lb_tmp[:, 4:6], ALU.subtract))
            step(dve.tensor_tensor(lb_tmp[:, 2:4], l1, lb_tmp[:, 4:6], ALU.subtract))
            dve.wait_ge(lam_in, 64)
            pairs = lam_rows[:, :, :].rearrange("p (m k) n -> p m k n", k=2)
            step(dve.tensor_tensor(lam_prod[:, :, :], pairs[:, :, 0, :], pairs[:, :, 1, :], ALU.mult))
            dve.reduce_sum(lam_sum[:, :], lam_prod[:, :, :].rearrange("p m (l d) -> p (m l) d", d=DA_DIM),
                           axis=AX).then_inc(vec_done, 1)
            for l in range(DEPTH):
                lam_init = 0.8 - 0.6 * math.exp(-0.3 * l)
                step(dve.tensor_scalar(da_g[:, 4 * l:4 * l + 4], vec[:, C_DAN + 4 * l:C_DAN + 4 * l + 4],
                                       1.0 - lam_init, None, ALU.mult))

            for l in range(DEPTH):
                m0 = MIX0[l]
                if l:
                    for c in range(3):
                        lo(m0 + c)
                xT_lo(2 * l)
                if l == 0:
                    dve.wait_ge(lam_done, 1)
                    step(dve.tensor_scalar(soft[:, 1, :], soft[:, 0, :], 2.0, None, ALU.add))
                    step(dve.reciprocal(soft[:, 1, :], soft[:, 1, :]))
                    step(dve.tensor_tensor(soft[:, 0, :], soft[:, 0, :], soft[:, 1, :], ALU.mult))
                    step(dve.tensor_tensor(soft[:, 1, :], soft[:, 0, :], soft[:, 0, :], ALU.mult))
                    step(dve.tensor_scalar(soft[:, 2, :], soft[:, 1, :], 1.0 / 19, 1.0 / 17, ALU.mult, ALU.add))
                    for k in range(15, 0, -2):
                        step(dve.tensor_tensor(soft[:, 2, :], soft[:, 2, :], soft[:, 1, :], ALU.mult))
                        step(dve.tensor_scalar(soft[:, 2, :], soft[:, 2, :], 1.0 / k, None, ALU.add))
                    step(dve.tensor_tensor(soft[:, 2, :], soft[:, 2, :], soft[:, 0, :], ALU.mult))
                    step(dve.tensor_scalar(soft[:, 3, :], v, 0.0, None, ALU.min))
                    step(dve.scalar_tensor_tensor(decay[:, :], soft[:, 2, :], -2.0, soft[:, 3, :],
                                                  ALU.mult, ALU.add))
                    step(dve.tensor_scalar(decay_neg[:, :], decay[:, :], -8.0, None, ALU.mult))
                    step(dve.tensor_scalar(decay[:, :], decay[:, :], 8.0, None, ALU.mult))
                    step(dve.tensor_tensor(lb_tmp[:, 4:6], lb_tmp[:, 0:2], lb_tmp[:, 2:4], ALU.add))
                    step(dve.reciprocal(lb_tmp[:, 4:6], lb_tmp[:, 4:6]))
                    step(dve.memset(lb[:, 0, :], 0.0))
                    step(dve.tensor_tensor(lb[:, 1, :], lb_tmp[:, 2:4], lb_tmp[:, 4:6], ALU.mult))
                    step(dve.tensor_scalar(lb_rest[:, :, :], lb[:, :, :], -1.0, 1.0, ALU.mult, ALU.add))
                    for k in range(DEPTH):
                        lam_init = 0.8 - 0.6 * math.exp(-0.3 * k)
                        last = dve.scalar_tensor_tensor(lam_one[:, k:k + 1], lam_sum[:, k:k + 1], lam_init,
                                                        lam_sum[:, DEPTH + k:DEPTH + k + 1], ALU.add, ALU.subtract)
                    last.then_inc(lam_done, 1)
                    for c in range(3):
                        lo(m0 + c)

                dve.wait_ge(taken, NCOL * l + 2)
                for c in range(2):
                    s = slice(c * SEQ, (c + 1) * SEQ)
                    step(dve.tensor_scalar(logf[:, s], logf[:, s], lb_rest[:, l, c:c + 1], lb[:, l, c:c + 1],
                                           ALU.mult, ALU.add))
                dve.tensor_scalar(logf[:, :], logf[:, :], 2.0 ** -63, None, ALU.max).then_inc(f_ready, 1)
                for c in range(2):
                    s = slice(c * SEQ, (c + 1) * SEQ)
                    dve.tensor_scalar(hk[:, s], hk[:, s], lb_rest[:, l, c:c + 1], None, ALU.mult)
                dve.tensor_tensor(hq[:, :], hq[:, :], sig[:, :], ALU.mult).then_inc(qk_ready, 1)
                lo(m0 + 3)
                dve.wait_ge(logf_done, l + 1)
                if l == 0:
                    dve.wait_ge(consts2, 1)
                for n in range(3):
                    step(dve.tensor_tensor_scan(run[n][:, :], keep[n][:, :], logf[:, :], 0.0, ALU.mult, ALU.add))
                dve.wait_ge(qk_ready, l + 1)
                relative(l, 1)
                relative(l, 2)
                dve.wait_ge(taken, NCOL * l + 3)
                for j in range(4):
                    for c in range(2):
                        w = vec[:, C_CW + 8 * l + 2 * j + c:C_CW + 8 * l + 2 * j + c + 1]
                        src = lx[:, c, j:j + SEQ]
                        if j == 0:
                            b = vec[:, C_CB + 2 * l + c:C_CB + 2 * l + c + 1]
                            step(dve.tensor_scalar(xc[:, c, :], src, w, b, ALU.mult, ALU.add))
                        else:
                            step(dve.scalar_tensor_tensor(xc[:, c, :], src, w, xc[:, c, :], ALU.mult, ALU.add))
                dve.sem_inc(xc_ready, 1)
                lo(m0 + 4)
                xcf = shared[:, 0, :]
                for m in range(1, HG_LEVELS):
                    sides(l, m)
                    if m + 2 < HG_LEVELS:
                        relative(l, m + 2)
                    take_level(l, m - 1)
                    lo(m0 + 4 + m)
                    if m == 1:
                        dve.wait_ge(taken, NCOL * l + 4)
                        c1 = 2.0 * math.sqrt(2.0 / math.pi)
                        step(dve.tensor_scalar(lgelu, lgelu, c1 * 0.044715, c1, ALU.mult, ALU.add))
                        dve.tensor_tensor(lgelu, lgelu, lgate, ALU.mult).then_inc(gelu_in, 1)
                    if m == 2 and l == 0:
                        dve.wait_ge(lamB_done, 1)
                        dve.tensor_copy(lam[:, :], bank[7][:, 0:DEPTH]).then_inc(lam_taken, 1)
                    if m == 4:
                        dve.wait_ge(tanh_done, l + 1)
                        dve.wait_ge(gelu_sig, l + 1)
                        step(dve.tensor_tensor(lgate, lgate, lgelu, ALU.mult))
                        step(dve.tensor_scalar(lgelu, lt, 1.0, None, ALU.add))
                        step(dve.reciprocal(lgelu, lgelu))
                        dve.scalar_tensor_tensor(lt, lt, 2.0, lgelu, ALU.mult,
                                                 ALU.mult).then_inc(root_in, 1)
                        step(dve.tensor_tensor(li[:, :], li[:, :], xcf, ALU.mult))
                    if m == 7:
                        dve.wait_ge(root_done, l + 1)
                        step(dve.tensor_tensor(li[:, :], li[:, :], lt, ALU.mult))
                        for c in range(2):
                            s = slice(c * SEQ, (c + 1) * SEQ)
                            step(dve.tensor_tensor_scan(lr[:, s], la[:, s], li[:, s], 0.0, ALU.mult, ALU.add))
                        dve.tensor_tensor(lr[:, :], lr[:, :], lgate, ALU.mult).then_inc(lru_out, 1)
                        dve.wait_ge(lru_hi, l + 1)
                        s = slice(2 * SEQ, 4 * SEQ)
                        dve.tensor_tensor(mixT_lo[:, s], lr[:, :], mixT_hi[:, s].bitcast(f32),
                                          ALU.subtract).then_inc(mix_lo, 1)
                        masked_scores(l, 0)
                    if m == 8:
                        masked_scores(l, 1)
                take_level(l, HG_LEVELS - 1)
                masked_scores(l, 2)
                step(dve.reduce_max(row_max[:, 0:8], prob1.rearrange("p m h k -> p (m h) k"), axis=AX))
                step(dve.reduce_max(row_max[:, 8:16], prob0.rearrange("p m h k -> p (m h) k"), axis=AX))
                dve.tensor_scalar(row_max[:, :], row_max[:, :], -DA_DIM ** -0.5, None, ALU.mult).then_inc(max_done, 1)
                lo(m0 + 13)
                lo(m0 + 14)
                dve.wait_ge(prob_done, l + 1)
                dve.wait_ge(lam_taken, 1)
                step(dve.reciprocal(row_inv[:, :], row_sum[:, :]))
                second = row_inv[:, :].rearrange("p (t m h) -> p t m h", t=2, m=2)[:, :, 1, :]
                step(dve.tensor_scalar(second, second, lam[:, l:l + 1], None, ALU.mult))
                for prob, at in ((prob1, 0), (prob0, 8)):
                    width = prob.shape[3]
                    pv = prob.rearrange("p m h k -> p (m h) k")
                    step(dve.tensor_tensor(pv, pv, row_inv[:, at:at + 8].unsqueeze(2).to_broadcast((P, 8, width)),
                                           ALU.mult))
                for n, prob in enumerate((prob1, prob0)):
                    last = dve.tensor_tensor(prob[:, 0, :, :], prob[:, 0, :, :], prob[:, 1, :, :], ALU.subtract)
                last.then_inc(w_done, 1)
                lo(m0 + 15)
                step(dve.tensor_tensor(hgate, hgate, hgate_sig, ALU.mult))
                dve.wait_ge(hsq_done, l + 1)
                o = [hout[:, t * 256:(t + 1) * 256] for t in range(TB)]
                step(head_norm(4, 4, 64, o, hms_done, hstd_done, l, hsq[:, :]))
                dve.tensor_tensor(hout[:, :], hout[:, :], hgate.rearrange("p t n -> p (t n)"),
                                  ALU.mult).then_inc(hout_done, 1)
                dve.wait_ge(hT_hi_ready, l + 1)
                for c in range(2):
                    s = slice(c * SEQ, (c + 1) * SEQ)
                    g = vec[:, C_HGN + 2 * l + c:C_HGN + 2 * l + c + 1]
                    last = dve.scalar_tensor_tensor(mixT_lo[:, s], bank[4][:, s], g, mixT_hi[:, s].bitcast(f32),
                                                    ALU.mult, ALU.subtract)
                last.then_inc(mix_lo, 1)
                dve.wait_ge(dsq_done, l + 1)
                o = [dout[:, t, :] for t in range(TB)]
                head_norm(4, 4, 128, o, dms_done, dstd_done, l,
                          dsq.rearrange("p t n -> p (t n)")).then_inc(dout_done, 1)
                dve.wait_ge(dT_hi_ready, l + 1)
                for h in range(DA_HEADS):
                    s = slice((4 + h) * SEQ, (5 + h) * SEQ)
                    last = dve.scalar_tensor_tensor(mixT_lo[:, s], bank[6 + h // 2][:, (h % 2) * SEQ:(h % 2 + 1) * SEQ],
                                                    da_g[:, 4 * l + h:4 * l + h + 1], mixT_hi[:, s].bitcast(f32),
                                                    ALU.mult, ALU.subtract)
                last.then_inc(mix_lo, 1)
                dve.wait_ge(used, m0 + N_MIX)
                residual(0)
                norm(2 * l)
                xT_lo(2 * l + 1)
                if l:
                    continue
                with dve.Fori(0, FB) as fb:
                    def hidden(h):
                        dve.wait_ge(d_silu, 2 * fb + h + 1)
                        dve.tensor_tensor(hid2[h][:, :], hid_sig[:, :], bank[2 * h + 1][:, :], ALU.mult).then_inc(d_h, 1)
                        dve.wait_ge(d_hi, 2 * fb + h + 1)
                        s = slice(h * 512, (h + 1) * 512)
                        dve.tensor_tensor(mixT_lo[:, s], hid2[h][:, :], mixT_hi[:, s].bitcast(f32),
                                          ALU.subtract).then_inc(d_lo, 1)

                    for k in range(5):
                        lo(DENSE0 + k, fb)
                    hidden(0)
                    lo(DENSE0 + 5, fb)
                    hidden(1)
                dve.wait_ge(used, DENSE0 + N_FFN)
                residual(4)
                norm(1)

            dve.wait_ge(xs_hi_done, 1)
            dve.tensor_tensor(rw_lo[:, :, :], rw[:, :, :], rw_hi[:, :, :].bitcast(f32),
                              ALU.subtract).then_inc(rw_split, 1)
            dve.wait_ge(logit_done, 1)
            step(dve.tensor_copy(logit[:, :, :], bank[4][:, 0:TB * E].rearrange("p (t e) -> p t e", t=TB)))
            for t in range(TB):
                step(dve.max(best[:, t, :], logit[:, t, :]))
            dve.tensor_tensor(gates[:, 3, :], best[:, :, 1], best[:, :, 0], ALU.subtract).then_inc(gap_done, 1)
            for t in range(TB):
                step(dve.max_index(best_at[:, t, :], best[:, t, :], logit[:, t, :]))
            step(dve.tensor_copy(best_f[:, :, :], best_at[:, :, :]))
            for k in range(TOP_K):
                for t in range(TB):
                    step(dve.tensor_scalar(hot[:, k, t, :], iota_row[:, 0:E], best_f[:, t, k:k + 1], None,
                                           ALU.is_equal))
            dve.tensor_tensor(routed[:, :, :], hot[:, 0, :, :], hot[:, 1, :, :], ALU.add).then_inc(routed_done, 1)
            dve.wait_ge(routed_done, 1)
            dve.wait_ge(gap_exp, 1)
            step(dve.tensor_scalar(gates[:, 1, :], gates[:, 0, :], 1.0, None, ALU.add))
            step(dve.reciprocal(gates[:, 1, :], gates[:, 1, :]))
            step(dve.tensor_tensor(gates[:, 2, :], gates[:, 0, :], gates[:, 1, :], ALU.mult))
            for t in range(TB):
                step(dve.tensor_scalar(combine[:, t, 0:E], hot[:, 0, t, :], gates[:, 1, t:t + 1], None, ALU.mult))
                step(dve.scalar_tensor_tensor(combine[:, t, 0:E], hot[:, 1, t, :], gates[:, 2, t:t + 1],
                                              combine[:, t, 0:E], ALU.mult, ALU.add))
            dve.wait_ge(rank_done, 1)
            rank = bank[5][:, 0:TB * E].rearrange("p (t e) -> p t e", t=TB)
            step(dve.scalar_tensor_tensor(place[:, :, 0:E], rank, 1.0, routed[:, :, :], ALU.add, ALU.mult))
            step(dve.tensor_scalar(place[:, :, 0:E], place[:, :, 0:E], -1.0, None, ALU.add))
            step(dve.tensor_scalar(over[:, 0, :], bank[5][:, 2 * E:3 * E], float(P), None, ALU.is_gt))
            step(dve.tensor_tensor_scan(over[:, 1, :], ones[:, 0:E], over[:, 0, :], 0.0, ALU.mult, ALU.add))
            step(dve.tensor_scalar(over[:, 2, :], over[:, 1, :], 0.0, None, ALU.mult))
            step(dve.tensor_copy(item_f[:, 1:1 + E], iota_row[:, 0:E]))
            for k in range(ITEMS - E):
                step(dve.scalar_tensor_tensor(over_sel[:, :], over[:, 1, :], float(k + 1), over[:, 0, :],
                                              ALU.is_equal, ALU.mult))
                sel = over_sel[:, :].unsqueeze(1).to_broadcast((P, TB, E))
                step(dve.tensor_tensor(over_tmp[:, :, :], combine[:, :, 0:E], sel, ALU.mult))
                step(dve.reduce_sum(combine[:, :, E + k:E + k + 1], over_tmp[:, :, :], axis=AX))
                step(dve.scalar_tensor_tensor(over_tmp[:, :, :], place[:, :, 0:E], 1.0 - P, sel, ALU.add, ALU.mult))
                step(dve.reduce_sum(place[:, :, E + k:E + k + 1], over_tmp[:, :, :], axis=AX))
                step(dve.tensor_scalar(place[:, :, E + k:E + k + 1], place[:, :, E + k:E + k + 1], -1.0, None, ALU.add))
                step(dve.tensor_tensor(over_tmp[:, 0, :], iota_row[:, 0:E], over_sel[:, :], ALU.mult))
                step(dve.reduce_sum(item_f[:, 1 + E + k:2 + E + k], over_tmp[:, 0, :], axis=AX))
            step(dve.tensor_scalar(item_f[:, 0:1], over[:, 1, E - 1:E], float(E), None, ALU.add))
            dve.tensor_copy(item_i[:, :], item_f[:, :]).then_inc(items_done, 1)
            dve.wait_ge(xs_hi_done, 2)
            dve.tensor_tensor(xs_lo[:, :, :], xres[:, :, :], xs_hi[:, :, :].bitcast(f32),
                              ALU.subtract).then_inc(xs_done, 1)
            dve.wait_ge(xs_done, 1)
            dve.tensor_scalar(xres[:, :, :], xres[:, :, :], ALPHA, None, ALU.mult).then_inc(m_acc, 4)
            dve.wait_ge(items_done, 1)
            n_items = dve.value_load(item_i[0:1, 0:1], min_val=E, max_val=ITEMS)
            with dve.Fori(0, n_items) as i:
                def hidden(n):
                    dve.wait_ge(m_silu, n)
                    dve.tensor_tensor(hid[:, :], hid_sig[:, :], bank[1][:, :], ALU.mult).then_inc(m_h, 1)

                def turned(n):
                    dve.wait_ge(m_T_hi, n)
                    dve.tensor_tensor(mixT_lo[:, 0:512], bank[2][:, :], mixT_hi[:, 0:512].bitcast(f32),
                                      ALU.subtract).then_inc(m_T_lo, 1)

                for t in range(TB):
                    dve.tensor_scalar(pick[:, t, :], iota_row[:, :], place[:, t, bass.ds(i, 1)], None, ALU.is_equal)
                dve.tensor_copy(gate_tok[:, :], combine[:, :, bass.ds(i, 1)].rearrange("p t a -> p (t a)")).then_inc(m_pick, 1)
                for k in range(3):
                    lo(MOE0 + k, FB * i)
                dve.wait_ge(m_xg_hi, i + 1)
                for k in range(2):
                    s = slice(k * 512, (k + 1) * 512)
                    last = dve.tensor_tensor(actT_lo[:, s], bank[6 + k][:, :], actT_hi[:, s].bitcast(f32), ALU.subtract)
                last.then_inc(m_xg_lo, 1)
                lo(MOE0 + 3, FB * i)
                hidden(FB * i + 1)
                with dve.Fori(1, FB) as fb:
                    turns = FB * i + fb - 1
                    for k in range(4):
                        lo(MOE0 + 4 + k, turns)
                    turned(FB * i + fb)
                    lo(MOE0 + 8, turns)
                    lo(MOE0 + 9, turns)
                    hidden(FB * i + fb + 1)
                lo(MOE0 + N_FFN - 2, FB * i)
                lo(MOE0 + N_FFN - 1, FB * i)
                turned(FB * i + FB)
                dve.wait_ge(m_y_hi, i + 1)
                for k in range(2):
                    s = slice(k * 512, (k + 1) * 512)
                    last = dve.scalar_tensor_tensor(y_lo[:, s], bank[4 + k][:, :], gate_slot[:, :],
                                                    y_hi[:, s].bitcast(f32), ALU.mult, ALU.subtract)
                last.then_inc(m_y_lo, 1)
                for t in range(TB):
                    for h in range(2):
                        q = 2 * t + h
                        dve.wait_ge(m_back, 4 * i + q + 1)
                        dve.wait_ge(m_acc, 4 * i + q + 1)
                        s = xres[:, t, h * 512:(h + 1) * 512]
                        dve.tensor_tensor(s, s, bank[(6, 7, 2, 3)[q]][:, :], ALU.add).then_inc(m_acc, 1)
            dve.wait_ge(m_acc, 4 * n_items + 4)
            norm(3)


_INS = ["x", "w_in", "w_out", "hg_lb_logits", "hg_norm_g", "lru_conv_w", "lru_conv_b", "lru_wa", "lru_ba",
        "lru_wx", "lru_bx", "lru_lambda", "da_lq1", "da_lk1", "da_lq2", "da_lk2", "da_norm_g",
        "ln1_g", "ln1_b", "ln2_g", "ln2_b", "ffn_wg", "ffn_wu", "ffn_wd", "router_w", "moe_wg", "moe_wu", "moe_wd"]


def kernel(**inputs):
    import numpy as np
    import concourse.bacc as bacc
    from concourse.bass_utils import run_bass_kernel_spmd

    nc = bacc.Bacc("TRN2", target_bir_lowering=False, num_devices=1)
    arrays, args = {}, []
    for name in _INS:
        a = np.ascontiguousarray(inputs[name])
        arrays[f"in_{name}"] = a
        args.append(nc.dram_tensor(f"in_{name}", a.shape, mybir.dt.from_np(a.dtype), kind="ExternalInput").ap())
    args.append(nc.dram_tensor("out_x", inputs["x"].shape, mybir.dt.float32, kind="ExternalOutput").ap())
    decoder_trunk(nc, *args)
    r = run_bass_kernel_spmd(nc, [arrays], core_ids=[0])
    return r.results[0]["out_x"]
```

```python
import math
from contextlib import ExitStack

import concourse.bass as bass
from concourse import mybir

P = 128
SLOT_RAW = 6
SLOT_SPLIT = 3
PIECE = 2048
FAR = -3.0e38


def decoder_trunk(nc, x, w_in, w_out, hg_lb_logits, hg_norm_g, lru_conv_w, lru_conv_b, lru_wa, lru_ba,
                  lru_wx, lru_bx, lru_lambda, da_lq1, da_lk1, da_lq2, da_lk2, da_norm_g,
                  ln1_g, ln1_b, ln2_g, ln2_b, ffn_wg, ffn_wu, ffn_wd, router_w, moe_wg, moe_wu, moe_wd, out):
    f32, f32r, bf16 = mybir.dt.float32, mybir.dt.float32r, mybir.dt.bfloat16
    i8, i32, u32 = mybir.dt.int8, mybir.dt.int32, mybir.dt.uint32
    ALU, ACT, AX = mybir.AluOpType, mybir.ActivationFunctionType, mybir.AxisListType.X

    _, SEQ, D = x.shape
    DEPTH = w_in.shape[0]
    TB = SEQ // P
    DC = D // P
    NCOL = w_in.shape[2] // 256
    F = ffn_wg.shape[2]
    FB = F // 512
    E = moe_wg.shape[1]
    TOP_K = 2
    ITEMS = E + (TOP_K * SEQ - 1) // (P + 1)
    ALPHA = (2.0 * DEPTH) ** 0.25
    EPS = 1e-5
    DA_HEADS, DA_DIM, HG_DIM = 4, 64, 64
    HG_LEVELS = 9
    assert (SEQ, D, DEPTH, NCOL, FB * 512, E) == (256, 1024, 2, 12, F, 8)

    HQ, HF, HI, HG, LX, LG, DQ, DK, DV = 0, 1, 2, 3, 4, 5, 6, 8, 10
    ORDER = [HQ, HF, LX, LG, HI, DQ, DQ + 1, DK, DK + 1, DV, DV + 1, HG]
    TOKEN_MAJOR = (HI, HG, DV, DV + 1)
    OUT_ORDER = [1, 0, 2, 3]
    N_MIX = NCOL + len(OUT_ORDER)
    N_FFN = 6 * FB
    MIX0 = [l * (N_MIX + N_FFN) for l in range(DEPTH)]
    DENSE0 = MIX0[0] + N_MIX
    MOE0 = MIX0[1] + N_MIX
    ITEM0 = MOE0 + 6
    SEAM0 = ITEM0 + 4 + 6 * (FB - 2)
    assert N_FFN % SLOT_RAW == 0 and SLOT_RAW % SLOT_SPLIT == 0

    C_LB, C_HGN, C_CW, C_CB, C_BA, C_BX, C_LAM, C_DAN, N_VEC = 0, 4, 8, 24, 28, 32, 36, 40, 48

    ctx = ExitStack()
    with ctx:
        def sb(name, shape, dt=f32, where=ctx):
            return where.enter_context(nc.sbuf_tensor(name, shape, dt))

        def sem(name):
            return ctx.enter_context(nc.semaphore(name))

        raw = [sb(f"raw{k}", [P, PIECE]) for k in range(SLOT_RAW)]
        w_hi = [sb(f"w_hi{k}", [P, PIECE], f32r) for k in range(SLOT_SPLIT)]
        w_lo = [sb(f"w_lo{k}", [P, PIECE], f32r) for k in range(SLOT_SPLIT)]
        xres = sb("xres", [P, TB, D])
        actT_hi = sb("actT_hi", [P, DC * SEQ], f32r)
        actT_lo = sb("actT_lo", [P, DC * SEQ], f32r)
        mixT_hi = sb("mixT_hi", [P, DC * SEQ], f32r)
        mixT_lo = sb("mixT_lo", [P, DC * SEQ], f32r)
        norm_gb = sb("norm_gb", [P, 2, D])
        ident = sb("ident", [P, P])
        iota_row = sb("iota_row", [P, P])
        before = sb("before", [P, P])
        ones = sb("ones", [P, P])
        zeros = sb("zeros", [P, P], bf16)
        far_mask = sb("far_mask", [P, 2 * P])
        pair = sb("pair", [P, 7, P], i8)
        keep = [sb(f"keep{n}", [P, 2 * SEQ], bf16) for n in range(3)]
        eps = sb("eps", [P, 1])
        vec_rows = sb("vec_rows", [N_VEC, P])
        vec = sb("vec", [P, N_VEC])
        gate_a = sb("gate_a", [P, DEPTH, 2, P])
        gate_x = sb("gate_x", [P, DEPTH, 2, P])
        lam_rows = sb("lam_rows", [1, 4, DEPTH * DA_DIM])
        lam_prod = sb("lam_prod", [1, 2, DEPTH * DA_DIM])
        lam_sum = sb("lam_sum", [1, 2 * DEPTH])
        lam_one = sb("lam_one", [1, DEPTH])
        lam = sb("lam", [P, DEPTH])
        lb = sb("lb", [P, DEPTH, 2])
        lb_rest = sb("lb_rest", [P, DEPTH, 2])
        lb_tmp = sb("lb_tmp", [P, 8])
        decay = sb("decay", [P, 2 * DEPTH])
        decay_neg = sb("decay_neg", [P, 2 * DEPTH])
        soft = sb("soft", [P, 4, 2 * DEPTH])
        da_g = sb("da_g", [P, DEPTH * 4])
        stats = sb("stats", [P, TB, 2, 6])
        mean_var = sb("mean_var", [P, TB, 2])
        std = sb("std", [P, TB])
        rstd = sb("rstd", [P, TB])
        with ExitStack() as mixer_only:
            def mb(name, shape, dt=f32):
                return sb(name, shape, dt, mixer_only)

            sig = mb("sig", [P, 2 * SEQ])
            hq = mb("hq", [P, 2 * SEQ])
            hk = mb("hk", [P, 2 * SEQ])
            logf = mb("logf", [P, 2 * SEQ])
            run = [mb(f"run{n}", [P, 2 * SEQ]) for n in range(3)]
            rel = [mb(f"rel{n}", [P, 2 * SEQ]) for n in range(2)]
            sides_t = mb("sides_t", [P, 2, 2 * SEQ])
            side = [sides_t[:, n, :] for n in range(2)]
            pairT = mb("pairT", [P, 3, 4, P])
            hv = mb("hv", [P, TB, 256])
            lx = mb("lx", [P, 2, 3 + SEQ])
            shared = mb("shared", [P, 4, 2 * SEQ])
            dq = mb("dq", [P, DA_HEADS, SEQ])
            dk = mb("dk", [P, DA_HEADS, SEQ])
            row_max = mb("row_max", [P, 16])
            row_sum = mb("row_sum", [P, 16])
            row_inv = mb("row_inv", [P, 16])
            head_ms = mb("head_ms", [P, 8])
            head_r = mb("head_r", [P, 8])
            pair_f = shared[:, 0:2, :].rearrange("p a n -> p (a n)")[:, 0:7 * P].rearrange("p (m t) -> p m t", m=7)
            xc = shared[:, 0, :].rearrange("p (c t) -> p c t", c=2)
            lgate, lgelu, lt = shared[:, 1, :], shared[:, 2, :], shared[:, 3, :]
            lr, li, la = run[0], run[1], logf
            hgate = logf[:, :].rearrange("p (t n) -> p t n", t=TB)
            hgate_sig = sig[:, :].rearrange("p (t n) -> p t n", t=TB)
            dv = [run[n][:, :].rearrange("p (t n) -> p t n", t=TB) for n in (2, 1)]
            prob1 = shared[:, :, :].rearrange("p a n -> p (a n)").rearrange(
                "p (m h k) -> p m h k", m=2, h=DA_HEADS)
            prob0 = sides_t[:, :, :].rearrange("p m (h k) -> p m h k", h=DA_HEADS)
            hsq, hout = rel
            dsq = shared[:, 0:2, :]
            dout = shared[:, 2:4, :]
        xs_hi = sb("xs_hi", [P, TB, D], f32r)
        xs_lo = sb("xs_lo", [P, TB, D], f32r)
        y_hi = sb("y_hi", [P, D], f32r)
        y_lo = sb("y_lo", [P, D], f32r)
        hid_sig = sb("hid_sig", [P, 512])
        hid2 = [sb(f"hid{n}", [P, 512]) for n in range(2)]
        hid = hid2[0]
        rw = sb("rw", [P, DC, E])
        rw_hi = sb("rw_hi", [P, DC, E], f32r)
        rw_lo = sb("rw_lo", [P, DC, E], f32r)
        logit = sb("logit", [P, TB, E])
        best = sb("best", [P, TB, 8])
        best_at = sb("best_at", [P, TB, 8], u32)
        best_f = sb("best_f", [P, TB, 8])
        hot = sb("hot", [P, TOP_K, TB, E])
        gates = sb("gates", [P, 4, TB])
        routed = sb("routed", [P, TB, E])
        combine = sb("combine", [P, TB, ITEMS])
        place = sb("place", [P, TB, ITEMS])
        over = sb("over", [P, 3, E])
        over_sel = sb("over_sel", [P, E])
        over_tmp = sb("over_tmp", [P, TB, E])
        item_f = sb("item_f", [P, 1 + ITEMS])
        item_i = sb("item_i", [P, 1 + ITEMS], i32)
        pick = sb("pick", [P, TB, P], f32r)
        pickT = sb("pickT", [P, SEQ], f32r)
        gate_tok = sb("gate_tok", [P, TB])
        gate_slot = sb("gate_slot", [P, 1])

        bank = [ctx.enter_context(nc.psum_tensor(f"bank{k}", [P, 512], f32)) for k in range(8)]

        full = [sem(f"full{k}") for k in range(SLOT_RAW)]
        hi_ready, lo_ready, used = sem("hi_ready"), sem("lo_ready"), sem("used")
        x_in, vec_in, gate_in, lam_in, norm_in, rw_in, stored = [
            sem(n) for n in "x_in vec_in gate_in lam_in norm_in rw_in stored".split()]
        consts, consts2, lam_taken, vecT_done, vec_done, lam_done, lamB_done, lx_blank = [
            sem(n) for n in "consts consts2 lam_taken vecT_done vec_done lam_done lamB_done lx_blank".split()]
        x_ready, xT_done, xT_hi_ready, xT_lo_ready, norm_used = [
            sem(n) for n in "x_ready xT_done xT_hi_ready xT_lo_ready norm_used".split()]
        taken, f_ready, k_sig, logf_done, qk_ready, rel_done, exp_done, side_done, level_done, level_taken = [
            sem(n) for n in ("taken f_ready k_sig logf_done qk_ready rel_done exp_done side_done "
                             "level_done level_taken").split()]
        xc_ready, gates_done, act_lru, tanh_done, root_in, root_done, gelu_in, gelu_sig, lru_out, lru_hi = [
            sem(n) for n in ("xc_ready gates_done act_lru tanh_done root_in root_done gelu_in gelu_sig "
                             "lru_out lru_hi").split()]
        score_done, score_taken, max_done, prob_done, w_done, wT_done, wT_taken = [
            sem(n) for n in "score_done score_taken max_done prob_done w_done wT_done wT_taken".split()]
        hpv_done, hsq_done, hms_done, hstd_done, hout_done, hT_done, hT_hi_ready, mix_lo = [
            sem(n) for n in "hpv_done hsq_done hms_done hstd_done hout_done hT_done hT_hi_ready mix_lo".split()]
        dpv_done, dsq_done, dms_done, dstd_done, dout_done, dT_done, dT_hi_ready = [
            sem(n) for n in "dpv_done dsq_done dms_done dstd_done dout_done dT_done dT_hi_ready".split()]
        hg_sig, var_done, ln_std = [sem(n) for n in "hg_sig var_done ln_std".split()]
        d_silu, d_h, d_hi, d_lo = [sem(n) for n in "d_silu d_h d_hi d_lo".split()]
        rw_split, logit_done, gap_done, gap_exp, routed_done, rank_done, items_done, xs_hi_done, xs_done = [
            sem(n) for n in ("rw_split logit_done gap_done gap_exp routed_done rank_done items_done "
                             "xs_hi_done xs_done").split()]
        m_pick, m_slot, m_gath, m_xg_hi, m_xg_lo, m_silu, m_h, m_T, m_T_hi, m_T_lo, m_y_hi, m_y_lo, m_back, m_acc = [
            sem(n) for n in ("m_pick m_slot m_gath m_xg_hi m_xg_lo m_silu m_h m_T m_T_hi m_T_lo m_y_hi m_y_lo "
                             "m_back m_acc").split()]
        dve_step, act_step, pool_step = sem("dve_step"), sem("act_step"), sem("pool_step")

        def ring(c, turns=0):
            return c % SLOT_RAW, c % SLOT_SPLIT, 16 * (c // SLOT_RAW + 1) + 16 * turns, c + SLOT_RAW * turns

        actT = [t[:, :].rearrange("p (c t) -> p c t", c=DC) for t in (actT_hi, actT_lo)]
        xg = [t[:, 0:DC * P].rearrange("p (c t) -> p c t", c=DC) for t in (actT_hi, actT_lo)]
        mixT = [t[:, :].rearrange("p (c t) -> p c t", c=DC) for t in (mixT_hi, mixT_lo)]

        in_v = w_in.rearrange("l (c p) (b n) -> l b p c n", p=P, n=256)
        out_v = w_out.rearrange("l (q c p) n -> l q p c n", p=P, c=2)
        up_v = [w[0].rearrange("(c p) (b n) -> b p c n", p=P, n=256) for w in (ffn_wg, ffn_wu)]
        down_v = ffn_wd[0].rearrange("(q c p) n -> q p c n", p=P, c=2)
        moe_up_v = [w[0].rearrange("e (c p) (b n) -> e b p c n", p=P, n=512) for w in (moe_wg, moe_wu)]
        moe_down_v = moe_wd[0].rearrange("e (q c p) n -> (e q) p c n", p=P, c=2)

        block = ctx.enter_context(nc.Block())

        @block.sync
        def _(sp):
            for t in range(TB):
                sp.dma_start(xres[:, t, :], x[0, t * P:(t + 1) * P, :]).then_inc(x_in, 16)

            def load(c, src, turns=0, reuse=True):
                slot, _, _, n = ring(c, turns)
                if reuse:
                    sp.wait_ge(lo_ready, n - SLOT_RAW + 1)
                dst = raw[slot][:, :].rearrange("p (c n) -> p c n", c=src.shape[1])
                sp.dma_start(dst, src).then_inc(full[slot], 16)

            def load_mixer(l):
                for j in range(NCOL):
                    load(MIX0[l] + j, in_v[l, ORDER[j]], reuse=MIX0[l] + j >= SLOT_RAW)
                for j, q in enumerate(OUT_ORDER):
                    load(MIX0[l] + NCOL + j, out_v[l, q])

            def load_up(c, m, e, b, turns):
                for h in range(2):
                    load(c + h, moe_up_v[m][e, b, :, 4 * h:4 * h + 4, :], turns)

            def load_down(c, e, b, turns):
                for h in range(2):
                    load(c + h, moe_down_v[2 * FB * e + 2 * b + h], turns)

            def load_blocks(e, i, last):
                load_up(ITEM0, 1, e, 1, FB * i)
                load_down(ITEM0 + 2, e, 0, FB * i)
                with sp.Fori(2, FB) as fb:
                    turns = FB * i + fb - 2
                    load_up(ITEM0 + 4, 0, e, fb, turns)
                    load_up(ITEM0 + 6, 1, e, fb, turns)
                    load_down(ITEM0 + 8, e, fb - 1, turns)
                if last:
                    load_down(SEAM0, e, FB - 1, FB * i)

            def load_seam(e, e_next, i):
                load_up(SEAM0, 0, e_next, 0, FB * i)
                load_up(SEAM0 + 2, 1, e_next, 0, FB * i)
                load_down(SEAM0 + 4, e, FB - 1, FB * i)
                load_up(SEAM0 + 6, 0, e_next, 1, FB * i)

            load_mixer(0)
            with sp.Fori(0, FB) as fb:
                for h in range(2):
                    for m in range(2):
                        load(DENSE0 + 2 * h + m, up_v[m][2 * fb + h], fb)
                for h in range(2):
                    load(DENSE0 + 4 + h, down_v[2 * fb + h], fb)
            load_mixer(1)
            load_up(MOE0, 0, 0, 0, 0)
            load_up(MOE0 + 2, 1, 0, 0, 0)
            load_up(MOE0 + 4, 0, 0, 1, 0)
            with sp.Fori(0, E - 1) as i:
                load_blocks(i, i, False)
                load_seam(i, i + 1, i)
            sp.wait_ge(items_done, 1)
            last_item = sp.value_load(item_i[0:1, 0:1], min_val=E - 1, max_val=ITEMS - 1)
            with sp.If(last_item > E - 1):
                with sp.Fori(E - 1, last_item) as i:
                    e = sp.value_load(item_i[0:1, bass.ds(i + 1, 1)], min_val=0, max_val=E - 1)
                    load_blocks(e, i, False)
                    e_next = sp.value_load(item_i[0:1, bass.ds(i + 2, 1)], min_val=0, max_val=E - 1)
                    load_seam(e, e_next, i)
            with sp.Fori(last_item, last_item + 1) as i:
                e = sp.value_load(item_i[0:1, bass.ds(i + 1, 1)], min_val=0, max_val=E - 1)
                load_blocks(e, i, True)
            for t in range(TB):
                sp.wait_ge(x_ready, TB * (2 * DEPTH - 1) + t + 1)
                sp.dma_start(out[0, t * P:(t + 1) * P, :], xres[:, t, :]).then_inc(stored, 16)
            sp.wait_ge(stored, 16 * TB)

        @block.gpsimd
        def _(pool):
            count = [0]

            def step(ins):
                count[0] += 1
                ins.then_inc(pool_step, 1)
                pool.wait_ge(pool_step, count[0])

            def select(t, pattern, op, base, mult, fill=0.0):
                step(pool.affine_select(out=t, in_=t, pattern=pattern, compare_op=op, fill=fill,
                                        base=base, channel_multiplier=mult))

            step(pool.memset(ident[:, :], 0.0))
            pool.affine_select(out=ident[:, :], in_=ident[:, :], pattern=[[-1, P]], compare_op=ALU.not_equal,
                               fill=1.0, base=0, channel_multiplier=1).then_inc(consts, 1)
            for g, t in ((lru_wa, gate_a), (lru_wx, gate_x)):
                step(pool.memset(t[:, :, :, :], 0.0))
                view = g.rearrange("l (c h) i j -> h i (l c) j", h=2)
                for h in range(2):
                    rows = slice(64 * h, 64 * h + 64)
                    dst = t[rows, :, :, 64 * h:64 * h + 64].rearrange("p l c j -> p (l c) j")
                    pool.dma_start(dst, view[h]).then_inc(gate_in, 16)
            pool.memset(lx[:, :, 0:3], 0.0).then_inc(lx_blank, 1)
            for n in range(2 * DEPTH):
                g, b = ((ln1_g, ln1_b), (ln2_g, ln2_b))[n % 2]
                if n:
                    pool.wait_ge(norm_used, n)
                pool.dma_start(norm_gb[:, 0, :], g[n // 2:n // 2 + 1, :].to_broadcast((P, D))).then_inc(norm_in, 16)
                pool.dma_start(norm_gb[:, 1, :], b[n // 2:n // 2 + 1, :].to_broadcast((P, D))).then_inc(norm_in, 16)
                if n:
                    continue
                step(pool.memset(eps[:, :], EPS))
                step(pool.memset(ones[:, :], 1.0))
                step(pool.memset(zeros[:, :], 0.0))
                for m, width in enumerate((16, 64, 256)):
                    step(pool.memset(keep[m][:, :], 1.0))
                    step(pool.memset(keep[m][:, :].rearrange("p (b w) -> p b w", w=width)[:, :, 0:1], 0.0))
                step(pool.memset(pair_f[:, :, :], 0.0))
                for m in range(7):
                    h = 1 << m
                    nb = P // (2 * h)
                    odd = pair_f[:, m, :].rearrange("p (b two h) -> p b two h", two=2, h=h)[:, :, 1, :]
                    step(pool.memset(odd, 1.0))
                    select(odd, [[-2 * h, nb], [0, h]], ALU.is_ge, 0, 1)
                    select(odd, [[2 * h, nb], [0, h]], ALU.is_ge, h - 1, -1)
                step(pool.tensor_copy(pair[:, :, :], pair_f[:, :, :]))
                step(pool.memset(far_mask[:, :], 0.0))
                select(far_mask[:, P:2 * P], [[-1, P]], ALU.is_ge, 0, 1, FAR)
                step(pool.memset(before[:, :], 1.0))
                select(before[:, :], [[1, P]], ALU.is_gt, 0, -1)
                pool.iota(iota_row[:, :], pattern=[[1, P]], base=0, channel_multiplier=0,
                          allow_small_or_imprecise_dtypes=True).then_inc(consts2, 1)

        @block.tensor
        def _(pe):
            def product(o, a, b, first, last):
                pe.matmul(o, a[0], b[0], start=first, stop=False, skip_group_check=True)
                pe.matmul(o, a[1], b[0], start=False, stop=False, skip_group_check=True)
                return pe.matmul(o, a[0], b[1], start=False, stop=last, skip_group_check=True)

            def piece(c, width, turns=0):
                _, k, _, n = ring(c, turns)
                pe.wait_ge(lo_ready, n + 1)
                return [t[:, :].rearrange("p (c n) -> p c n", n=width) for t in (w_hi[k], w_lo[k])]

            def transpose_x(n):
                for t in range(TB):
                    if n == 0:
                        pe.wait_ge(x_in, 16 * TB)
                        pe.wait_ge(consts, 1)
                    else:
                        pe.wait_ge(x_ready, TB * (n - 1) + t + 1)
                    for c in range(DC):
                        o = bank[c // 2][:, (c % 2) * SEQ + t * P:(c % 2) * SEQ + (t + 1) * P]
                        last = pe.transpose(o, xres[:, t, c * P:(c + 1) * P], ident[:, :])
                last.then_inc(xT_done, 1)
                pe.wait_ge(xT_lo_ready, 4 * (n + 1))

            def project(l, j):
                w = piece(MIX0[l] + j, 256)
                if j >= 4:
                    pe.wait_ge(taken, NCOL * l + j - 3)
                for g in range(2):
                    for c in range(DC):
                        if ORDER[j] in TOKEN_MAJOR:
                            a = [t[:, c, g * P:(g + 1) * P] for t in actT]
                            b = [t[:, c, :] for t in w]
                        else:
                            a = [t[:, c, g * P:(g + 1) * P] for t in w]
                            b = [t[:, c, :] for t in actT]
                        last = product(bank[j % 4][:, g * 256:(g + 1) * 256], a, b, c == 0, c == DC - 1)
                last.then_inc(used, 1)

            def level(l, m):
                if m == 0:
                    pe.wait_ge(qk_ready, l + 1)
                    a, b = hk[:, :], hq[:, :]
                else:
                    pe.wait_ge(side_done, 8 * l + m)
                    a = b = side[m % 2]
                    pe.wait_ge(level_taken, HG_LEVELS * l + m)
                for h in range(2):
                    r = slice(64 * h, 64 * h + 64)
                    for c in range(2):
                        if m == HG_LEVELS - 1:
                            last = pe.matmul(bank[4 + h][:, c * P:(c + 1) * P], a[r, c * SEQ:c * SEQ + P],
                                             b[r, c * SEQ + P:(c + 1) * SEQ], start=True, stop=True)
                            continue
                        for t in range(TB):
                            s = slice(c * SEQ + t * P, c * SEQ + (t + 1) * P)
                            last = pe.matmul(bank[4 + h][:, t * 256 + c * P:t * 256 + (c + 1) * P],
                                             a[r, s], b[r, s], start=True, stop=True)
                last.then_inc(level_done, 1)

            def lru_gates(l):
                pe.wait_ge(xc_ready, l + 1)
                pe.wait_ge(gate_in, 64)
                for k, g in enumerate((gate_a, gate_x)):
                    for c in range(2):
                        last = pe.matmul(bank[6 + k][:, c * SEQ:(c + 1) * SEQ], g[:, l, c, :], xc[:, c, :],
                                         start=True, stop=True)
                last.then_inc(gates_done, 1)

            def scores(l, r):
                if r == 0:
                    pe.wait_ge(taken, NCOL * l + 9)
                    pe.wait_ge(act_lru, l + 1)
                else:
                    pe.wait_ge(score_taken, 3 * l + r)
                for m in range(2):
                    rows = slice(64 * m, 64 * m + 64)
                    if r < 2:
                        for h in range(2):
                            last = pe.matmul(bank[6 + m][:, h * 256:(h + 1) * 256], dq[rows, 2 * r + h, P:2 * P],
                                             dk[rows, 2 * r + h, :], start=True, stop=True)
                    else:
                        for h in range(DA_HEADS):
                            last = pe.matmul(bank[6 + m][:, h * P:(h + 1) * P], dq[rows, h, 0:P],
                                             dk[rows, h, 0:P], start=True, stop=True)
                last.then_inc(score_done, 1)

            def out_project(l, j):
                w = piece(MIX0[l] + NCOL + j, D)
                for c in range(2):
                    d = 2 * OUT_ORDER[j] + c
                    for t in range(TB):
                        for h in range(2):
                            last = product(bank[2 * t + h][:, :], [m[:, d, t * P:(t + 1) * P] for m in mixT],
                                           [v[:, c, h * 512:(h + 1) * 512] for v in w],
                                           j == 0 and c == 0, j == 3 and c == 1)
                last.then_inc(used, 1)

            pe.wait_ge(consts, 1)
            pe.wait_ge(vec_in, 16 * 8)
            pe.transpose(bank[7][:, 0:N_VEC], vec_rows[:, :], ident[0:N_VEC, 0:N_VEC]).then_inc(vecT_done, 1)

            for l in range(DEPTH):
                transpose_x(2 * l)
                for j in range(NCOL):
                    project(l, j)
                    if j == 4 and l == 0:
                        pe.wait_ge(consts2, 1)
                        pe.wait_ge(lam_done, 1)
                        pe.matmul(bank[7][:, 0:DEPTH], ones[0:1, :], lam_one[:, :], start=True,
                                  stop=True).then_inc(lamB_done, 1)
                    if j >= 3:
                        level(l, j - 3)
                    if j == 5:
                        if l == 0:
                            pe.wait_ge(lam_taken, 1)
                        lru_gates(l)
                    if j >= 9:
                        scores(l, j - 9)
                pe.wait_ge(taken, NCOL * (l + 1))
                pe.wait_ge(mix_lo, 3 * l + 1)
                out_project(l, 0)
                pe.wait_ge(level_taken, HG_LEVELS * (l + 1))
                for t in range(TB):
                    for u in range(4):
                        head = 2 * (u % 2) + u // 2
                        o = bank[4 + t][:, head * 64:(head + 1) * 64]
                        v = [hv[:, b, head * 64:(head + 1) * 64] for b in range(TB)]
                        last = pe.matmul(o, pairT[:, t, u, :], v[t], start=True, stop=t == 0)
                        if t == 1:
                            last = pe.matmul(o, pairT[:, 2, u, :], v[0], start=False, stop=True)
                last.then_inc(hpv_done, 1)
                pe.wait_ge(hout_done, l + 1)
                for c in range(2):
                    for t in range(TB):
                        last = pe.transpose(bank[4][:, c * SEQ + t * P:c * SEQ + (t + 1) * P],
                                            hout[:, :].rearrange("p (t n) -> p t n", t=TB)[:, t, c * P:(c + 1) * P],
                                            ident[:, :])
                last.then_inc(hT_done, 1)
                pe.wait_ge(mix_lo, 3 * l + 2)
                out_project(l, 1)
                pe.wait_ge(w_done, l + 1)
                for b, w in enumerate((prob0[:, 0, :, :], prob1[:, 0, :, P:2 * P], prob1[:, 0, :, 0:P])):
                    for h in range(DA_HEADS):
                        last = pe.transpose(bank[5 + b][:, h * P:(h + 1) * P], w[:, h, :], ident[:, :])
                last.then_inc(wT_done, 1)
                pe.wait_ge(wT_taken, l + 1)
                for t in range(TB):
                    for h in range(DA_HEADS):
                        o = bank[4 + t][:, h * P:(h + 1) * P]
                        last = pe.matmul(o, pairT[:, t, h, :], dv[h // 2][:, t, (h % 2) * P:(h % 2 + 1) * P], start=True, stop=t == 0)
                        if t == 1:
                            last = pe.matmul(o, pairT[:, 2, h, :], dv[h // 2][:, 0, (h % 2) * P:(h % 2 + 1) * P],
                                             start=False, stop=True)
                last.then_inc(dpv_done, 1)
                pe.wait_ge(dout_done, l + 1)
                for h in range(DA_HEADS):
                    for t in range(TB):
                        last = pe.transpose(bank[6 + h // 2][:, (h % 2) * SEQ + t * P:(h % 2) * SEQ + (t + 1) * P],
                                            dout[:, t, h * P:(h + 1) * P], ident[:, :])
                last.then_inc(dT_done, 1)
                pe.wait_ge(mix_lo, 3 * l + 3)
                out_project(l, 2)
                out_project(l, 3)
                transpose_x(2 * l + 1)
                if l:
                    continue
                for k in range(4):
                    pe.matmul(bank[4 + k][:, :], zeros[:, :], keep[0][:, :], start=True, stop=False,
                              skip_group_check=True)
                with pe.Fori(0, FB) as fb:
                    for k in range(4):
                        w = piece(DENSE0 + k, 256, fb)
                        for g in range(2):
                            for c in range(DC):
                                last = product(bank[k][:, g * SEQ:(g + 1) * SEQ],
                                               [t[:, c, g * P:(g + 1) * P] for t in w],
                                               [t[:, c, :] for t in actT], c == 0, c == DC - 1)
                        last.then_inc(used, 1)
                    for h in range(2):
                        w = piece(DENSE0 + 4 + h, D, fb)
                        pe.wait_ge(d_lo, 2 * fb + h + 1)
                        for c in range(2):
                            for t in range(TB):
                                for n in range(2):
                                    last = product(bank[4 + 2 * t + n][:, :],
                                                   [m[:, 2 * h + c, t * P:(t + 1) * P] for m in mixT],
                                                   [v[:, c, n * 512:(n + 1) * 512] for v in w], False, True)
                        last.then_inc(used, 1)

            pe.wait_ge(rw_split, 1)
            for t in range(TB):
                for c in range(DC):
                    last = product(bank[4][:, t * E:(t + 1) * E], [a[:, c, t * P:(t + 1) * P] for a in actT],
                                   [rw_hi[:, c, :], rw_lo[:, c, :]], c == 0, c == DC - 1)
            last.then_inc(logit_done, 1)
            pe.wait_ge(routed_done, 1)
            pe.matmul(bank[5][:, 0:E], before[:, :], routed[:, 0, :], start=True, stop=True)
            pe.matmul(bank[5][:, E:2 * E], before[:, :], routed[:, 1, :], start=True, stop=False)
            pe.matmul(bank[5][:, E:2 * E], ones[:, :], routed[:, 0, :], start=False, stop=True)
            pe.matmul(bank[5][:, 2 * E:3 * E], ones[:, :], routed[:, 0, :], start=True, stop=False)
            pe.matmul(bank[5][:, 2 * E:3 * E], ones[:, :], routed[:, 1, :], start=False,
                      stop=True).then_inc(rank_done, 1)

            pe.wait_ge(items_done, 1)
            pe.wait_ge(xs_done, 1)
            last_item = pe.value_load(item_i[0:1, 0:1], min_val=E - 1, max_val=ITEMS - 1)
            hT = [t[:, 0:4 * P].rearrange("p (c t) -> p c t", c=4) for t in (mixT_hi, mixT_lo)]

            def up(c, m, turns):
                for h in range(2):
                    w = piece(c + h, 512, turns)
                    for k in range(4):
                        last = product(bank[m][:, :], [a[:, 4 * h + k, :] for a in xg],
                                       [t[:, k, :] for t in w], h + k == 0, h + k == 4)
                    last.then_inc(used, 1)

            def turn(n):
                pe.wait_ge(m_h, n)
                for k in range(4):
                    last = pe.transpose(bank[2][:, k * P:(k + 1) * P], hid[:, k * P:(k + 1) * P], ident[:, :])
                last.then_inc(m_T, 1)

            def down(c, n, turns, end=False):
                pe.wait_ge(m_T_lo, n)
                for h in range(2):
                    w = piece(c + h, D, turns)
                    for k in range(2):
                        for m in range(2):
                            last = product(bank[4 + m][:, :], [t[:, 2 * h + k, :] for t in hT],
                                           [t[:, k, m * 512:(m + 1) * 512] for t in w],
                                           False, end and h + k == 2)
                    last.then_inc(used, 1)

            def gather(n):
                pe.wait_ge(m_pick, n)
                for t in range(TB):
                    pe.transpose(bank[3][:, t * P:(t + 1) * P], pick[:, t, :].bitcast(f32), ident[:, :])
                for t in range(TB):
                    pe.matmul(bank[3][:, SEQ:SEQ + 1], pick[:, t, :].bitcast(f32), gate_tok[:, t:t + 1],
                              start=t == 0, stop=t == TB - 1)
                for c in range(DC):
                    for t in range(TB):
                        for k, x_part in enumerate((xs_hi, xs_lo)):
                            last = pe.matmul(bank[6 + c // 4][:, (c % 4) * P:(c % 4 + 1) * P],
                                             x_part[:, t, c * P:(c + 1) * P], pick[:, t, :],
                                             start=t + k == 0, stop=t + k == 2)
                last.then_inc(m_gath, 1)

            def scatter(n):
                pe.wait_ge(m_y_lo, n)
                for t in range(TB):
                    for h in range(2):
                        o = bank[4 + 2 * t + h][:, :]
                        pe.matmul(o, pickT[:, t * P:(t + 1) * P], y_hi[:, h * 512:(h + 1) * 512],
                                  start=True, stop=False)
                        pe.matmul(o, pickT[:, t * P:(t + 1) * P], y_lo[:, h * 512:(h + 1) * 512],
                                  start=False, stop=True).then_inc(m_back, 1)

            def start_item(i):
                turn(FB * i + 1)
                up(ITEM0, 1, FB * i)
                pe.wait_ge(m_acc, 4 * i + 4)
                for m in range(2):
                    pe.matmul(bank[4 + m][:, :], zeros[:, :], keep[0][:, :], start=True, stop=False,
                              skip_group_check=True)
                down(ITEM0 + 2, FB * i + 1, FB * i)

            def middle(c, n, turns, before_down=None):
                pe.wait_ge(m_silu, n)
                up(c, 0, turns)
                turn(n)
                up(c + 2, 1, turns)
                if before_down is not None:
                    gather(before_down)
                down(c + 4, n, turns)

            gather(1)
            pe.wait_ge(m_xg_lo, 1)
            up(MOE0, 0, 0)
            up(MOE0 + 2, 1, 0)
            pe.wait_ge(m_silu, 1)
            up(MOE0 + 4, 0, 0)
            with pe.Fori(0, last_item) as i:
                start_item(i)
                with pe.Fori(2, FB - 1) as fb:
                    middle(ITEM0 + 4, FB * i + fb, FB * i + fb - 2)
                middle(SEAM0 - 6, FB * i + FB - 1, FB * i, i + 2)
                pe.wait_ge(m_silu, FB * i + FB)
                pe.wait_ge(m_xg_lo, i + 2)
                up(SEAM0, 0, FB * i)
                turn(FB * i + FB)
                up(SEAM0 + 2, 1, FB * i)
                down(SEAM0 + 4, FB * i + FB, FB * i)
                pe.wait_ge(m_silu, FB * i + FB + 1)
                up(SEAM0 + 6, 0, FB * i)
                scatter(i + 1)
            i = last_item
            start_item(i)
            with pe.Fori(2, FB) as fb:
                middle(ITEM0 + 4, FB * i + fb, FB * i + fb - 2)
            turn(FB * i + FB)
            down(SEAM0, FB * i + FB, FB * i, True)
            scatter(i + 1)

        @block.scalar
        def _(act):
            count = [0]

            def step(ins):
                count[0] += 1
                ins.then_inc(act_step, 1)
                act.wait_ge(act_step, count[0])

            def hi(c, turns=0):
                slot, k, landed, n = ring(c, turns)
                act.wait_ge(full[slot], landed)
                if c >= SLOT_SPLIT:
                    act.wait_ge(used, n - SLOT_SPLIT + 1)
                act.activation(w_hi[k][:, :], raw[slot][:, :], ACT.Copy).then_inc(hi_ready, 1)

            def xT_hi(n):
                act.wait_ge(xT_done, n + 1)
                for k in range(4):
                    act.activation(actT_hi[:, k * 512:(k + 1) * 512], bank[k][:, :],
                                   ACT.Copy).then_inc(xT_hi_ready, 1)

            rows = [(hg_lb_logits, C_LB, 4), (hg_norm_g, C_HGN, 4), (lru_conv_b, C_CB, 4), (lru_ba, C_BA, 4),
                    (lru_bx, C_BX, 4), (lru_lambda, C_LAM, 4), (da_norm_g, C_DAN, 8)]
            for v, at, n in rows:
                act.dma_start(vec_rows[at:at + n, :], v.rearrange("l (c p) -> (l c) p", p=P)).then_inc(vec_in, 16)
            act.dma_start(vec_rows[C_CW:C_CW + 16, :],
                          lru_conv_w.rearrange("l j (c p) -> (l j c) p", p=P)).then_inc(vec_in, 16)
            for k, v in enumerate((da_lq1, da_lk1, da_lq2, da_lk2)):
                act.dma_start(lam_rows[:, k, :], v.rearrange("(a l) d -> a (l d)", a=1)).then_inc(lam_in, 16)

            def exps(l, m):
                act.wait_ge(rel_done, 8 * l + m)
                act.activation(rel[m % 2][:, :], rel[m % 2][:, :], ACT.Exp).then_inc(exp_done, 1)

            for l in range(DEPTH):
                if l:
                    for c in range(3):
                        hi(MIX0[l] + c)
                xT_hi(2 * l)
                if l == 0:
                    act.wait_ge(vec_done, 1)
                    act.activation(soft[:, 0, :], soft[:, 0, :], ACT.Exp)
                    act.activation(lb_tmp[:, 0:4], lb_tmp[:, 0:4], ACT.Exp)
                    act.activation(lam_sum[:, :], lam_sum[:, :], ACT.Exp).then_inc(lam_done, 1)
                    for c in range(3):
                        hi(MIX0[l] + c)
                for j in range(NCOL):
                    hi(MIX0[l] + j + 3)
                    act.wait_ge(used, MIX0[l] + j + 1)
                    b = bank[j % 4]
                    b3 = b[:, :].rearrange("p (t n) -> p t n", t=2)
                    kind = ORDER[j]
                    if kind == HQ:
                        act.activation(hq[:, :], b[:, :], ACT.Copy)
                        done = act.activation(sig[:, :], b[:, :], ACT.Sigmoid)
                    elif kind == HF:
                        act.activation(logf[:, :], b[:, :], ACT.Sigmoid)
                        done = act.activation(hk[:, :], b[:, :], ACT.Sigmoid, scale=-1.0)
                    elif kind == HI:
                        done = act.activation(hv[:, :, :], b3, ACT.Copy)
                    elif kind == HG:
                        act.activation(hgate, b3, ACT.Copy)
                        done = act.activation(hgate_sig, b3, ACT.Sigmoid)
                    elif kind == LX:
                        if l == 0:
                            act.wait_ge(lx_blank, 1)
                        done = act.activation(lx[:, :, 3:3 + SEQ], b3, ACT.Copy)
                    elif kind == LG:
                        if l == 0:
                            act.wait_ge(consts2, 1)
                        act.activation(lgate, b[:, :], ACT.Copy)
                        done = act.activation(lgelu, b[:, :], ACT.Square)
                    elif kind in (DQ, DQ + 1):
                        h = 2 * (kind - DQ)
                        done = act.activation(dq[:, h:h + 2, :], b3, ACT.Copy)
                    elif kind in (DK, DK + 1):
                        h = 2 * (kind - DK)
                        done = act.activation(dk[:, h:h + 2, :], b3, ACT.Copy)
                    else:
                        done = act.activation(dv[kind - DV], b3, ACT.Copy)
                    done.then_inc(taken, 1)
                    if j == 2:
                        act.wait_ge(f_ready, l + 1)
                        act.activation(logf[:, :], logf[:, :], ACT.Ln).then_inc(logf_done, 1)
                        exps(l, 1)
                        exps(l, 2)
                    if 3 <= j <= 8:
                        exps(l, j)
                    if j == 6:
                        act.wait_ge(gates_done, l + 1)
                        for c in range(2):
                            s = slice(c * SEQ, (c + 1) * SEQ)
                            act.activation(lr[:, s], bank[6][:, s], ACT.Sigmoid,
                                           bias=vec[:, C_BA + 2 * l + c:C_BA + 2 * l + c + 1])
                            last = act.activation(li[:, s], bank[7][:, s], ACT.Sigmoid,
                                                  bias=vec[:, C_BX + 2 * l + c:C_BX + 2 * l + c + 1])
                        last.then_inc(act_lru, 1)
                        act.wait_ge(act_lru, l + 1)
                        act.wait_ge(gelu_in, l + 1)
                        act.activation(lgelu, lgelu, ACT.Sigmoid).then_inc(gelu_sig, 1)
                        for c in range(2):
                            s = slice(c * SEQ, (c + 1) * SEQ)
                            act.activation(lt[:, s], lr[:, s], ACT.Tanh,
                                           scale=decay_neg[:, 2 * l + c:2 * l + c + 1])
                            last = act.activation(la[:, s], lr[:, s], ACT.Exp,
                                                  scale=decay[:, 2 * l + c:2 * l + c + 1])
                        last.then_inc(tanh_done, 1)
                    if j == 9:
                        act.wait_ge(root_in, l + 1)
                        act.activation(lt, lt, ACT.Sqrt).then_inc(root_done, 1)
                        act.wait_ge(lru_out, l + 1)
                        act.activation(mixT_hi[:, 2 * SEQ:4 * SEQ], lr[:, :], ACT.Copy).then_inc(lru_hi, 1)
                act.wait_ge(max_done, l + 1)
                for k in range(16):
                    t = (prob1 if k < 8 else prob0)[:, (k // 4) % 2, k % 4, :]
                    last = act.activation(t, t, ACT.Exp, bias=row_max[:, k:k + 1], scale=DA_DIM ** -0.5,
                                          accum_out=row_sum[:, k:k + 1])
                last.then_inc(prob_done, 1)
                hi(MIX0[l] + N_MIX - 1)
                act.wait_ge(hpv_done, l + 1)
                for t in range(TB):
                    last = act.activation(hsq[:, t * 256:(t + 1) * 256], bank[4 + t][:, 0:256], ACT.Square)
                last.then_inc(hsq_done, 1)
                act.wait_ge(hms_done, l + 1)
                act.activation(head_r[:, :], head_ms[:, :], ACT.Sqrt, bias=eps[:, :],
                               scale=1.0 / HG_DIM).then_inc(hstd_done, 1)
                act.wait_ge(hT_done, l + 1)
                for c in range(2):
                    last = act.activation(mixT_hi[:, c * SEQ:(c + 1) * SEQ], bank[4][:, c * SEQ:(c + 1) * SEQ],
                                          ACT.Copy, scale=vec[:, C_HGN + 2 * l + c:C_HGN + 2 * l + c + 1])
                last.then_inc(hT_hi_ready, 1)
                act.wait_ge(wT_done, l + 1)
                for b in range(3):
                    last = act.activation(pairT[:, b, :, :], bank[5 + b][:, :].rearrange("p (h t) -> p h t", h=4),
                                          ACT.Copy)
                last.then_inc(wT_taken, 1)
                act.wait_ge(dpv_done, l + 1)
                for t in range(TB):
                    last = act.activation(dsq[:, t, :], bank[4 + t][:, :], ACT.Square)
                last.then_inc(dsq_done, 1)
                act.wait_ge(dms_done, l + 1)
                act.activation(head_r[:, :], head_ms[:, :], ACT.Sqrt, bias=eps[:, :],
                               scale=1.0 / (2 * DA_DIM)).then_inc(dstd_done, 1)
                act.wait_ge(dT_done, l + 1)
                for h in range(DA_HEADS):
                    last = act.activation(mixT_hi[:, (4 + h) * SEQ:(5 + h) * SEQ],
                                          bank[6 + h // 2][:, (h % 2) * SEQ:(h % 2 + 1) * SEQ], ACT.Copy,
                                          scale=da_g[:, 4 * l + h:4 * l + h + 1])
                last.then_inc(dT_hi_ready, 1)

                def norm_std(n):
                    act.wait_ge(var_done, n + 1)
                    act.activation(std[:, :], mean_var[:, :, 1], ACT.Sqrt, bias=eps[:, :]).then_inc(ln_std, 1)

                norm_std(2 * l)
                xT_hi(2 * l + 1)
                if l:
                    continue
                with act.Fori(0, FB) as fb:
                    def hidden(h):
                        act.wait_ge(used, DENSE0 + 2 * h + 2 + SLOT_RAW * fb)
                        act.activation(hid_sig[:, :], bank[2 * h][:, :], ACT.Silu).then_inc(d_silu, 1)
                        act.wait_ge(d_h, 2 * fb + h + 1)
                        act.activation(mixT_hi[:, h * 512:(h + 1) * 512], hid2[h][:, :], ACT.Copy).then_inc(d_hi, 1)

                    for k in range(5):
                        hi(DENSE0 + k, fb)
                    hidden(0)
                    hi(DENSE0 + 5, fb)
                    hidden(1)
                norm_std(1)

            act.dma_start(rw[:, :, :], router_w[0].rearrange("(c p) e -> p c e", p=P)).then_inc(rw_in, 16)
            act.wait_ge(rw_in, 16)
            act.activation(rw_hi[:, :, :], rw[:, :, :], ACT.Copy).then_inc(xs_hi_done, 1)
            act.activation(xs_hi[:, :, :], xres[:, :, :], ACT.Copy).then_inc(xs_hi_done, 1)
            act.wait_ge(gap_done, 1)
            act.activation(gates[:, 0, :], gates[:, 3, :], ACT.Exp).then_inc(gap_exp, 1)
            act.wait_ge(items_done, 1)
            last_item = act.value_load(item_i[0:1, 0:1], min_val=E - 1, max_val=ITEMS - 1)

            def silu(n, done):
                act.wait_ge(used, done)
                act.activation(hid_sig[:, :], bank[0][:, :], ACT.Silu).then_inc(m_silu, 1)

            def turned(n):
                act.wait_ge(m_T, n)
                act.activation(mixT_hi[:, 0:512], bank[2][:, :], ACT.Copy).then_inc(m_T_hi, 1)

            def gathered(n):
                act.wait_ge(m_gath, n)
                for k in range(2):
                    last = act.activation(actT_hi[:, k * 512:(k + 1) * 512], bank[6 + k][:, :], ACT.Copy)
                last.then_inc(m_xg_hi, 1)

            def gathered_pick(n):
                act.activation(pickT[:, :], bank[3][:, 0:SEQ], ACT.Copy)
                act.activation(gate_slot[:, :], bank[3][:, SEQ:SEQ + 1], ACT.Copy).then_inc(m_slot, 1)

            def output(n, done):
                act.wait_ge(used, done)
                act.wait_ge(m_slot, n)
                for k in range(2):
                    last = act.activation(y_hi[:, k * 512:(k + 1) * 512], bank[4 + k][:, :], ACT.Copy,
                                          scale=gate_slot[:, :])
                last.then_inc(m_y_hi, 1)

            def start_item(i):
                hi(ITEM0 + 2, FB * i)
                turned(FB * i + 1)
                hi(ITEM0 + 3, FB * i)
                hi(ITEM0 + 4, FB * i)
                silu(FB * i + 2, ITEM0 + 2 + N_FFN * i)

            def middle(c, n, turns):
                for k in range(1, 5):
                    hi(c + k, turns)
                turned(n)
                hi(c + 5, turns)
                hi(c + 6, turns)
                silu(n + 1, c + 4 + SLOT_RAW * turns)

            for k in range(3):
                hi(MOE0 + k)
            gathered(1)
            gathered_pick(1)
            for k in range(3, 7):
                hi(MOE0 + k)
                if k == 6:
                    silu(1, MOE0 + 4)
            hi(MOE0 + 7)
            with act.Fori(0, last_item) as i:
                start_item(i)
                with act.Fori(2, FB - 1) as fb:
                    middle(ITEM0 + 4, FB * i + fb, FB * i + fb - 2)
                middle(SEAM0 - 6, FB * i + FB - 1, FB * i)
                gathered(i + 2)
                for k in range(1, 5):
                    hi(SEAM0 + k, FB * i)
                turned(FB * i + FB)
                hi(SEAM0 + 5, FB * i)
                hi(SEAM0 + 6, FB * i)
                silu(FB * i + FB + 1, SEAM0 + 4 + N_FFN * i)
                hi(SEAM0 + 7, FB * i)
                output(i + 1, SEAM0 + 6 + N_FFN * i)
                hi(SEAM0 + 8, FB * i)
                hi(SEAM0 + 9, FB * i)
                act.wait_ge(m_back, 4 * i + 4)
                gathered_pick(i + 2)
            i = last_item
            start_item(i)
            with act.Fori(2, FB) as fb:
                middle(ITEM0 + 4, FB * i + fb, FB * i + fb - 2)
            hi(SEAM0 + 1, FB * i)
            turned(FB * i + FB)
            output(i + 1, SEAM0 + 2 + N_FFN * i)
            act.wait_ge(var_done, 4)
            act.activation(std[:, :], mean_var[:, :, 1], ACT.Sqrt, bias=eps[:, :]).then_inc(ln_std, 1)

        @block.vector
        def _(dve):
            count = [0]

            def step(ins):
                count[0] += 1
                ins.then_inc(dve_step, 1)
                dve.wait_ge(dve_step, count[0])

            def lo(c, turns=0):
                slot, k, _, n = ring(c, turns)
                dve.wait_ge(hi_ready, n + 1)
                dve.tensor_tensor(w_lo[k][:, :], raw[slot][:, :], w_hi[k][:, :].bitcast(f32),
                                  ALU.subtract).then_inc(lo_ready, 1)

            def xT_lo(n):
                for k in range(4):
                    s = slice(k * 512, (k + 1) * 512)
                    dve.wait_ge(xT_hi_ready, 4 * n + k + 1)
                    dve.tensor_tensor(actT_lo[:, s], bank[k][:, :], actT_hi[:, s].bitcast(f32),
                                      ALU.subtract).then_inc(xT_lo_ready, 1)

            def norm(n):
                for t in range(TB):
                    for h in range(2):
                        step(dve.bn_stats(stats[:, t, h, :], xres[:, t, h * 512:(h + 1) * 512]))
                for t in range(TB):
                    last = dve.bn_aggr(mean_var[:, t, :], stats[:, t, :, :].rearrange("p a b -> p (a b)"))
                last.then_inc(var_done, 1)
                dve.wait_ge(ln_std, n + 1)
                dve.wait_ge(var_done, n + 1)
                step(dve.reciprocal(rstd[:, :], std[:, :]))
                dve.wait_ge(norm_in, 32 * (n + 1))
                for t in range(TB):
                    step(dve.tensor_scalar(xres[:, t, :], xres[:, t, :], mean_var[:, t, 0:1], rstd[:, t:t + 1],
                                           ALU.subtract, ALU.mult))
                    step(dve.tensor_tensor(xres[:, t, :], xres[:, t, :], norm_gb[:, 0, :], ALU.mult))
                    last = dve.tensor_tensor(xres[:, t, :], xres[:, t, :], norm_gb[:, 1, :], ALU.add)
                    last.then_inc(x_ready, 1)
                dve.wait_ge(x_ready, TB * (n + 1))
                dve.sem_inc(norm_used, 1)

            def residual(first):
                for t in range(TB):
                    for h in range(2):
                        s = xres[:, t, h * 512:(h + 1) * 512]
                        step(dve.scalar_tensor_tensor(s, s, ALPHA, bank[first + 2 * t + h][:, :], ALU.mult, ALU.add))

            def relative(l, m):
                h = 1 << (m - 1)
                r = run[0 if h <= 8 else 1 if h <= 32 else 2]
                v, o = [t[:, :].rearrange("p (b two h) -> p b two h", two=2, h=h) for t in (r, rel[m % 2])]
                edge = v[:, :, 0, h - 1:h].to_broadcast((P, 2 * SEQ // (2 * h), h))
                dve.tensor_tensor(o[:, :, 0, :], edge, v[:, :, 0, :], ALU.subtract)
                dve.tensor_tensor(o[:, :, 1, :], v[:, :, 1, :], edge, ALU.subtract).then_inc(rel_done, 1)

            def sides(l, m):
                h = 1 << (m - 1)
                e, o, k, q = [t.rearrange("p (b two h) -> p b two h", two=2, h=h)
                              for t in (rel[m % 2][:, :], side[m % 2], hk[:, :], hq[:, :])]
                dve.wait_ge(exp_done, 8 * l + m)
                if m > 2:
                    dve.wait_ge(level_done, HG_LEVELS * l + m - 1)
                dve.tensor_tensor(o[:, :, 0, :], e[:, :, 0, :], k[:, :, 0, :], ALU.mult)
                dve.tensor_tensor(o[:, :, 1, :], e[:, :, 1, :], q[:, :, 1, :], ALU.mult).then_inc(side_done, 1)
                dve.wait_ge(side_done, 8 * l + m)

            def take_level(l, m):
                dve.wait_ge(level_done, HG_LEVELS * l + m + 1)
                for h in range(2):
                    if m == HG_LEVELS - 1:
                        last = dve.tensor_copy(pairT[:, 2, 2 * h:2 * h + 2, :],
                                               bank[4 + h][:, 0:256].rearrange("p (c t) -> p c t", c=2))
                        continue
                    s = bank[4 + h][:, :].rearrange("p (b c t) -> p b c t", b=2, c=2)
                    o = pairT[:, 0:2, 2 * h:2 * h + 2, :]
                    if m == 0:
                        mask = ident[:, :].unsqueeze(1).unsqueeze(1).to_broadcast((P, 2, 2, P))
                        last = dve.tensor_tensor(o, s, mask, ALU.mult)
                    else:
                        mask = pair[:, m - 1, :].unsqueeze(1).unsqueeze(1).to_broadcast((P, 2, 2, P))
                        last = dve.copy_predicated(o, mask, s)
                last.then_inc(level_taken, 1)
                dve.wait_ge(level_taken, HG_LEVELS * l + m + 1)

            def masked_scores(l, r):
                dve.wait_ge(score_done, 3 * l + r + 1)
                for m in range(2):
                    if r < 2:
                        o = prob1[:, m, 2 * r:2 * r + 2, :]
                        mask = far_mask[:, :].unsqueeze(1).to_broadcast((P, 2, 2 * P))
                        s = bank[6 + m][:, :].rearrange("p (h k) -> p h k", h=2)
                    else:
                        o = prob0[:, m, :, :]
                        mask = far_mask[:, P:2 * P].unsqueeze(1).to_broadcast((P, DA_HEADS, P))
                        s = bank[6 + m][:, :].rearrange("p (h k) -> p h k", h=DA_HEADS)
                    last = dve.tensor_tensor(o, s, mask, ALU.add)
                last.then_inc(score_taken, 1)
                dve.wait_ge(score_taken, 3 * l + r + 1)

            def head_norm(first, heads, width, o, ms_sem, std_sem, l, sq):
                ms = head_ms[:, :]
                dve.reduce_sum(ms, sq.rearrange("p (g w) -> p g w", w=width), axis=AX).then_inc(ms_sem, 1)
                dve.wait_ge(std_sem, l + 1)
                step(dve.reciprocal(head_r[:, :], head_r[:, :]))
                for t in range(TB):
                    s = bank[first + t][:, 0:heads * width].rearrange("p (g w) -> p g w", w=width)
                    r = head_r[:, t * heads:(t + 1) * heads].unsqueeze(2).to_broadcast((P, heads, width))
                    last = dve.tensor_tensor(o[t].rearrange("p (g w) -> p g w", w=width), s, r, ALU.mult)
                return last

            dve.wait_ge(vecT_done, 1)
            step(dve.tensor_copy(vec[:, :], bank[7][:, 0:N_VEC]))
            v = vec[:, C_LAM:C_LAM + 2 * DEPTH]
            step(dve.tensor_scalar(soft[:, 1, :], v, -1.0, None, ALU.mult))
            step(dve.tensor_tensor(soft[:, 0, :], v, soft[:, 1, :], ALU.min))
            l0, l1 = vec[:, C_LB:C_LB + 2], vec[:, C_LB + 2:C_LB + 4]
            step(dve.tensor_tensor(lb_tmp[:, 4:6], l0, l1, ALU.max))
            step(dve.tensor_tensor(lb_tmp[:, 0:2], l0, lb_tmp[:, 4:6], ALU.subtract))
            step(dve.tensor_tensor(lb_tmp[:, 2:4], l1, lb_tmp[:, 4:6], ALU.subtract))
            dve.wait_ge(lam_in, 64)
            pairs = lam_rows[:, :, :].rearrange("p (m k) n -> p m k n", k=2)
            step(dve.tensor_tensor(lam_prod[:, :, :], pairs[:, :, 0, :], pairs[:, :, 1, :], ALU.mult))
            dve.reduce_sum(lam_sum[:, :], lam_prod[:, :, :].rearrange("p m (l d) -> p (m l) d", d=DA_DIM),
                           axis=AX).then_inc(vec_done, 1)
            for l in range(DEPTH):
                lam_init = 0.8 - 0.6 * math.exp(-0.3 * l)
                step(dve.tensor_scalar(da_g[:, 4 * l:4 * l + 4], vec[:, C_DAN + 4 * l:C_DAN + 4 * l + 4],
                                       1.0 - lam_init, None, ALU.mult))

            for l in range(DEPTH):
                m0 = MIX0[l]
                if l:
                    for c in range(3):
                        lo(m0 + c)
                xT_lo(2 * l)
                if l == 0:
                    dve.wait_ge(lam_done, 1)
                    step(dve.tensor_scalar(soft[:, 1, :], soft[:, 0, :], 2.0, None, ALU.add))
                    step(dve.reciprocal(soft[:, 1, :], soft[:, 1, :]))
                    step(dve.tensor_tensor(soft[:, 0, :], soft[:, 0, :], soft[:, 1, :], ALU.mult))
                    step(dve.tensor_tensor(soft[:, 1, :], soft[:, 0, :], soft[:, 0, :], ALU.mult))
                    step(dve.tensor_scalar(soft[:, 2, :], soft[:, 1, :], 1.0 / 19, 1.0 / 17, ALU.mult, ALU.add))
                    for k in range(15, 0, -2):
                        step(dve.tensor_tensor(soft[:, 2, :], soft[:, 2, :], soft[:, 1, :], ALU.mult))
                        step(dve.tensor_scalar(soft[:, 2, :], soft[:, 2, :], 1.0 / k, None, ALU.add))
                    step(dve.tensor_tensor(soft[:, 2, :], soft[:, 2, :], soft[:, 0, :], ALU.mult))
                    step(dve.tensor_scalar(soft[:, 3, :], v, 0.0, None, ALU.min))
                    step(dve.scalar_tensor_tensor(decay[:, :], soft[:, 2, :], -2.0, soft[:, 3, :],
                                                  ALU.mult, ALU.add))
                    step(dve.tensor_scalar(decay_neg[:, :], decay[:, :], -8.0, None, ALU.mult))
                    step(dve.tensor_scalar(decay[:, :], decay[:, :], 8.0, None, ALU.mult))
                    step(dve.tensor_tensor(lb_tmp[:, 4:6], lb_tmp[:, 0:2], lb_tmp[:, 2:4], ALU.add))
                    step(dve.reciprocal(lb_tmp[:, 4:6], lb_tmp[:, 4:6]))
                    step(dve.memset(lb[:, 0, :], 0.0))
                    step(dve.tensor_tensor(lb[:, 1, :], lb_tmp[:, 2:4], lb_tmp[:, 4:6], ALU.mult))
                    step(dve.tensor_scalar(lb_rest[:, :, :], lb[:, :, :], -1.0, 1.0, ALU.mult, ALU.add))
                    for k in range(DEPTH):
                        lam_init = 0.8 - 0.6 * math.exp(-0.3 * k)
                        last = dve.scalar_tensor_tensor(lam_one[:, k:k + 1], lam_sum[:, k:k + 1], lam_init,
                                                        lam_sum[:, DEPTH + k:DEPTH + k + 1], ALU.add, ALU.subtract)
                    last.then_inc(lam_done, 1)
                    for c in range(3):
                        lo(m0 + c)

                dve.wait_ge(taken, NCOL * l + 2)
                for c in range(2):
                    s = slice(c * SEQ, (c + 1) * SEQ)
                    step(dve.tensor_scalar(logf[:, s], logf[:, s], lb_rest[:, l, c:c + 1], lb[:, l, c:c + 1],
                                           ALU.mult, ALU.add))
                dve.tensor_scalar(logf[:, :], logf[:, :], 2.0 ** -63, None, ALU.max).then_inc(f_ready, 1)
                for c in range(2):
                    s = slice(c * SEQ, (c + 1) * SEQ)
                    dve.tensor_scalar(hk[:, s], hk[:, s], lb_rest[:, l, c:c + 1], None, ALU.mult)
                dve.tensor_tensor(hq[:, :], hq[:, :], sig[:, :], ALU.mult).then_inc(qk_ready, 1)
                lo(m0 + 3)
                dve.wait_ge(logf_done, l + 1)
                if l == 0:
                    dve.wait_ge(consts2, 1)
                for n in range(3):
                    step(dve.tensor_tensor_scan(run[n][:, :], keep[n][:, :], logf[:, :], 0.0, ALU.mult, ALU.add))
                dve.wait_ge(qk_ready, l + 1)
                relative(l, 1)
                relative(l, 2)
                dve.wait_ge(taken, NCOL * l + 3)
                for j in range(4):
                    for c in range(2):
                        w = vec[:, C_CW + 8 * l + 2 * j + c:C_CW + 8 * l + 2 * j + c + 1]
                        src = lx[:, c, j:j + SEQ]
                        if j == 0:
                            b = vec[:, C_CB + 2 * l + c:C_CB + 2 * l + c + 1]
                            step(dve.tensor_scalar(xc[:, c, :], src, w, b, ALU.mult, ALU.add))
                        else:
                            step(dve.scalar_tensor_tensor(xc[:, c, :], src, w, xc[:, c, :], ALU.mult, ALU.add))
                dve.sem_inc(xc_ready, 1)
                lo(m0 + 4)
                xcf = shared[:, 0, :]
                for m in range(1, HG_LEVELS):
                    sides(l, m)
                    if m + 2 < HG_LEVELS:
                        relative(l, m + 2)
                    take_level(l, m - 1)
                    lo(m0 + 4 + m)
                    if m == 1:
                        dve.wait_ge(taken, NCOL * l + 4)
                        c1 = 2.0 * math.sqrt(2.0 / math.pi)
                        step(dve.tensor_scalar(lgelu, lgelu, c1 * 0.044715, c1, ALU.mult, ALU.add))
                        dve.tensor_tensor(lgelu, lgelu, lgate, ALU.mult).then_inc(gelu_in, 1)
                    if m == 2 and l == 0:
                        dve.wait_ge(lamB_done, 1)
                        dve.tensor_copy(lam[:, :], bank[7][:, 0:DEPTH]).then_inc(lam_taken, 1)
                    if m == 4:
                        dve.wait_ge(tanh_done, l + 1)
                        dve.wait_ge(gelu_sig, l + 1)
                        step(dve.tensor_tensor(lgate, lgate, lgelu, ALU.mult))
                        step(dve.tensor_scalar(lgelu, lt, 1.0, None, ALU.add))
                        step(dve.reciprocal(lgelu, lgelu))
                        dve.scalar_tensor_tensor(lt, lt, 2.0, lgelu, ALU.mult,
                                                 ALU.mult).then_inc(root_in, 1)
                        step(dve.tensor_tensor(li[:, :], li[:, :], xcf, ALU.mult))
                    if m == 7:
                        dve.wait_ge(root_done, l + 1)
                        step(dve.tensor_tensor(li[:, :], li[:, :], lt, ALU.mult))
                        for c in range(2):
                            s = slice(c * SEQ, (c + 1) * SEQ)
                            step(dve.tensor_tensor_scan(lr[:, s], la[:, s], li[:, s], 0.0, ALU.mult, ALU.add))
                        dve.tensor_tensor(lr[:, :], lr[:, :], lgate, ALU.mult).then_inc(lru_out, 1)
                        dve.wait_ge(lru_hi, l + 1)
                        s = slice(2 * SEQ, 4 * SEQ)
                        dve.tensor_tensor(mixT_lo[:, s], lr[:, :], mixT_hi[:, s].bitcast(f32),
                                          ALU.subtract).then_inc(mix_lo, 1)
                        masked_scores(l, 0)
                    if m == 8:
                        masked_scores(l, 1)
                take_level(l, HG_LEVELS - 1)
                masked_scores(l, 2)
                step(dve.reduce_max(row_max[:, 0:8], prob1.rearrange("p m h k -> p (m h) k"), axis=AX))
                step(dve.reduce_max(row_max[:, 8:16], prob0.rearrange("p m h k -> p (m h) k"), axis=AX))
                dve.tensor_scalar(row_max[:, :], row_max[:, :], -DA_DIM ** -0.5, None, ALU.mult).then_inc(max_done, 1)
                lo(m0 + 13)
                lo(m0 + 14)
                dve.wait_ge(prob_done, l + 1)
                dve.wait_ge(lam_taken, 1)
                step(dve.reciprocal(row_inv[:, :], row_sum[:, :]))
                second = row_inv[:, :].rearrange("p (t m h) -> p t m h", t=2, m=2)[:, :, 1, :]
                step(dve.tensor_scalar(second, second, lam[:, l:l + 1], None, ALU.mult))
                for prob, at in ((prob1, 0), (prob0, 8)):
                    width = prob.shape[3]
                    pv = prob.rearrange("p m h k -> p (m h) k")
                    step(dve.tensor_tensor(pv, pv, row_inv[:, at:at + 8].unsqueeze(2).to_broadcast((P, 8, width)),
                                           ALU.mult))
                for n, prob in enumerate((prob1, prob0)):
                    last = dve.tensor_tensor(prob[:, 0, :, :], prob[:, 0, :, :], prob[:, 1, :, :], ALU.subtract)
                last.then_inc(w_done, 1)
                lo(m0 + 15)
                step(dve.tensor_tensor(hgate, hgate, hgate_sig, ALU.mult))
                dve.wait_ge(hsq_done, l + 1)
                o = [hout[:, t * 256:(t + 1) * 256] for t in range(TB)]
                step(head_norm(4, 4, 64, o, hms_done, hstd_done, l, hsq[:, :]))
                dve.tensor_tensor(hout[:, :], hout[:, :], hgate.rearrange("p t n -> p (t n)"),
                                  ALU.mult).then_inc(hout_done, 1)
                dve.wait_ge(hT_hi_ready, l + 1)
                for c in range(2):
                    s = slice(c * SEQ, (c + 1) * SEQ)
                    g = vec[:, C_HGN + 2 * l + c:C_HGN + 2 * l + c + 1]
                    last = dve.scalar_tensor_tensor(mixT_lo[:, s], bank[4][:, s], g, mixT_hi[:, s].bitcast(f32),
                                                    ALU.mult, ALU.subtract)
                last.then_inc(mix_lo, 1)
                dve.wait_ge(dsq_done, l + 1)
                o = [dout[:, t, :] for t in range(TB)]
                head_norm(4, 4, 128, o, dms_done, dstd_done, l,
                          dsq.rearrange("p t n -> p (t n)")).then_inc(dout_done, 1)
                dve.wait_ge(dT_hi_ready, l + 1)
                for h in range(DA_HEADS):
                    s = slice((4 + h) * SEQ, (5 + h) * SEQ)
                    last = dve.scalar_tensor_tensor(mixT_lo[:, s], bank[6 + h // 2][:, (h % 2) * SEQ:(h % 2 + 1) * SEQ],
                                                    da_g[:, 4 * l + h:4 * l + h + 1], mixT_hi[:, s].bitcast(f32),
                                                    ALU.mult, ALU.subtract)
                last.then_inc(mix_lo, 1)
                dve.wait_ge(used, m0 + N_MIX)
                residual(0)
                norm(2 * l)
                xT_lo(2 * l + 1)
                if l:
                    continue
                with dve.Fori(0, FB) as fb:
                    def hidden(h):
                        dve.wait_ge(d_silu, 2 * fb + h + 1)
                        dve.tensor_tensor(hid2[h][:, :], hid_sig[:, :], bank[2 * h + 1][:, :], ALU.mult).then_inc(d_h, 1)
                        dve.wait_ge(d_hi, 2 * fb + h + 1)
                        s = slice(h * 512, (h + 1) * 512)
                        dve.tensor_tensor(mixT_lo[:, s], hid2[h][:, :], mixT_hi[:, s].bitcast(f32),
                                          ALU.subtract).then_inc(d_lo, 1)

                    for k in range(5):
                        lo(DENSE0 + k, fb)
                    hidden(0)
                    lo(DENSE0 + 5, fb)
                    hidden(1)
                dve.wait_ge(used, DENSE0 + N_FFN)
                residual(4)
                norm(1)

            dve.wait_ge(xs_hi_done, 1)
            dve.tensor_tensor(rw_lo[:, :, :], rw[:, :, :], rw_hi[:, :, :].bitcast(f32),
                              ALU.subtract).then_inc(rw_split, 1)
            dve.wait_ge(logit_done, 1)
            step(dve.tensor_copy(logit[:, :, :], bank[4][:, 0:TB * E].rearrange("p (t e) -> p t e", t=TB)))
            for t in range(TB):
                step(dve.max(best[:, t, :], logit[:, t, :]))
            dve.tensor_tensor(gates[:, 3, :], best[:, :, 1], best[:, :, 0], ALU.subtract).then_inc(gap_done, 1)
            for t in range(TB):
                step(dve.max_index(best_at[:, t, :], best[:, t, :], logit[:, t, :]))
            step(dve.tensor_copy(best_f[:, :, :], best_at[:, :, :]))
            for k in range(TOP_K):
                for t in range(TB):
                    step(dve.tensor_scalar(hot[:, k, t, :], iota_row[:, 0:E], best_f[:, t, k:k + 1], None,
                                           ALU.is_equal))
            dve.tensor_tensor(routed[:, :, :], hot[:, 0, :, :], hot[:, 1, :, :], ALU.add).then_inc(routed_done, 1)
            dve.wait_ge(routed_done, 1)
            dve.wait_ge(gap_exp, 1)
            step(dve.tensor_scalar(gates[:, 1, :], gates[:, 0, :], 1.0, None, ALU.add))
            step(dve.reciprocal(gates[:, 1, :], gates[:, 1, :]))
            step(dve.tensor_tensor(gates[:, 2, :], gates[:, 0, :], gates[:, 1, :], ALU.mult))
            for t in range(TB):
                step(dve.tensor_scalar(combine[:, t, 0:E], hot[:, 0, t, :], gates[:, 1, t:t + 1], None, ALU.mult))
                step(dve.scalar_tensor_tensor(combine[:, t, 0:E], hot[:, 1, t, :], gates[:, 2, t:t + 1],
                                              combine[:, t, 0:E], ALU.mult, ALU.add))
            dve.wait_ge(rank_done, 1)
            rank = bank[5][:, 0:TB * E].rearrange("p (t e) -> p t e", t=TB)
            step(dve.scalar_tensor_tensor(place[:, :, 0:E], rank, 1.0, routed[:, :, :], ALU.add, ALU.mult))
            step(dve.tensor_scalar(place[:, :, 0:E], place[:, :, 0:E], -1.0, None, ALU.add))
            step(dve.tensor_scalar(over[:, 0, :], bank[5][:, 2 * E:3 * E], float(P), None, ALU.is_gt))
            step(dve.tensor_tensor_scan(over[:, 1, :], ones[:, 0:E], over[:, 0, :], 0.0, ALU.mult, ALU.add))
            step(dve.tensor_scalar(over[:, 2, :], over[:, 1, :], 0.0, None, ALU.mult))
            step(dve.tensor_copy(item_f[:, 1:1 + E], iota_row[:, 0:E]))
            for k in range(ITEMS - E):
                step(dve.scalar_tensor_tensor(over_sel[:, :], over[:, 1, :], float(k + 1), over[:, 0, :],
                                              ALU.is_equal, ALU.mult))
                sel = over_sel[:, :].unsqueeze(1).to_broadcast((P, TB, E))
                step(dve.tensor_tensor(over_tmp[:, :, :], combine[:, :, 0:E], sel, ALU.mult))
                step(dve.reduce_sum(combine[:, :, E + k:E + k + 1], over_tmp[:, :, :], axis=AX))
                step(dve.scalar_tensor_tensor(over_tmp[:, :, :], place[:, :, 0:E], 1.0 - P, sel, ALU.add, ALU.mult))
                step(dve.reduce_sum(place[:, :, E + k:E + k + 1], over_tmp[:, :, :], axis=AX))
                step(dve.tensor_scalar(place[:, :, E + k:E + k + 1], place[:, :, E + k:E + k + 1], -1.0, None, ALU.add))
                step(dve.tensor_tensor(over_tmp[:, 0, :], iota_row[:, 0:E], over_sel[:, :], ALU.mult))
                step(dve.reduce_sum(item_f[:, 1 + E + k:2 + E + k], over_tmp[:, 0, :], axis=AX))
            step(dve.tensor_scalar(item_f[:, 0:1], over[:, 1, E - 1:E], float(E - 1), None, ALU.add))
            dve.tensor_copy(item_i[:, :], item_f[:, :]).then_inc(items_done, 1)
            dve.wait_ge(xs_hi_done, 2)
            dve.tensor_tensor(xs_lo[:, :, :], xres[:, :, :], xs_hi[:, :, :].bitcast(f32),
                              ALU.subtract).then_inc(xs_done, 1)
            dve.wait_ge(xs_done, 1)
            dve.tensor_scalar(xres[:, :, :], xres[:, :, :], ALPHA, None, ALU.mult).then_inc(m_acc, 4)
            dve.wait_ge(items_done, 1)
            last_item = dve.value_load(item_i[0:1, 0:1], min_val=E - 1, max_val=ITEMS - 1)

            def hidden(n):
                dve.wait_ge(m_silu, n)
                dve.tensor_tensor(hid[:, :], hid_sig[:, :], bank[1][:, :], ALU.mult).then_inc(m_h, 1)

            def turned(n):
                dve.wait_ge(m_T_hi, n)
                dve.tensor_tensor(mixT_lo[:, 0:512], bank[2][:, :], mixT_hi[:, 0:512].bitcast(f32),
                                  ALU.subtract).then_inc(m_T_lo, 1)

            def choose(i):
                for t in range(TB):
                    dve.tensor_scalar(pick[:, t, :], iota_row[:, :], place[:, t, bass.ds(i, 1)], None, ALU.is_equal)
                dve.tensor_copy(gate_tok[:, :], combine[:, :, bass.ds(i, 1)].rearrange(
                    "p t a -> p (t a)")).then_inc(m_pick, 1)

            def gathered(n):
                dve.wait_ge(m_xg_hi, n)
                for k in range(2):
                    s = slice(k * 512, (k + 1) * 512)
                    last = dve.tensor_tensor(actT_lo[:, s], bank[6 + k][:, :], actT_hi[:, s].bitcast(f32), ALU.subtract)
                last.then_inc(m_xg_lo, 1)

            def output(n):
                dve.wait_ge(m_y_hi, n)
                for k in range(2):
                    s = slice(k * 512, (k + 1) * 512)
                    last = dve.scalar_tensor_tensor(y_lo[:, s], bank[4 + k][:, :], gate_slot[:, :],
                                                    y_hi[:, s].bitcast(f32), ALU.mult, ALU.subtract)
                last.then_inc(m_y_lo, 1)

            def accumulate(i):
                for t in range(TB):
                    for h in range(2):
                        q = 2 * t + h
                        dve.wait_ge(m_back, 4 * i + q + 1)
                        dve.wait_ge(m_acc, 4 * i + q + 1)
                        s = xres[:, t, h * 512:(h + 1) * 512]
                        dve.tensor_tensor(s, s, bank[4 + q][:, :], ALU.add).then_inc(m_acc, 1)

            def start_item(i):
                lo(ITEM0 + 2, FB * i)
                turned(FB * i + 1)
                lo(ITEM0 + 3, FB * i)
                lo(ITEM0 + 4, FB * i)
                hidden(FB * i + 2)

            def middle(c, n, turns):
                for k in range(1, 5):
                    lo(c + k, turns)
                turned(n)
                lo(c + 5, turns)
                lo(c + 6, turns)
                hidden(n + 1)

            choose(0)
            for k in range(3):
                lo(MOE0 + k)
            gathered(1)
            for k in range(3, 7):
                lo(MOE0 + k)
            hidden(1)
            lo(MOE0 + 7)
            with dve.Fori(0, last_item) as i:
                start_item(i)
                choose(i + 1)
                with dve.Fori(2, FB - 1) as fb:
                    middle(ITEM0 + 4, FB * i + fb, FB * i + fb - 2)
                middle(SEAM0 - 6, FB * i + FB - 1, FB * i)
                gathered(i + 2)
                for k in range(1, 5):
                    lo(SEAM0 + k, FB * i)
                turned(FB * i + FB)
                lo(SEAM0 + 5, FB * i)
                lo(SEAM0 + 6, FB * i)
                hidden(FB * i + FB + 1)
                lo(SEAM0 + 7, FB * i)
                output(i + 1)
                lo(SEAM0 + 8, FB * i)
                lo(SEAM0 + 9, FB * i)
                accumulate(i)
            i = last_item
            start_item(i)
            with dve.Fori(2, FB) as fb:
                middle(ITEM0 + 4, FB * i + fb, FB * i + fb - 2)
            lo(SEAM0 + 1, FB * i)
            turned(FB * i + FB)
            output(i + 1)
            accumulate(i)
            dve.wait_ge(m_acc, 4 * last_item + 8)
            norm(3)


_INS = ["x", "w_in", "w_out", "hg_lb_logits", "hg_norm_g", "lru_conv_w", "lru_conv_b", "lru_wa", "lru_ba",
        "lru_wx", "lru_bx", "lru_lambda", "da_lq1", "da_lk1", "da_lq2", "da_lk2", "da_norm_g",
        "ln1_g", "ln1_b", "ln2_g", "ln2_b", "ffn_wg", "ffn_wu", "ffn_wd", "router_w", "moe_wg", "moe_wu", "moe_wd"]


def kernel(**inputs):
    import numpy as np
    import concourse.bacc as bacc
    from concourse.bass_utils import run_bass_kernel_spmd

    nc = bacc.Bacc("TRN2", target_bir_lowering=False, num_devices=1)
    arrays, args = {}, []
    for name in _INS:
        a = np.ascontiguousarray(inputs[name])
        arrays[f"in_{name}"] = a
        args.append(nc.dram_tensor(f"in_{name}", a.shape, mybir.dt.from_np(a.dtype), kind="ExternalInput").ap())
    args.append(nc.dram_tensor("out_x", inputs["x"].shape, mybir.dt.float32, kind="ExternalOutput").ap())
    decoder_trunk(nc, *args)
    r = run_bass_kernel_spmd(nc, [arrays], core_ids=[0])
    return r.results[0]["out_x"]
```

```python
import math
from contextlib import ExitStack

import concourse.bass as bass
from concourse import mybir

P = 128
SLOT_RAW = 6
SLOT_SPLIT = 3
PIECE = 2048
FAR = -3.0e38


def decoder_trunk(nc, x, w_in, w_out, hg_lb_logits, hg_norm_g, lru_conv_w, lru_conv_b, lru_wa, lru_ba,
                  lru_wx, lru_bx, lru_lambda, da_lq1, da_lk1, da_lq2, da_lk2, da_norm_g,
                  ln1_g, ln1_b, ln2_g, ln2_b, ffn_wg, ffn_wu, ffn_wd, router_w, moe_wg, moe_wu, moe_wd, out):
    f32, f32r, bf16 = mybir.dt.float32, mybir.dt.float32r, mybir.dt.bfloat16
    i8, i32, u32 = mybir.dt.int8, mybir.dt.int32, mybir.dt.uint32
    ALU, ACT, AX = mybir.AluOpType, mybir.ActivationFunctionType, mybir.AxisListType.X

    _, SEQ, D = x.shape
    DEPTH = w_in.shape[0]
    TB = SEQ // P
    DC = D // P
    NCOL = w_in.shape[2] // 256
    F = ffn_wg.shape[2]
    FB = F // 512
    E = moe_wg.shape[1]
    TOP_K = 2
    ITEMS = E + (TOP_K * SEQ - 1) // (P + 1)
    ALPHA = (2.0 * DEPTH) ** 0.25
    EPS = 1e-5
    DA_HEADS, DA_DIM, HG_DIM = 4, 64, 64
    HG_LEVELS = 9
    assert (SEQ, D, DEPTH, NCOL, FB * 512, E) == (256, 1024, 2, 12, F, 8)

    HQ, HF, HI, HG, LX, LG, DQ, DK, DV = 0, 1, 2, 3, 4, 5, 6, 8, 10
    ORDER = [HQ, HF, LX, LG, HI, DQ, DQ + 1, DK, DK + 1, HG, DV, DV + 1]
    TOKEN_MAJOR = (HI, HG, DV, DV + 1)
    OUT_ORDER = [1, 0, 2, 3]
    N_MIX = NCOL + len(OUT_ORDER)
    N_FFN = 6 * FB
    MIX0 = [l * (N_MIX + N_FFN) for l in range(DEPTH)]
    DENSE0 = MIX0[0] + N_MIX
    MOE0 = MIX0[1] + N_MIX
    ITEM0 = MOE0 + 6
    SEAM0 = ITEM0 + 4 + 6 * (FB - 2)
    assert N_FFN % SLOT_RAW == 0 and SLOT_RAW % SLOT_SPLIT == 0

    C_LB, C_HGN, C_CW, C_CB, C_BA, C_BX, C_LAM, C_DAN, N_VEC = 0, 4, 8, 24, 28, 32, 36, 40, 48

    ctx = ExitStack()
    with ctx:
        def sb(name, shape, dt=f32, where=ctx):
            return where.enter_context(nc.sbuf_tensor(name, shape, dt))

        def sem(name):
            return ctx.enter_context(nc.semaphore(name))

        raw = [sb(f"raw{k}", [P, PIECE]) for k in range(SLOT_RAW)]
        w_hi = [sb(f"w_hi{k}", [P, PIECE], f32r) for k in range(SLOT_SPLIT)]
        w_lo = [sb(f"w_lo{k}", [P, PIECE], f32r) for k in range(SLOT_SPLIT)]
        xres = sb("xres", [P, TB, D])
        actT_hi = sb("actT_hi", [P, DC * SEQ], f32r)
        actT_lo = sb("actT_lo", [P, DC * SEQ], f32r)
        mixT_hi = sb("mixT_hi", [P, DC * SEQ], f32r)
        mixT_lo = sb("mixT_lo", [P, DC * SEQ], f32r)
        norm_gb = sb("norm_gb", [P, 2, D])
        ident = sb("ident", [P, P])
        iota_row = sb("iota_row", [P, P])
        before = sb("before", [P, P], bf16)
        all_ones = sb("all_ones", [P, P], bf16)
        ones = sb("ones", [P, P])
        zeros = sb("zeros", [P, P], bf16)
        far_mask = sb("far_mask", [P, 2 * P])
        pair = sb("pair", [P, 7, P], i8)
        keep = [sb(f"keep{n}", [P, 2 * SEQ], bf16) for n in range(3)]
        eps = sb("eps", [P, 1])
        vec_rows = sb("vec_rows", [N_VEC, P])
        vec = sb("vec", [P, N_VEC])
        gate_a = sb("gate_a", [P, DEPTH, 2, P])
        gate_x = sb("gate_x", [P, DEPTH, 2, P])
        lam_sum = sb("lam_sum", [1, 2 * DEPTH])
        lam_one = sb("lam_one", [1, DEPTH])
        lam_neg = sb("lam_neg", [P, DEPTH])
        lb = sb("lb", [P, DEPTH, 2])
        lb_rest = sb("lb_rest", [P, DEPTH, 2])
        lb_tmp = sb("lb_tmp", [P, 8])
        decay = sb("decay", [P, 2 * DEPTH])
        decay_neg = sb("decay_neg", [P, 2 * DEPTH])
        soft = sb("soft", [P, 4, 2 * DEPTH])
        da_g = sb("da_g", [P, DEPTH * 4])
        rw = sb("rw", [P, DC, E])
        rw_hi = sb("rw_hi", [P, DC, E], f32r)
        rw_lo = sb("rw_lo", [P, DC, E], f32r)
        stats = sb("stats", [P, TB, 2, 6])
        mean_var = sb("mean_var", [P, TB, 2])
        std = sb("std", [P, TB])
        rstd = sb("rstd", [P, TB])
        with ExitStack() as mixer_only:
            def mb(name, shape, dt=f32):
                return sb(name, shape, dt, mixer_only)

            sig = mb("sig", [P, 2 * SEQ])
            hq = mb("hq", [P, 2 * SEQ])
            hk = mb("hk", [P, 2 * SEQ])
            logf = mb("logf", [P, 2 * SEQ])
            run = [mb(f"run{n}", [P, 2 * SEQ]) for n in range(3)]
            rel = [mb(f"rel{n}", [P, 2 * SEQ]) for n in range(2)]
            sides_t = mb("sides_t", [P, 2, 2 * SEQ])
            side = [sides_t[:, n, :] for n in range(2)]
            pairT = mb("pairT", [P, 3, 4, P])
            hv = mb("hv", [P, TB, 256])
            lx = mb("lx", [P, 2, 3 + SEQ])
            shared = mb("shared", [P, 4, 2 * SEQ])
            dq = mb("dq", [P, DA_HEADS, SEQ])
            dk = mb("dk", [P, DA_HEADS, SEQ])
            row_max = mb("row_max", [P, 16])
            row_sum = mb("row_sum", [P, 16])
            row_inv = mb("row_inv", [P, 16])
            ratio = mb("ratio", [P, 8])
            head_ms = mb("head_ms", [P, 8])
            head_r = mb("head_r", [P, 8])
            lam_rows = hv[0:1, :, :].rearrange("p t n -> p (t n)").rearrange("p (k n) -> p k n", k=4)
            lam_prod = dq[0:1, 0, :].rearrange("p (m n) -> p m n", m=2)
            pair_f = shared[:, 0:2, :].rearrange("p a n -> p (a n)")[:, 0:7 * P].rearrange("p (m t) -> p m t", m=7)
            xc = shared[:, 0, :].rearrange("p (c t) -> p c t", c=2)
            lgate, lgelu, lt = shared[:, 1, :], shared[:, 2, :], shared[:, 3, :]
            lr, li, la = run[0], lx[:, :, 3:3 + SEQ], logf
            lt2 = lt.rearrange("p (c t) -> p c t", c=2)
            hgate = logf[:, :].rearrange("p (t n) -> p t n", t=TB)
            hgate_sig = sig[:, :].rearrange("p (t n) -> p t n", t=TB)
            dv = [run[n][:, :].rearrange("p (t n) -> p t n", t=TB) for n in (2, 1)]
            prob1 = shared[:, :, :].rearrange("p a n -> p (a n)").rearrange(
                "p (m h k) -> p m h k", m=2, h=DA_HEADS)
            prob0 = sides_t[:, :, :].rearrange("p m (h k) -> p m h k", h=DA_HEADS)
            hsq, hout = rel
            dsq = shared[:, 0:2, :]
            dout = shared[:, 2:4, :]
        hid_sig = sb("hid_sig", [P, 512])
        hid2 = [sb(f"hid{n}", [P, 512]) for n in range(2)]
        hid = hid2[0]
        xs_hi = sb("xs_hi", [P, TB, D], f32r)
        xs_lo = sb("xs_lo", [P, TB, D], f32r)
        xg_tok = sb("xg_tok", [P, D])
        y_hi = sb("y_hi", [P, D], f32r)
        y_lo = sb("y_lo", [P, D], f32r)
        logitT = sb("logitT", [E, SEQ])
        logit = sb("logit", [P, TB, E])
        best = sb("best", [P, TB, 8])
        best_at = sb("best_at", [P, TB, 8], u32)
        best_f = sb("best_f", [P, TB, 8])
        hot = sb("hot", [P, TOP_K, TB, E])
        gates = sb("gates", [P, 4, TB])
        routed = sb("routed", [P, TB, E], bf16)
        combine = sb("combine", [P, TB, ITEMS])
        place = sb("place", [P, TB, ITEMS])
        over = sb("over", [P, 3, E])
        over_sel = sb("over_sel", [P, E])
        over_tmp = sb("over_tmp", [P, TB, E])
        item_f = sb("item_f", [P, 1 + ITEMS])
        item_i = sb("item_i", [P, 1 + ITEMS], i32)
        pick = sb("pick", [P, TB, P], f32r)
        pickT = sb("pickT", [P, SEQ], f32r)
        gate_tok = sb("gate_tok", [P, TB])
        gate_slot = sb("gate_slot", [P, 1])

        bank = [ctx.enter_context(nc.psum_tensor(f"bank{k}", [P, 512], f32)) for k in range(8)]

        full = [sem(f"full{k}") for k in range(SLOT_RAW)]
        hi_ready, lo_ready, used = sem("hi_ready"), sem("lo_ready"), sem("used")
        x_in = [sem(f"x_in{t}") for t in range(TB)]
        vec_in, gate_in, lam_in, norm_in, rw_in, stored = [
            sem(n) for n in "vec_in gate_in lam_in norm_in rw_in stored".split()]
        consts, consts2, lam_taken, vecT_done, vec_done, lam_exp, lam_done, lamB_done, lx_blank = [
            sem(n) for n in "consts consts2 lam_taken vecT_done vec_done lam_exp lam_done lamB_done lx_blank".split()]
        early_done, x_ready, xT_done, xT_hi_ready, xT_lo_ready, norm_used = [
            sem(n) for n in "early_done x_ready xT_done xT_hi_ready xT_lo_ready norm_used".split()]
        taken, f_ready, k_sig, logf_done, qk_ready, rel_done, exp_done, side_done, level_done, level_taken = [
            sem(n) for n in ("taken f_ready k_sig logf_done qk_ready rel_done exp_done side_done "
                             "level_done level_taken").split()]
        xc_ready, gates_done, act_lru, tanh_done, root_in, root_done, gelu_in, gelu_sig, lru_out, lru_hi = [
            sem(n) for n in ("xc_ready gates_done act_lru tanh_done root_in root_done gelu_in gelu_sig "
                             "lru_out lru_hi").split()]
        score_done, score_taken, max_done, prob_done, ratio_done, w_done, wT_done, wT_taken = [
            sem(n) for n in "score_done score_taken max_done prob_done ratio_done w_done wT_done wT_taken".split()]
        hpv_done, hsq_done, hms_done, hstd_done, hgate_done, hout_done, hT_done, hT_hi_ready, mix_lo = [
            sem(n) for n in "hpv_done hsq_done hms_done hstd_done hgate_done hout_done hT_done hT_hi_ready mix_lo".split()]
        dpv_done, dsq_done, dms_done, dstd_done, dout_done, dT_done, dT_hi_ready = [
            sem(n) for n in "dpv_done dsq_done dms_done dstd_done dout_done dT_done dT_hi_ready".split()]
        soft_ready, decay_done, var_done, ln_std = [sem(n) for n in "soft_ready decay_done var_done ln_std".split()]
        d_silu, d_h, d_hi, d_lo, dense_early = [sem(n) for n in "d_silu d_h d_hi d_lo dense_early".split()]
        rw_hi_done, rw_split, logitT_done, logitT_taken, logit_done, gap_done, gap_exp, routed_done, rank_done, items_done, xs_hi_done, xs_done = [
            sem(n) for n in ("rw_hi_done rw_split logitT_done logitT_taken logit_done gap_done gap_exp routed_done rank_done items_done "
                             "xs_hi_done xs_done").split()]
        m_pick, m_pickT, m_slot, m_gath, m_xg_tok, m_xgT, m_xg_hi, m_xg_lo, m_silu, m_h, m_T, m_T_hi, m_T_lo, m_y_hi, m_y_lo, m_back, m_acc = [
            sem(n) for n in ("m_pick m_pickT m_slot m_gath m_xg_tok m_xgT m_xg_hi m_xg_lo m_silu m_h m_T m_T_hi m_T_lo m_y_hi m_y_lo "
                             "m_back m_acc").split()]
        dve_step, act_step, pool_step = sem("dve_step"), sem("act_step"), sem("pool_step")

        def ring(c, turns=0):
            return c % SLOT_RAW, c % SLOT_SPLIT, 16 * (c // SLOT_RAW + 1) + 16 * turns, c + SLOT_RAW * turns

        actT = [t[:, :].rearrange("p (c t) -> p c t", c=DC) for t in (actT_hi, actT_lo)]
        xg = [t[:, 0:DC * P].rearrange("p (c t) -> p c t", c=DC) for t in (actT_hi, actT_lo)]
        mixT = [t[:, :].rearrange("p (c t) -> p c t", c=DC) for t in (mixT_hi, mixT_lo)]

        def xT_part(k, q):
            return actT[k][:, 4 * (q % 2):4 * (q % 2) + 4, q // 2 * P:(q // 2 + 1) * P]

        def round_heads(r):
            return (1, (2 * r, 2 * r + 1)) if r < 2 else (0, tuple(range(DA_HEADS)))

        in_v = w_in.rearrange("l (c p) (b n) -> l b p c n", p=P, n=256)
        out_v = w_out.rearrange("l (q c p) n -> l q p c n", p=P, c=2)
        up_v = [w[0].rearrange("(c p) (b n) -> b p c n", p=P, n=256) for w in (ffn_wg, ffn_wu)]
        down_v = ffn_wd[0].rearrange("(q c p) n -> q p c n", p=P, c=2)
        moe_up_v = [w[0].rearrange("e (c p) (b n) -> e b p c n", p=P, n=512) for w in (moe_wg, moe_wu)]
        moe_down_v = moe_wd[0].rearrange("e (q c p) n -> (e q) p c n", p=P, c=2)

        block = ctx.enter_context(nc.Block())

        @block.sync
        def _(sp):
            def load(c, src, turns=0, reuse=True):
                slot, _, _, n = ring(c, turns)
                if reuse:
                    sp.wait_ge(lo_ready, n - SLOT_RAW + 1)
                dst = raw[slot][:, :].rearrange("p (c n) -> p c n", c=src.shape[1])
                sp.dma_start(dst, src).then_inc(full[slot], 16)

            def load_vectors():
                rows = [(hg_lb_logits, C_LB, 4), (hg_norm_g, C_HGN, 4), (lru_conv_b, C_CB, 4), (lru_ba, C_BA, 4),
                        (lru_bx, C_BX, 4), (lru_lambda, C_LAM, 4), (da_norm_g, C_DAN, 8)]
                for v, at, n in rows:
                    sp.dma_start(vec_rows[at:at + n, :], v.rearrange("l (c p) -> (l c) p", p=P)).then_inc(vec_in, 16)
                sp.dma_start(vec_rows[C_CW:C_CW + 16, :],
                             lru_conv_w.rearrange("l j (c p) -> (l j c) p", p=P)).then_inc(vec_in, 16)
                for k, v in enumerate((da_lq1, da_lk1, da_lq2, da_lk2)):
                    sp.dma_start(lam_rows[:, k, :], v.rearrange("(a l) d -> a (l d)", a=1)).then_inc(lam_in, 16)

            def load_router():
                sp.dma_start(rw[:, :, :], router_w[0].rearrange("(c p) e -> p c e", p=P)).then_inc(rw_in, 16)

            def load_mixer(l):
                for j in range(NCOL):
                    load(MIX0[l] + j, in_v[l, ORDER[j]], reuse=MIX0[l] + j >= SLOT_RAW)
                    if l == 0 and j == 0:
                        for t in range(TB):
                            sp.dma_start(xres[:, t, :], x[0, t * P:(t + 1) * P, :]).then_inc(x_in[t], 16)
                    if l == 0 and j == 2:
                        load_vectors()
                for j, q in enumerate(OUT_ORDER):
                    load(MIX0[l] + NCOL + j, out_v[l, q])

            def load_up(c, m, e, b, turns):
                for h in range(2):
                    load(c + h, moe_up_v[m][e, b, :, 4 * h:4 * h + 4, :], turns)

            def load_down(c, e, b, turns):
                for h in range(2):
                    load(c + h, moe_down_v[2 * FB * e + 2 * b + h], turns)

            def load_blocks(e, i, last):
                load_up(ITEM0, 1, e, 1, FB * i)
                load_down(ITEM0 + 2, e, 0, FB * i)
                with sp.Fori(2, FB) as fb:
                    turns = FB * i + fb - 2
                    load_up(ITEM0 + 4, 0, e, fb, turns)
                    load_up(ITEM0 + 6, 1, e, fb, turns)
                    load_down(ITEM0 + 8, e, fb - 1, turns)
                if last:
                    load_down(SEAM0, e, FB - 1, FB * i)

            def load_seam(e, e_next, i):
                load_up(SEAM0, 0, e_next, 0, FB * i)
                load_up(SEAM0 + 2, 1, e_next, 0, FB * i)
                load_down(SEAM0 + 4, e, FB - 1, FB * i)
                load_up(SEAM0 + 6, 0, e_next, 1, FB * i)

            load_mixer(0)
            with sp.Fori(0, FB) as fb:
                for h in range(2):
                    for m in range(2):
                        load(DENSE0 + 2 * h + m, up_v[m][2 * fb + h], fb)
                for h in range(2):
                    load(DENSE0 + 4 + h, down_v[2 * fb + h], fb)
            load_router()
            load_mixer(1)
            load_up(MOE0, 0, 0, 0, 0)
            load_up(MOE0 + 2, 1, 0, 0, 0)
            load_up(MOE0 + 4, 0, 0, 1, 0)
            with sp.Fori(0, E - 1) as i:
                load_blocks(i, i, False)
                load_seam(i, i + 1, i)
            sp.wait_ge(items_done, 1)
            last_item = sp.value_load(item_i[0:1, 0:1], min_val=E - 1, max_val=ITEMS - 1)
            with sp.If(last_item > E - 1):
                with sp.Fori(E - 1, last_item) as i:
                    e = sp.value_load(item_i[0:1, bass.ds(i + 1, 1)], min_val=0, max_val=E - 1)
                    load_blocks(e, i, False)
                    e_next = sp.value_load(item_i[0:1, bass.ds(i + 2, 1)], min_val=0, max_val=E - 1)
                    load_seam(e, e_next, i)
            with sp.Fori(last_item, last_item + 1) as i:
                e = sp.value_load(item_i[0:1, bass.ds(i + 1, 1)], min_val=0, max_val=E - 1)
                load_blocks(e, i, True)
            for q in range(2 * TB):
                sp.wait_ge(x_ready, 2 * TB * (2 * DEPTH - 1) + q + 1)
                cols = slice(q % 2 * 512, (q % 2 + 1) * 512)
                sp.dma_start(out[0, q // 2 * P:(q // 2 + 1) * P, cols], xres[:, q // 2, cols]).then_inc(stored, 16)
            sp.wait_ge(stored, 16 * 2 * TB)

        @block.gpsimd
        def _(pool):
            count = [0]

            def step(ins):
                count[0] += 1
                ins.then_inc(pool_step, 1)
                pool.wait_ge(pool_step, count[0])

            def select(t, pattern, op, base, mult, fill=0.0):
                step(pool.affine_select(out=t, in_=t, pattern=pattern, compare_op=op, fill=fill,
                                        base=base, channel_multiplier=mult))

            step(pool.memset(ident[:, :], 0.0))
            pool.affine_select(out=ident[:, :], in_=ident[:, :], pattern=[[-1, P]], compare_op=ALU.not_equal,
                               fill=1.0, base=0, channel_multiplier=1).then_inc(consts, 1)
            for g, t in ((lru_wa, gate_a), (lru_wx, gate_x)):
                step(pool.memset(t[:, :, :, :], 0.0))
                view = g.rearrange("l (c h) i j -> h i (l c) j", h=2)
                for h in range(2):
                    rows = slice(64 * h, 64 * h + 64)
                    dst = t[rows, :, :, 64 * h:64 * h + 64].rearrange("p l c j -> p (l c) j")
                    pool.dma_start(dst, view[h]).then_inc(gate_in, 16)
            pool.memset(lx[:, :, 0:3], 0.0).then_inc(lx_blank, 1)
            for n in range(2 * DEPTH):
                g, b = ((ln1_g, ln1_b), (ln2_g, ln2_b))[n % 2]
                if n:
                    pool.wait_ge(norm_used, n)
                pool.dma_start(norm_gb[:, 0, :], g[n // 2:n // 2 + 1, :].to_broadcast((P, D))).then_inc(norm_in, 16)
                pool.dma_start(norm_gb[:, 1, :], b[n // 2:n // 2 + 1, :].to_broadcast((P, D))).then_inc(norm_in, 16)
                if n:
                    continue
                step(pool.memset(eps[:, :], EPS))
                step(pool.memset(ones[:, :], 1.0))
                step(pool.memset(all_ones[:, :], 1.0))
                step(pool.memset(zeros[:, :], 0.0))
                for m, width in enumerate((16, 64, 256)):
                    step(pool.memset(keep[m][:, :], 1.0))
                    step(pool.memset(keep[m][:, :].rearrange("p (b w) -> p b w", w=width)[:, :, 0:1], 0.0))
                step(pool.memset(pair_f[:, :, :], 0.0))
                for m in range(7):
                    h = 1 << m
                    nb = P // (2 * h)
                    odd = pair_f[:, m, :].rearrange("p (b two h) -> p b two h", two=2, h=h)[:, :, 1, :]
                    step(pool.memset(odd, 1.0))
                    select(odd, [[-2 * h, nb], [0, h]], ALU.is_ge, 0, 1)
                    select(odd, [[2 * h, nb], [0, h]], ALU.is_ge, h - 1, -1)
                step(pool.tensor_copy(pair[:, :, :], pair_f[:, :, :]))
                step(pool.memset(far_mask[:, :], 0.0))
                select(far_mask[:, P:2 * P], [[-1, P]], ALU.is_ge, 0, 1, FAR)
                step(pool.memset(before[:, :], 1.0))
                select(before[:, :], [[1, P]], ALU.is_gt, 0, -1)
                pool.iota(iota_row[:, :], pattern=[[1, P]], base=0, channel_multiplier=0,
                          allow_small_or_imprecise_dtypes=True).then_inc(consts2, 1)
                pool.wait_ge(soft_ready, 1)
                step(pool.tensor_tensor(soft[:, 0, :], soft[:, 0, :], soft[:, 1, :], ALU.mult))
                step(pool.tensor_tensor(soft[:, 1, :], soft[:, 0, :], soft[:, 0, :], ALU.mult))
                step(pool.tensor_scalar(soft[:, 2, :], soft[:, 1, :], 1.0 / 19, 1.0 / 17, ALU.mult, ALU.add))
                for k in range(15, 0, -2):
                    step(pool.tensor_tensor(soft[:, 2, :], soft[:, 2, :], soft[:, 1, :], ALU.mult))
                    step(pool.tensor_scalar(soft[:, 2, :], soft[:, 2, :], 1.0 / k, None, ALU.add))
                step(pool.tensor_tensor(soft[:, 2, :], soft[:, 2, :], soft[:, 0, :], ALU.mult))
                step(pool.tensor_scalar(soft[:, 2, :], soft[:, 2, :], -2.0, None, ALU.mult))
                step(pool.tensor_tensor(decay[:, :], soft[:, 2, :], soft[:, 3, :], ALU.add))
                for l in range(DEPTH):
                    lam_init = 0.8 - 0.6 * math.exp(-0.3 * l)
                    step(pool.tensor_scalar(da_g[:, 4 * l:4 * l + 4], vec[:, C_DAN + 4 * l:C_DAN + 4 * l + 4],
                                            1.0 - lam_init, None, ALU.mult))
                step(pool.tensor_scalar(decay_neg[:, :], decay[:, :], -8.0, None, ALU.mult))
                pool.tensor_scalar(decay[:, :], decay[:, :], 8.0, None, ALU.mult).then_inc(decay_done, 1)

        @block.tensor
        def _(pe):
            def product(o, a, b, first, last):
                pe.matmul(o, a[0], b[0], start=first, stop=False, skip_group_check=True)
                pe.matmul(o, a[1], b[0], start=False, stop=False, skip_group_check=True)
                return pe.matmul(o, a[0], b[1], start=False, stop=last, skip_group_check=True)

            def piece(c, width, turns=0):
                _, k, _, n = ring(c, turns)
                pe.wait_ge(lo_ready, n + 1)
                return [t[:, :].rearrange("p (c n) -> p c n", n=width) for t in (w_hi[k], w_lo[k])]

            def transpose_x(n):
                for q in range(2 * TB):
                    t, h = q // 2, q % 2
                    if n == 0:
                        pe.wait_ge(x_in[t], 16)
                        pe.wait_ge(consts, 1)
                    else:
                        pe.wait_ge(x_ready, 2 * TB * (n - 1) + q + 1)
                    for c in range(4):
                        last = pe.transpose(bank[q][:, c * P:(c + 1) * P],
                                            xres[:, t, (4 * h + c) * P:(4 * h + c + 1) * P], ident[:, :])
                    last.then_inc(xT_done, 1)
                pe.wait_ge(xT_lo_ready, 2 * TB * (n + 1))

            def project(l, j):
                w = piece(MIX0[l] + j, 256)
                if j >= 4:
                    pe.wait_ge(taken, NCOL * l + j - 3)
                for g in range(2):
                    for c in range(DC):
                        if ORDER[j] in TOKEN_MAJOR:
                            a = [t[:, c, g * P:(g + 1) * P] for t in actT]
                            b = [t[:, c, :] for t in w]
                        else:
                            a = [t[:, c, g * P:(g + 1) * P] for t in w]
                            b = [t[:, c, :] for t in actT]
                        last = product(bank[j % 4][:, g * 256:(g + 1) * 256], a, b, c == 0, c == DC - 1)
                last.then_inc(used, 1)

            def level(l, m):
                if m == 0:
                    pe.wait_ge(qk_ready, l + 1)
                    a, b = hk[:, :], hq[:, :]
                else:
                    pe.wait_ge(side_done, 8 * l + m)
                    a = b = side[m % 2]
                    pe.wait_ge(level_taken, HG_LEVELS * l + m)
                for h in range(2):
                    r = slice(64 * h, 64 * h + 64)
                    for c in range(2):
                        if m == HG_LEVELS - 1:
                            last = pe.matmul(bank[4 + h][:, c * P:(c + 1) * P], a[r, c * SEQ:c * SEQ + P],
                                             b[r, c * SEQ + P:(c + 1) * SEQ], start=True, stop=True)
                            continue
                        for t in range(TB):
                            at = c * SEQ + t * P
                            o = bank[4 + h][:, t * 256 + c * P:t * 256 + (c + 1) * P]
                            if m == HG_LEVELS - 2:
                                last = pe.matmul(o[0:P // 2, P // 2:P], a[r, at:at + P // 2],
                                                 b[r, at + P // 2:at + P], start=True, stop=True)
                            else:
                                last = pe.matmul(o, a[r, at:at + P], b[r, at:at + P], start=True, stop=True)
                last.then_inc(level_done, 1)

            def lru_gates(l):
                pe.wait_ge(xc_ready, l + 1)
                pe.wait_ge(gate_in, 64)
                for k, g in enumerate((gate_a, gate_x)):
                    for c in range(2):
                        last = pe.matmul(bank[6 + k][:, c * SEQ:(c + 1) * SEQ], g[:, l, c, :], xc[:, c, :],
                                         start=True, stop=True)
                last.then_inc(gates_done, 1)

            def scores(l, r):
                if r == 0:
                    pe.wait_ge(taken, NCOL * l + 9)
                    pe.wait_ge(act_lru, l + 1)
                else:
                    pe.wait_ge(score_taken, 3 * l + r)
                for m in range(2):
                    rows = slice(64 * m, 64 * m + 64)
                    if r < 2:
                        for h in range(2):
                            last = pe.matmul(bank[6 + m][:, h * 256:(h + 1) * 256], dq[rows, 2 * r + h, P:2 * P],
                                             dk[rows, 2 * r + h, :], start=True, stop=True)
                    else:
                        for h in range(DA_HEADS):
                            last = pe.matmul(bank[6 + m][:, h * P:(h + 1) * P], dq[rows, h, 0:P],
                                             dk[rows, h, 0:P], start=True, stop=True)
                last.then_inc(score_done, 1)

            def out_project(l, j, between=None):
                w = piece(MIX0[l] + NCOL + j, D)

                def part(c, t):
                    d = 2 * OUT_ORDER[j] + c
                    for h in range(2):
                        last = product(bank[2 * t + h][:, :], [m[:, d, t * P:(t + 1) * P] for m in mixT],
                                       [v[:, c, h * 512:(h + 1) * 512] for v in w],
                                       j == 0 and c == 0, j == 3 and c == 1)
                    return last

                if j < 3:
                    for c in range(2):
                        for t in range(TB):
                            last = part(c, t)
                        if c == 0 and between is not None:
                            between(l)
                else:
                    for t in range(TB):
                        for c in range(2):
                            last = part(c, t)
                        if t == 0:
                            last.then_inc(early_done, 1)
                last.then_inc(used, 1)

            def hgrn_values(l):
                pe.wait_ge(level_taken, HG_LEVELS * (l + 1))
                for t in range(TB):
                    for u in range(4):
                        head = 2 * (u % 2) + u // 2
                        o = bank[4 + t][:, head * 64:(head + 1) * 64]
                        v = [hv[:, b, head * 64:(head + 1) * 64] for b in range(TB)]
                        last = pe.matmul(o, pairT[:, t, u, :], v[t], start=True, stop=t == 0)
                        if t == 1:
                            last = pe.matmul(o, pairT[:, 2, u, :], v[0], start=False, stop=True)
                last.then_inc(hpv_done, 1)

            def transpose_weights(k, w):
                for h in range(DA_HEADS):
                    last = pe.transpose(bank[k][:, h * P:(h + 1) * P], w[:, h, :], ident[:, :])
                last.then_inc(wT_done, 1)

            for l in range(DEPTH):
                transpose_x(2 * l)
                for j in range(NCOL):
                    project(l, j)
                    if j == 0 and l == 0:
                        pe.wait_ge(vec_in, 16 * 8)
                        pe.transpose(bank[7][:, 0:N_VEC], vec_rows[:, :], ident[0:N_VEC, 0:N_VEC]).then_inc(vecT_done, 1)
                    if j == 3 and l == 0:
                        pe.wait_ge(consts2, 1)
                        pe.wait_ge(lam_done, 1)
                        pe.matmul(bank[7][:, 0:DEPTH], ones[0:1, :], lam_one[:, :], start=True,
                                  stop=True).then_inc(lamB_done, 1)
                    if j in (9, 10):
                        scores(l, j - 9)
                    if j >= 3:
                        level(l, j - 3)
                    if j == 11:
                        scores(l, 2)
                    if j == 4:
                        if l == 0:
                            pe.wait_ge(lam_taken, 1)
                        lru_gates(l)
                pe.wait_ge(taken, NCOL * (l + 1))
                pe.wait_ge(mix_lo, 4 * l + 1)
                out_project(l, 0, hgrn_values)
                pe.wait_ge(score_taken, 3 * l + 3)
                pe.wait_ge(w_done, 3 * l + 2)
                transpose_weights(6, prob1[:, 0, :, P:2 * P])
                transpose_weights(7, prob1[:, 0, :, 0:P])
                pe.wait_ge(hout_done, l + 1)
                for c in range(2):
                    for t in range(TB):
                        last = pe.transpose(bank[4][:, c * SEQ + t * P:c * SEQ + (t + 1) * P],
                                            hout[:, :].rearrange("p (t n) -> p t n", t=TB)[:, t, c * P:(c + 1) * P],
                                            ident[:, :])
                last.then_inc(hT_done, 1)
                pe.wait_ge(w_done, 3 * l + 3)
                transpose_weights(5, prob0[:, 0, :, :])
                pe.wait_ge(wT_taken, 3 * l + 3)
                for t in range(TB):
                    for h in range(DA_HEADS):
                        o = bank[6 + t][:, h * P:(h + 1) * P]
                        v = [dv[h // 2][:, b, (h % 2) * P:(h % 2 + 1) * P] for b in range(TB)]
                        last = pe.matmul(o, pairT[:, t, h, :], v[t], start=True, stop=t == 0)
                        if t == 1:
                            last = pe.matmul(o, pairT[:, 2, h, :], v[0], start=False, stop=True)
                last.then_inc(dpv_done, 1)
                pe.wait_ge(mix_lo, 4 * l + 2)
                out_project(l, 1)
                pe.wait_ge(dout_done, l + 1)
                for h in range(DA_HEADS):
                    for t in range(TB):
                        last = pe.transpose(bank[4 + h // 2][:, (h % 2) * SEQ + t * P:(h % 2) * SEQ + (t + 1) * P],
                                            dout[:, t, h * P:(h + 1) * P], ident[:, :])
                last.then_inc(dT_done, 1)
                pe.wait_ge(mix_lo, 4 * l + 3)
                out_project(l, 2)
                pe.wait_ge(mix_lo, 4 * l + 4)
                out_project(l, 3)
                transpose_x(2 * l + 1)
                if l:
                    continue
                for k in range(4):
                    pe.matmul(bank[4 + k][:, :], zeros[:, :], keep[0][:, :], start=True, stop=False,
                              skip_group_check=True)
                with pe.Fori(0, FB) as fb:
                    for k in range(4):
                        w = piece(DENSE0 + k, 256, fb)
                        for g in range(2):
                            for c in range(DC):
                                last = product(bank[k][:, g * SEQ:(g + 1) * SEQ],
                                               [t[:, c, g * P:(g + 1) * P] for t in w],
                                               [t[:, c, :] for t in actT], c == 0, c == DC - 1)
                        last.then_inc(used, 1)
                    for h in range(2):
                        w = piece(DENSE0 + 4 + h, D, fb)
                        pe.wait_ge(d_lo, 2 * fb + h + 1)
                        for t in range(TB):
                            for c in range(2):
                                for n in range(2):
                                    last = product(bank[4 + 2 * t + n][:, :],
                                                   [m[:, 2 * h + c, t * P:(t + 1) * P] for m in mixT],
                                                   [v[:, c, n * 512:(n + 1) * 512] for v in w], False, True)
                            if t == 0:
                                last.then_inc(dense_early, 1)
                        last.then_inc(used, 1)

            pe.wait_ge(rw_split, 1)
            for c in range(DC):
                last = product(bank[4][0:E, 0:SEQ], [rw_hi[:, c, :], rw_lo[:, c, :]], [a[:, c, :] for a in actT],
                               c == 0, c == DC - 1)
            last.then_inc(logitT_done, 1)
            pe.wait_ge(logitT_taken, 1)
            for t in range(TB):
                last = pe.transpose(bank[5][:, t * E:(t + 1) * E], logitT[:, t * P:(t + 1) * P], ident[0:E, 0:E])
            last.then_inc(logit_done, 1)
            pe.wait_ge(routed_done, 1)
            pe.matmul(bank[4][:, 0:E], before[:, :], routed[:, 0, :], start=True, stop=True)
            pe.matmul(bank[4][:, E:2 * E], before[:, :], routed[:, 1, :], start=True, stop=False)
            pe.matmul(bank[4][:, E:2 * E], all_ones[:, :], routed[:, 0, :], start=False, stop=True)
            pe.matmul(bank[4][:, 2 * E:3 * E], all_ones[:, :], routed[:, 0, :], start=True, stop=False)
            pe.matmul(bank[4][:, 2 * E:3 * E], all_ones[:, :], routed[:, 1, :], start=False,
                      stop=True).then_inc(rank_done, 1)
            for _ in range(14):
                pe.matmul(bank[3][:, :], zeros[:, :], keep[0][:, :], start=True, stop=True)

            hT = [t[:, 0:4 * P].rearrange("p (c t) -> p c t", c=4) for t in (mixT_hi, mixT_lo)]

            def up(c, m, turns, new=None):
                for h in range(2):
                    if new is not None:
                        pe.wait_ge(m_xg_lo, 2 * new + h - 1)
                    w = piece(c + h, 512, turns)
                    for k in range(4):
                        last = product(bank[m][:, :], [a[:, 4 * h + k, :] for a in xg],
                                       [t[:, k, :] for t in w], h + k == 0, h + k == 4)
                    last.then_inc(used, 1)

            def turn(n):
                pe.wait_ge(m_h, n)
                for k in range(4):
                    last = pe.transpose(bank[2][:, k * P:(k + 1) * P], hid[:, k * P:(k + 1) * P], ident[:, :])
                last.then_inc(m_T, 1)

            def down(c, n, turns, end=False):
                pe.wait_ge(m_T_lo, n)
                for h in range(2):
                    w = piece(c + h, D, turns)
                    for k in range(2):
                        for m in range(2):
                            last = product(bank[4 + m][:, :], [t[:, 2 * h + k, :] for t in hT],
                                           [t[:, k, m * 512:(m + 1) * 512] for t in w],
                                           False, end and h + k == 2)
                    last.then_inc(used, 1)

            def gather(n):
                pe.wait_ge(m_pick, n)
                for h in range(2):
                    for t in range(TB):
                        for k, x_part in enumerate((xs_hi, xs_lo)):
                            last = pe.matmul(bank[6 + h][:, :], pick[:, t, :], x_part[:, t, h * 512:(h + 1) * 512],
                                             start=t + k == 0, stop=t + k == 2)
                    last.then_inc(m_gath, 1)
                for t in range(TB):
                    pe.transpose(bank[3][:, t * P:(t + 1) * P], pick[:, t, :].bitcast(f32), ident[:, :])
                for t in range(TB):
                    last = pe.matmul(bank[3][:, SEQ:SEQ + 1], pick[:, t, :].bitcast(f32), gate_tok[:, t:t + 1],
                                     start=t == 0, stop=t == TB - 1)
                last.then_inc(m_pickT, 1)

            def transpose_gathered(n):
                for h in range(2):
                    pe.wait_ge(m_xg_tok, 2 * n + h - 1)
                    for c in range(4):
                        last = pe.transpose(bank[6 + h][:, c * P:(c + 1) * P],
                                            xg_tok[:, (4 * h + c) * P:(4 * h + c + 1) * P], ident[:, :])
                    last.then_inc(m_xgT, 1)

            def scatter(n):
                pe.wait_ge(m_y_lo, n)
                for t in range(TB):
                    for h in range(2):
                        o = bank[4 + 2 * t + h][:, :]
                        pe.matmul(o, pickT[:, t * P:(t + 1) * P], y_hi[:, h * 512:(h + 1) * 512],
                                  start=True, stop=False)
                        pe.matmul(o, pickT[:, t * P:(t + 1) * P], y_lo[:, h * 512:(h + 1) * 512],
                                  start=False, stop=True).then_inc(m_back, 1)

            def start_item(i):
                turn(FB * i + 1)
                up(ITEM0, 1, FB * i)
                pe.wait_ge(m_acc, 4 * i + 4)
                for m in range(2):
                    pe.matmul(bank[4 + m][:, :], zeros[:, :], keep[0][:, :], start=True, stop=False,
                              skip_group_check=True)
                down(ITEM0 + 2, FB * i + 1, FB * i)

            def middle(c, n, turns, next_item=None):
                pe.wait_ge(m_silu, n)
                up(c, 0, turns)
                turn(n)
                if next_item is not None:
                    gather(next_item)
                up(c + 2, 1, turns)
                if next_item is not None:
                    transpose_gathered(next_item)
                down(c + 4, n, turns)

            pe.wait_ge(xs_done, TB)
            gather(1)
            transpose_gathered(1)
            up(MOE0, 0, 0, 1)
            up(MOE0 + 2, 1, 0)
            pe.wait_ge(m_silu, 1)
            up(MOE0 + 4, 0, 0)
            pe.wait_ge(items_done, 1)
            last_item = pe.value_load(item_i[0:1, 0:1], min_val=E - 1, max_val=ITEMS - 1)
            with pe.Fori(0, last_item) as i:
                start_item(i)
                with pe.Fori(2, FB - 1) as fb:
                    middle(ITEM0 + 4, FB * i + fb, FB * i + fb - 2)
                middle(SEAM0 - 6, FB * i + FB - 1, FB * i, i + 2)
                pe.wait_ge(m_silu, FB * i + FB)
                up(SEAM0, 0, FB * i, i + 2)
                turn(FB * i + FB)
                up(SEAM0 + 2, 1, FB * i)
                down(SEAM0 + 4, FB * i + FB, FB * i)
                pe.wait_ge(m_silu, FB * i + FB + 1)
                up(SEAM0 + 6, 0, FB * i)
                scatter(i + 1)
            i = last_item
            start_item(i)
            with pe.Fori(2, FB) as fb:
                middle(ITEM0 + 4, FB * i + fb, FB * i + fb - 2)
            turn(FB * i + FB)
            down(SEAM0, FB * i + FB, FB * i, True)
            scatter(i + 1)

        @block.scalar
        def _(act):
            count = [0]

            def step(ins):
                count[0] += 1
                ins.then_inc(act_step, 1)
                act.wait_ge(act_step, count[0])

            def hi(c, turns=0):
                slot, k, landed, n = ring(c, turns)
                act.wait_ge(full[slot], landed)
                if c >= SLOT_SPLIT:
                    act.wait_ge(used, n - SLOT_SPLIT + 1)
                act.activation(w_hi[k][:, :], raw[slot][:, :], ACT.Copy).then_inc(hi_ready, 1)

            def xT_hi(n):
                for q in range(2 * TB):
                    act.wait_ge(xT_done, 2 * TB * n + q + 1)
                    act.activation(xT_part(0, q), bank[q][:, :].rearrange("p (c t) -> p c t", c=4),
                                   ACT.Copy).then_inc(xT_hi_ready, 1)

            def exps(l, m):
                act.wait_ge(rel_done, 8 * l + m)
                act.activation(rel[m % 2][:, :], rel[m % 2][:, :], ACT.Exp).then_inc(exp_done, 1)

            def norm_std(n):
                for t in range(TB):
                    act.wait_ge(var_done, TB * n + t + 1)
                    act.activation(std[:, t:t + 1], mean_var[:, t, 1:2], ACT.Sqrt,
                                   bias=eps[:, :]).then_inc(ln_std, 1)

            def softmax(l, r):
                act.wait_ge(max_done, 3 * l + r + 1)
                t, heads = round_heads(r)
                for m in range(2):
                    for h in heads:
                        k = 8 * t + 4 * m + h
                        v = (prob0, prob1)[t][:, m, h, :]
                        last = act.activation(v, v, ACT.Exp, bias=row_max[:, k:k + 1], scale=DA_DIM ** -0.5,
                                              accum_out=row_sum[:, k:k + 1])
                last.then_inc(prob_done, 1)

            def take_weights(l, n):
                act.wait_ge(wT_done, 3 * l + n + 1)
                act.activation(pairT[:, (1, 2, 0)[n], :, :],
                               bank[(6, 7, 5)[n]][:, :].rearrange("p (h t) -> p h t", h=4),
                               ACT.Copy).then_inc(wT_taken, 1)

            for l in range(DEPTH):
                if l == 0:
                    hi(0)
                xT_hi(2 * l)
                for c in range(2 if l else 1, 3):
                    hi(MIX0[l] + c)
                for j in range(NCOL):
                    hi(MIX0[l] + j + 3)
                    act.wait_ge(used, MIX0[l] + j + 1)
                    b = bank[j % 4]
                    b3 = b[:, :].rearrange("p (t n) -> p t n", t=2)
                    kind = ORDER[j]
                    if kind == HQ:
                        act.activation(hq[:, :], b[:, :], ACT.Copy)
                        done = act.activation(sig[:, :], b[:, :], ACT.Sigmoid)
                    elif kind == HF:
                        act.activation(logf[:, :], b[:, :], ACT.Sigmoid)
                        done = act.activation(hk[:, :], b[:, :], ACT.Sigmoid, scale=-1.0)
                    elif kind == HI:
                        done = act.activation(hv[:, :, :], b3, ACT.Copy)
                    elif kind == HG:
                        act.activation(hgate, b3, ACT.Copy)
                        done = act.activation(hgate_sig, b3, ACT.Sigmoid)
                    elif kind == LX:
                        if l == 0:
                            act.wait_ge(lx_blank, 1)
                        done = act.activation(lx[:, :, 3:3 + SEQ], b3, ACT.Copy)
                    elif kind == LG:
                        if l == 0:
                            act.wait_ge(consts2, 1)
                        act.activation(lgate, b[:, :], ACT.Copy)
                        done = act.activation(lgelu, b[:, :], ACT.Square)
                    elif kind in (DQ, DQ + 1):
                        h = 2 * (kind - DQ)
                        done = act.activation(dq[:, h:h + 2, :], b3, ACT.Copy)
                    elif kind in (DK, DK + 1):
                        h = 2 * (kind - DK)
                        done = act.activation(dk[:, h:h + 2, :], b3, ACT.Copy)
                    else:
                        done = act.activation(dv[kind - DV], b3, ACT.Copy)
                    done.then_inc(taken, 1)
                    if j == 0 and l == 0:
                        act.wait_ge(vec_done, 1)
                        act.activation(soft[:, 0, :], soft[:, 0, :], ACT.Exp)
                        act.activation(lb_tmp[:, 0:4], lb_tmp[:, 0:4], ACT.Exp)
                        act.activation(lam_sum[:, :], lam_sum[:, :], ACT.Exp).then_inc(lam_exp, 1)
                    if j == 1:
                        act.wait_ge(f_ready, l + 1)
                        act.activation(logf[:, :], logf[:, :], ACT.Ln).then_inc(logf_done, 1)
                    if j == 2:
                        exps(l, 1)
                        exps(l, 2)
                    if 3 <= j <= 8:
                        exps(l, j)
                    if j == 5:
                        act.wait_ge(gates_done, l + 1)
                        for c in range(2):
                            s = slice(c * SEQ, (c + 1) * SEQ)
                            act.activation(lr[:, s], bank[6][:, s], ACT.Sigmoid,
                                           bias=vec[:, C_BA + 2 * l + c:C_BA + 2 * l + c + 1])
                            last = act.activation(li[:, c, :], bank[7][:, s], ACT.Sigmoid,
                                                  bias=vec[:, C_BX + 2 * l + c:C_BX + 2 * l + c + 1])
                        last.then_inc(act_lru, 1)
                        act.wait_ge(act_lru, l + 1)
                        act.wait_ge(gelu_in, l + 1)
                        act.wait_ge(decay_done, 1)
                        act.activation(lgelu, lgelu, ACT.Sigmoid).then_inc(gelu_sig, 1)
                        for c in range(2):
                            s = slice(c * SEQ, (c + 1) * SEQ)
                            act.activation(lt[:, s], lr[:, s], ACT.Tanh,
                                           scale=decay_neg[:, 2 * l + c:2 * l + c + 1])
                            last = act.activation(la[:, s], lr[:, s], ACT.Exp,
                                                  scale=decay[:, 2 * l + c:2 * l + c + 1])
                        last.then_inc(tanh_done, 1)
                    if j == 7:
                        act.wait_ge(root_in, l + 1)
                        act.activation(lt, lt, ACT.Sqrt).then_inc(root_done, 1)
                    if j == 8:
                        act.wait_ge(lru_out, l + 1)
                        act.activation(mixT_hi[:, 2 * SEQ:4 * SEQ], lr[:, :], ACT.Copy).then_inc(lru_hi, 1)
                    if j >= 10:
                        softmax(l, j - 10)
                softmax(l, 2)
                if l == DEPTH - 1:
                    act.wait_ge(rw_in, 16)
                    act.activation(rw_hi[:, :, :], rw[:, :, :], ACT.Copy).then_inc(rw_hi_done, 1)
                act.wait_ge(hpv_done, l + 1)
                for t in range(TB):
                    last = act.activation(hsq[:, t * 256:(t + 1) * 256], bank[4 + t][:, 0:256], ACT.Square)
                last.then_inc(hsq_done, 1)
                act.wait_ge(hms_done, l + 1)
                act.activation(head_r[:, :], head_ms[:, :], ACT.Sqrt, bias=eps[:, :],
                               scale=1.0 / HG_DIM).then_inc(hstd_done, 1)
                hi(MIX0[l] + N_MIX - 1)
                take_weights(l, 0)
                take_weights(l, 1)
                act.wait_ge(hT_done, l + 1)
                for c in range(2):
                    last = act.activation(mixT_hi[:, c * SEQ:(c + 1) * SEQ], bank[4][:, c * SEQ:(c + 1) * SEQ],
                                          ACT.Copy, scale=vec[:, C_HGN + 2 * l + c:C_HGN + 2 * l + c + 1])
                last.then_inc(hT_hi_ready, 1)
                take_weights(l, 2)
                act.wait_ge(dpv_done, l + 1)
                for t in range(TB):
                    for h in range(DA_HEADS):
                        last = act.activation(dsq[:, t, h * P:(h + 1) * P], bank[6 + t][:, h * P:(h + 1) * P],
                                              ACT.Square, accum_out=head_ms[:, 4 * t + h:4 * t + h + 1])
                last.then_inc(dsq_done, 1)
                act.wait_ge(dms_done, l + 1)
                act.activation(head_r[:, :], head_r[:, :], ACT.Sqrt, bias=eps[:, :],
                               scale=1.0 / (2 * DA_DIM)).then_inc(dstd_done, 1)
                act.wait_ge(dT_done, l + 1)
                for h in range(DA_HEADS):
                    last = act.activation(mixT_hi[:, (4 + h) * SEQ:(5 + h) * SEQ],
                                          bank[4 + h // 2][:, (h % 2) * SEQ:(h % 2 + 1) * SEQ], ACT.Copy,
                                          scale=da_g[:, 4 * l + h:4 * l + h + 1])
                    if h % 2:
                        last.then_inc(dT_hi_ready, 1)
                for c in range(2):
                    hi(MIX0[l] + N_MIX + c)

                norm_std(2 * l)
                xT_hi(2 * l + 1)
                if l:
                    continue
                with act.Fori(0, FB) as fb:
                    def hidden(h):
                        act.wait_ge(used, DENSE0 + 2 * h + 2 + SLOT_RAW * fb)
                        act.activation(hid_sig[:, :], bank[2 * h][:, :], ACT.Silu).then_inc(d_silu, 1)
                        act.wait_ge(d_h, 2 * fb + h + 1)
                        act.activation(mixT_hi[:, h * 512:(h + 1) * 512], hid2[h][:, :], ACT.Copy).then_inc(d_hi, 1)

                    for k in range(2, 5):
                        hi(DENSE0 + k, fb)
                    hidden(0)
                    hi(DENSE0 + 5, fb)
                    hidden(1)
                    hi(DENSE0 + 6, fb)
                    hi(DENSE0 + 7, fb)
                norm_std(1)

            for t in range(TB):
                act.activation(xs_hi[:, t, :], xres[:, t, :], ACT.Copy).then_inc(xs_hi_done, 1)
            act.wait_ge(gap_done, 1)
            act.activation(gates[:, 0, :], gates[:, 3, :], ACT.Exp).then_inc(gap_exp, 1)

            def silu(n, done):
                act.wait_ge(used, done)
                act.activation(hid_sig[:, :], bank[0][:, :], ACT.Silu).then_inc(m_silu, 1)

            def turned(n):
                act.wait_ge(m_T, n)
                act.activation(mixT_hi[:, 0:512], bank[2][:, :], ACT.Copy).then_inc(m_T_hi, 1)

            def gathered_rows(n):
                for k in range(2):
                    act.wait_ge(m_gath, 2 * n + k - 1)
                    act.activation(xg_tok[:, k * 512:(k + 1) * 512], bank[6 + k][:, :], ACT.Copy).then_inc(m_xg_tok, 1)

            def gathered(n):
                for k in range(2):
                    act.wait_ge(m_xgT, 2 * n + k - 1)
                    act.activation(actT_hi[:, k * 512:(k + 1) * 512], bank[6 + k][:, :], ACT.Copy).then_inc(m_xg_hi, 1)

            def gathered_pick(n):
                act.wait_ge(m_pickT, n)
                act.activation(pickT[:, :], bank[3][:, 0:SEQ], ACT.Copy)
                act.activation(gate_slot[:, :], bank[3][:, SEQ:SEQ + 1], ACT.Copy).then_inc(m_slot, 1)

            def output(n, done):
                act.wait_ge(used, done)
                act.wait_ge(m_slot, n)
                for k in range(2):
                    last = act.activation(y_hi[:, k * 512:(k + 1) * 512], bank[4 + k][:, :], ACT.Copy,
                                          scale=gate_slot[:, :])
                last.then_inc(m_y_hi, 1)

            def start_item(i):
                hi(ITEM0 + 2, FB * i)
                turned(FB * i + 1)
                hi(ITEM0 + 3, FB * i)
                hi(ITEM0 + 4, FB * i)
                silu(FB * i + 2, ITEM0 + 2 + N_FFN * i)

            def middle(c, n, turns, next_item=None):
                for k in range(1, 5):
                    hi(c + k, turns)
                turned(n)
                if next_item is not None:
                    gathered_rows(next_item)
                hi(c + 5, turns)
                hi(c + 6, turns)
                silu(n + 1, c + 4 + SLOT_RAW * turns)

            hi(MOE0 + 2)
            gathered_rows(1)
            gathered(1)
            gathered_pick(1)
            for k in range(3, 6):
                hi(MOE0 + k)
            silu(1, MOE0 + 4)
            hi(MOE0 + 6)
            hi(MOE0 + 7)
            act.wait_ge(items_done, 1)
            last_item = act.value_load(item_i[0:1, 0:1], min_val=E - 1, max_val=ITEMS - 1)
            with act.Fori(0, last_item) as i:
                start_item(i)
                with act.Fori(2, FB - 1) as fb:
                    middle(ITEM0 + 4, FB * i + fb, FB * i + fb - 2)
                middle(SEAM0 - 6, FB * i + FB - 1, FB * i, i + 2)
                gathered(i + 2)
                for k in range(1, 5):
                    hi(SEAM0 + k, FB * i)
                turned(FB * i + FB)
                hi(SEAM0 + 5, FB * i)
                hi(SEAM0 + 6, FB * i)
                silu(FB * i + FB + 1, SEAM0 + 4 + N_FFN * i)
                hi(SEAM0 + 7, FB * i)
                output(i + 1, SEAM0 + 6 + N_FFN * i)
                hi(SEAM0 + 8, FB * i)
                hi(SEAM0 + 9, FB * i)
                act.wait_ge(m_back, 4 * i + 4)
                gathered_pick(i + 2)
            i = last_item
            start_item(i)
            with act.Fori(2, FB) as fb:
                middle(ITEM0 + 4, FB * i + fb, FB * i + fb - 2)
            hi(SEAM0 + 1, FB * i)
            turned(FB * i + FB)
            output(i + 1, SEAM0 + 2 + N_FFN * i)
            norm_std(3)

        @block.vector
        def _(dve):
            count = [0]

            def step(ins):
                count[0] += 1
                ins.then_inc(dve_step, 1)
                dve.wait_ge(dve_step, count[0])

            def lo(c, turns=0):
                slot, k, _, n = ring(c, turns)
                dve.wait_ge(hi_ready, n + 1)
                dve.tensor_tensor(w_lo[k][:, :], raw[slot][:, :], w_hi[k][:, :].bitcast(f32),
                                  ALU.subtract).then_inc(lo_ready, 1)

            def mark(ins):
                count[0] += 1
                ins.then_inc(dve_step, 1)
                return count[0]

            def xT_lo_part(n, q):
                dve.wait_ge(xT_hi_ready, 2 * TB * n + q + 1)
                dve.tensor_tensor(xT_part(1, q), bank[q][:, :].rearrange("p (c t) -> p c t", c=4),
                                  xT_part(0, q).bitcast(f32), ALU.subtract).then_inc(xT_lo_ready, 1)

            def xT_lo(n):
                for q in range(2 * TB):
                    xT_lo_part(n, q)

            def half(t, h):
                return xres[:, t, h * 512:(h + 1) * 512]

            def norm_statistics(n, t, first=None):
                if first is not None:
                    made = [mark(dve.scalar_tensor_tensor(half(t, h), half(t, h), ALPHA, bank[first + 2 * t + h][:, :],
                                                          ALU.mult, ALU.add)) for h in range(2)]
                for h in range(2):
                    if first is not None:
                        dve.wait_ge(dve_step, made[h])
                    last = mark(dve.bn_stats(stats[:, t, h, :], half(t, h)))
                dve.wait_ge(dve_step, last)
                dve.bn_aggr(mean_var[:, t, :], stats[:, t, :, :].rearrange("p a b -> p (a b)")).then_inc(var_done, 1)

            def norm_apply(n, t):
                dve.wait_ge(norm_in, 32 * (n + 1))
                dve.wait_ge(var_done, TB * n + t + 1)
                made = [mark(dve.scalar_tensor_tensor(half(t, h), half(t, h), mean_var[:, t, 0:1],
                                                      norm_gb[:, 0, h * 512:(h + 1) * 512], ALU.subtract, ALU.mult))
                        for h in range(2)]
                dve.wait_ge(ln_std, TB * n + t + 1)
                r = mark(dve.reciprocal(rstd[:, t:t + 1], std[:, t:t + 1]))
                dve.wait_ge(dve_step, r)
                for h in range(2):
                    dve.scalar_tensor_tensor(half(t, h), half(t, h), rstd[:, t:t + 1],
                                             norm_gb[:, 1, h * 512:(h + 1) * 512], ALU.mult,
                                             ALU.add).then_inc(x_ready, 1)

            def residual_norm(n, first, early, early_count, count_used):
                dve.wait_ge(early, early_count)
                norm_statistics(n, 0, first)
                dve.wait_ge(used, count_used)
                norm_statistics(n, 1, first)
                norm_apply(n, 0)
                norm_apply(n, 1)
                dve.wait_ge(x_ready, 2 * TB * (n + 1))
                dve.sem_inc(norm_used, 1)
                xT_lo(n + 1)

            def relative(l, m):
                h = 1 << (m - 1)
                r = run[0 if h <= 8 else 1 if h <= 32 else 2]
                v, o = [t[:, :].rearrange("p (b two h) -> p b two h", two=2, h=h) for t in (r, rel[m % 2])]
                edge = v[:, :, 0, h - 1:h].to_broadcast((P, 2 * SEQ // (2 * h), h))
                dve.tensor_tensor(o[:, :, 0, :], edge, v[:, :, 0, :], ALU.subtract)
                dve.tensor_tensor(o[:, :, 1, :], v[:, :, 1, :], edge, ALU.subtract).then_inc(rel_done, 1)

            def sides(l, m):
                h = 1 << (m - 1)
                e, o, k, q = [t.rearrange("p (b two h) -> p b two h", two=2, h=h)
                              for t in (rel[m % 2][:, :], side[m % 2], hk[:, :], hq[:, :])]
                dve.wait_ge(exp_done, 8 * l + m)
                if m > 2:
                    dve.wait_ge(level_done, HG_LEVELS * l + m - 1)
                dve.tensor_tensor(o[:, :, 0, :], e[:, :, 0, :], k[:, :, 0, :], ALU.mult)
                dve.tensor_tensor(o[:, :, 1, :], e[:, :, 1, :], q[:, :, 1, :], ALU.mult).then_inc(side_done, 1)
                dve.wait_ge(side_done, 8 * l + m)

            def take_level(l, m):
                dve.wait_ge(level_done, HG_LEVELS * l + m + 1)
                for h in range(2):
                    if m == HG_LEVELS - 1:
                        last = dve.tensor_copy(pairT[:, 2, 2 * h:2 * h + 2, :],
                                               bank[4 + h][:, 0:256].rearrange("p (c t) -> p c t", c=2))
                        continue
                    s = bank[4 + h][:, :].rearrange("p (b c t) -> p b c t", b=2, c=2)
                    o = pairT[:, 0:2, 2 * h:2 * h + 2, :]
                    if m == 0:
                        mask = ident[:, :].unsqueeze(1).unsqueeze(1).to_broadcast((P, 2, 2, P))
                        last = dve.tensor_tensor(o, s, mask, ALU.mult)
                    elif m == HG_LEVELS - 2:
                        last = dve.tensor_copy(o[0:P // 2, :, :, P // 2:P], s[0:P // 2, :, :, P // 2:P])
                    else:
                        mask = pair[:, m - 1, :].unsqueeze(1).unsqueeze(1).to_broadcast((P, 2, 2, P))
                        last = dve.copy_predicated(o, mask, s)
                last.then_inc(level_taken, 1)
                dve.wait_ge(level_taken, HG_LEVELS * l + m + 1)

            def of_round(tile, r):
                t, heads = round_heads(r)
                v = tile[:, 8 * t:8 * t + 8].rearrange("p (m h) -> p m h", m=2)
                return v[:, :, heads[0]:heads[-1] + 1]

            def masked_scores(l, r):
                dve.wait_ge(score_done, 3 * l + r + 1)
                t, heads = round_heads(r)
                width = (t + 1) * P
                p = (prob0, prob1)[t][:, :, heads[0]:heads[-1] + 1, :]
                mask = far_mask[:, 2 * P - width:2 * P].unsqueeze(1).to_broadcast((P, len(heads), width))
                for m in range(2):
                    s = bank[6 + m][:, :].rearrange("p (h k) -> p h k", k=width)
                    last = dve.tensor_tensor(p[:, m, :, :], s, mask, ALU.add)
                last.then_inc(score_taken, 1)
                dve.wait_ge(score_taken, 3 * l + r + 1)
                step(dve.reduce_max(of_round(row_max, r), p, axis=AX))
                dve.tensor_scalar(of_round(row_max, r), of_round(row_max, r), -DA_DIM ** -0.5, None,
                                  ALU.mult).then_inc(max_done, 1)

            def weights(l, r):
                dve.wait_ge(prob_done, 3 * l + r + 1)
                t, heads = round_heads(r)
                step(dve.reciprocal(of_round(row_inv, r), of_round(row_sum, r)))
                c = ratio[:, 4 * t + heads[0]:4 * t + heads[-1] + 1]
                dve.scalar_tensor_tensor(c, of_round(row_sum, r)[:, 0, :], lam_neg[:, l:l + 1],
                                         of_round(row_inv, r)[:, 1, :], ALU.mult, ALU.mult).then_inc(ratio_done, 1)
                dve.wait_ge(ratio_done, 3 * l + r + 1)
                p = (prob0, prob1)[t]
                for h in heads:
                    last = dve.scalar_tensor_tensor(p[:, 0, h, :], p[:, 1, h, :], ratio[:, 4 * t + h:4 * t + h + 1],
                                                    p[:, 0, h, :], ALU.mult, ALU.add)
                last.then_inc(w_done, 1)

            def scale_heads(first, heads, width, o):
                for t in range(TB):
                    s = bank[first + t][:, 0:heads * width].rearrange("p (g w) -> p g w", w=width)
                    r = head_r[:, t * heads:(t + 1) * heads].unsqueeze(2).to_broadcast((P, heads, width))
                    last = dve.tensor_tensor(o[t].rearrange("p (g w) -> p g w", w=width), s, r, ALU.mult)
                return last

            v = vec[:, C_LAM:C_LAM + 2 * DEPTH]

            def parameters():
                dve.wait_ge(vecT_done, 1)
                step(dve.tensor_copy(vec[:, :], bank[7][:, 0:N_VEC]))
                step(dve.tensor_scalar(soft[:, 1, :], v, -1.0, None, ALU.mult))
                step(dve.tensor_tensor(soft[:, 0, :], v, soft[:, 1, :], ALU.min))
                l0, l1 = vec[:, C_LB:C_LB + 2], vec[:, C_LB + 2:C_LB + 4]
                step(dve.tensor_tensor(lb_tmp[:, 4:6], l0, l1, ALU.max))
                step(dve.tensor_tensor(lb_tmp[:, 0:2], l0, lb_tmp[:, 4:6], ALU.subtract))
                step(dve.tensor_tensor(lb_tmp[:, 2:4], l1, lb_tmp[:, 4:6], ALU.subtract))
                dve.wait_ge(lam_in, 64)
                pairs = lam_rows[:, :, :].rearrange("p (m k) n -> p m k n", k=2)
                step(dve.tensor_tensor(lam_prod[:, :, :], pairs[:, :, 0, :], pairs[:, :, 1, :], ALU.mult))
                dve.reduce_sum(lam_sum[:, :], lam_prod[:, :, :].rearrange("p m (l d) -> p (m l) d", d=DA_DIM),
                               axis=AX).then_inc(vec_done, 1)
                lo(3)
                dve.wait_ge(lam_exp, 1)
                step(dve.tensor_tensor(lb_tmp[:, 4:6], lb_tmp[:, 0:2], lb_tmp[:, 2:4], ALU.add))
                step(dve.reciprocal(lb_tmp[:, 4:6], lb_tmp[:, 4:6]))
                step(dve.memset(lb[:, 0, :], 0.0))
                step(dve.tensor_tensor(lb[:, 1, :], lb_tmp[:, 2:4], lb_tmp[:, 4:6], ALU.mult))
                step(dve.tensor_scalar(lb_rest[:, :, :], lb[:, :, :], -1.0, 1.0, ALU.mult, ALU.add))
                for k in range(DEPTH):
                    lam_init = 0.8 - 0.6 * math.exp(-0.3 * k)
                    last = dve.scalar_tensor_tensor(lam_one[:, k:k + 1], lam_sum[:, k:k + 1], lam_init,
                                                    lam_sum[:, DEPTH + k:DEPTH + k + 1], ALU.add, ALU.subtract)
                last.then_inc(lam_done, 1)
                step(dve.tensor_scalar(soft[:, 1, :], soft[:, 0, :], 2.0, None, ALU.add))
                step(dve.tensor_scalar(soft[:, 3, :], v, 0.0, None, ALU.min))
                dve.reciprocal(soft[:, 1, :], soft[:, 1, :]).then_inc(soft_ready, 1)

            for l in range(DEPTH):
                m0 = MIX0[l]
                if l == 0:
                    lo(0)
                    xT_lo(0)
                for c in range(2 if l else 1, 3):
                    lo(m0 + c)
                if l:
                    lo(m0 + 3)
                else:
                    parameters()

                dve.wait_ge(taken, NCOL * l + 2)
                for c in range(2):
                    s = slice(c * SEQ, (c + 1) * SEQ)
                    last = mark(dve.tensor_scalar(logf[:, s], logf[:, s], lb_rest[:, l, c:c + 1], lb[:, l, c:c + 1],
                                                  ALU.mult, ALU.add))
                dve.wait_ge(dve_step, last)
                dve.tensor_scalar(logf[:, :], logf[:, :], 2.0 ** -63, None, ALU.max).then_inc(f_ready, 1)
                for c in range(2):
                    s = slice(c * SEQ, (c + 1) * SEQ)
                    dve.tensor_scalar(hk[:, s], hk[:, s], lb_rest[:, l, c:c + 1], None, ALU.mult)
                dve.tensor_tensor(hq[:, :], hq[:, :], sig[:, :], ALU.mult).then_inc(qk_ready, 1)
                dve.wait_ge(logf_done, l + 1)
                if l == 0:
                    dve.wait_ge(consts2, 1)
                for n in range(3):
                    step(dve.tensor_tensor_scan(run[n][:, :], keep[n][:, :], logf[:, :], 0.0, ALU.mult, ALU.add))
                dve.wait_ge(qk_ready, l + 1)
                relative(l, 1)
                relative(l, 2)
                lo(m0 + 4)
                dve.wait_ge(taken, NCOL * l + 3)
                for j in range(4):
                    made = []
                    for c in range(2):
                        w = vec[:, C_CW + 8 * l + 2 * j + c:C_CW + 8 * l + 2 * j + c + 1]
                        src = lx[:, c, j:j + SEQ]
                        if j == 0:
                            b = vec[:, C_CB + 2 * l + c:C_CB + 2 * l + c + 1]
                            last = mark(dve.tensor_scalar(xc[:, c, :], src, w, b, ALU.mult, ALU.add))
                        else:
                            dve.wait_ge(dve_step, conv_step[c])
                            last = mark(dve.scalar_tensor_tensor(xc[:, c, :], src, w, xc[:, c, :], ALU.mult, ALU.add))
                        made.append(last)
                    conv_step = made
                dve.wait_ge(dve_step, last)
                dve.sem_inc(xc_ready, 1)
                for m in range(1, HG_LEVELS):
                    if m == 1 and l == 0:
                        dve.wait_ge(lamB_done, 1)
                        dve.tensor_scalar(lam_neg[:, :], bank[7][:, 0:DEPTH], -1.0, None, ALU.mult).then_inc(lam_taken, 1)
                    sides(l, m)
                    if m + 2 < HG_LEVELS:
                        relative(l, m + 2)
                    take_level(l, m - 1)
                    lo(m0 + 4 + m)
                    if m == 1:
                        dve.wait_ge(taken, NCOL * l + 4)
                        c1 = 2.0 * math.sqrt(2.0 / math.pi)
                        step(dve.tensor_scalar(lgelu, lgelu, c1 * 0.044715, c1, ALU.mult, ALU.add))
                        dve.tensor_tensor(lgelu, lgelu, lgate, ALU.mult).then_inc(gelu_in, 1)
                    if m == 3:
                        dve.wait_ge(tanh_done, l + 1)
                        dve.wait_ge(gelu_sig, l + 1)
                        step(dve.tensor_tensor(lgate, lgate, lgelu, ALU.mult))
                        step(dve.tensor_tensor(lgelu, la[:, :], la[:, :], ALU.mult))
                        dve.scalar_tensor_tensor(lt, lgelu, 1.0, lt, ALU.add, ALU.mult).then_inc(root_in, 1)
                        step(dve.tensor_tensor(li, li, xc, ALU.mult))
                    if m == 5:
                        dve.wait_ge(root_done, l + 1)
                        step(dve.tensor_tensor(li, li, lt2, ALU.mult))
                        for c in range(2):
                            s = slice(c * SEQ, (c + 1) * SEQ)
                            step(dve.tensor_tensor_scan(lr[:, s], la[:, s], li[:, c, :], 0.0, ALU.mult, ALU.add))
                        dve.tensor_tensor(lr[:, :], lr[:, :], lgate, ALU.mult).then_inc(lru_out, 1)
                    if m == 6:
                        dve.wait_ge(lru_hi, l + 1)
                        s = slice(2 * SEQ, 4 * SEQ)
                        dve.tensor_tensor(mixT_lo[:, s], lr[:, :], mixT_hi[:, s].bitcast(f32),
                                          ALU.subtract).then_inc(mix_lo, 1)
                    if m in (6, 7):
                        masked_scores(l, m - 6)
                    if m == 8:
                        weights(l, 0)
                        take_level(l, m)
                        masked_scores(l, 2)
                lo(m0 + 13)
                weights(l, 1)
                dve.tensor_tensor(hgate, hgate, hgate_sig, ALU.mult).then_inc(hgate_done, 1)
                dve.wait_ge(hsq_done, l + 1)
                dve.reduce_sum(head_ms[:, :], hsq[:, :].rearrange("p (g w) -> p g w", w=HG_DIM),
                               axis=AX).then_inc(hms_done, 1)
                weights(l, 2)
                dve.wait_ge(hstd_done, l + 1)
                step(dve.reciprocal(head_r[:, :], head_r[:, :]))
                step(scale_heads(4, 4, 64, [hout[:, t * 256:(t + 1) * 256] for t in range(TB)]))
                dve.wait_ge(hgate_done, l + 1)
                dve.tensor_tensor(hout[:, :], hout[:, :], hgate.rearrange("p t n -> p (t n)"),
                                  ALU.mult).then_inc(hout_done, 1)
                inv = row_inv[:, :].rearrange("p (t m h) -> p t m h", t=2, m=2)[:, :, 0, :]
                inv2 = ratio[:, :].rearrange("p (t h) -> p t h", t=2)
                dve.wait_ge(w_done, 3 * l + 3)
                step(dve.tensor_tensor(inv2, inv, inv, ALU.mult))
                dve.wait_ge(hT_hi_ready, l + 1)
                for c in range(2):
                    s = slice(c * SEQ, (c + 1) * SEQ)
                    g = vec[:, C_HGN + 2 * l + c:C_HGN + 2 * l + c + 1]
                    last = dve.scalar_tensor_tensor(mixT_lo[:, s], bank[4][:, s], g, mixT_hi[:, s].bitcast(f32),
                                                    ALU.mult, ALU.subtract)
                last.then_inc(mix_lo, 1)
                lo(m0 + 14)
                dve.wait_ge(dsq_done, l + 1)
                dve.tensor_tensor(head_r[:, :], head_ms[:, :], ratio[:, :], ALU.mult).then_inc(dms_done, 1)
                dve.wait_ge(dstd_done, l + 1)
                step(dve.reciprocal(head_r[:, :], head_r[:, :]))
                factor = head_r[:, :].rearrange("p (t h) -> p t h", t=2)
                step(dve.tensor_tensor(factor, factor, inv, ALU.mult))
                scale_heads(6, 4, 128, [dout[:, t, :] for t in range(TB)]).then_inc(dout_done, 1)
                for h in range(DA_HEADS):
                    if h % 2 == 0:
                        dve.wait_ge(dT_hi_ready, 2 * l + h // 2 + 1)
                    s = slice((4 + h) * SEQ, (5 + h) * SEQ)
                    last = dve.scalar_tensor_tensor(mixT_lo[:, s], bank[4 + h // 2][:, (h % 2) * SEQ:(h % 2 + 1) * SEQ],
                                                    da_g[:, 4 * l + h:4 * l + h + 1], mixT_hi[:, s].bitcast(f32),
                                                    ALU.mult, ALU.subtract)
                    if h % 2:
                        last.then_inc(mix_lo, 1)
                lo(m0 + 15)
                lo(m0 + N_MIX)
                if l == DEPTH - 1:
                    dve.wait_ge(rw_hi_done, 1)
                    dve.tensor_tensor(rw_lo[:, :, :], rw[:, :, :], rw_hi[:, :, :].bitcast(f32),
                                      ALU.subtract).then_inc(rw_split, 1)
                residual_norm(2 * l, 0, early_done, l + 1, m0 + N_MIX)
                lo(m0 + N_MIX + 1)
                if l:
                    continue
                with dve.Fori(0, FB) as fb:
                    def hidden(h):
                        dve.wait_ge(d_silu, 2 * fb + h + 1)
                        dve.tensor_tensor(hid2[h][:, :], hid_sig[:, :], bank[2 * h + 1][:, :], ALU.mult).then_inc(d_h, 1)
                        dve.wait_ge(d_hi, 2 * fb + h + 1)
                        s = slice(h * 512, (h + 1) * 512)
                        dve.tensor_tensor(mixT_lo[:, s], hid2[h][:, :], mixT_hi[:, s].bitcast(f32),
                                          ALU.subtract).then_inc(d_lo, 1)

                    for k in range(2, 5):
                        lo(DENSE0 + k, fb)
                    hidden(0)
                    lo(DENSE0 + 5, fb)
                    hidden(1)
                    lo(DENSE0 + 6, fb)
                    lo(DENSE0 + 7, fb)
                residual_norm(1, 4, dense_early, 2 * FB, DENSE0 + N_FFN)

            def x_lo(t):
                dve.wait_ge(xs_hi_done, t + 1)
                dve.tensor_tensor(xs_lo[:, t, :], xres[:, t, :], xs_hi[:, t, :].bitcast(f32),
                                  ALU.subtract).then_inc(xs_done, 1)

            dve.wait_ge(logitT_done, 1)
            dve.tensor_copy(logitT[:, :], bank[4][0:E, 0:SEQ]).then_inc(logitT_taken, 1)
            x_lo(0)
            dve.wait_ge(logit_done, 1)
            step(dve.tensor_copy(logit[:, :, :], bank[5][:, 0:TB * E].rearrange("p (t e) -> p t e", t=TB)))
            for t in range(TB):
                last = mark(dve.max(best[:, t, :], logit[:, t, :]))
            dve.wait_ge(dve_step, last)
            dve.tensor_tensor(gates[:, 3, :], best[:, :, 1], best[:, :, 0], ALU.subtract).then_inc(gap_done, 1)
            for t in range(TB):
                last = mark(dve.max_index(best_at[:, t, :], best[:, t, :], logit[:, t, :]))
            dve.wait_ge(dve_step, last)
            step(dve.tensor_copy(best_f[:, :, :], best_at[:, :, :]))
            for k in range(TOP_K):
                last = mark(dve.tensor_tensor(hot[:, k, :, :], iota_row[:, 0:E].unsqueeze(1).to_broadcast((P, TB, E)),
                                              best_f[:, :, k:k + 1].to_broadcast((P, TB, E)), ALU.is_equal))
            dve.wait_ge(dve_step, last)
            dve.tensor_tensor(routed[:, :, :], hot[:, 0, :, :], hot[:, 1, :, :], ALU.add).then_inc(routed_done, 1)
            dve.wait_ge(routed_done, 1)
            x_lo(1)
            dve.wait_ge(gap_exp, 1)
            step(dve.tensor_scalar(gates[:, 1, :], gates[:, 0, :], 1.0, None, ALU.add))
            step(dve.reciprocal(gates[:, 1, :], gates[:, 1, :]))
            step(dve.tensor_tensor(gates[:, 2, :], gates[:, 0, :], gates[:, 1, :], ALU.mult))
            for t in range(TB):
                last = mark(dve.tensor_scalar(combine[:, t, 0:E], hot[:, 0, t, :], gates[:, 1, t:t + 1], None, ALU.mult))
            dve.wait_ge(dve_step, last)
            for t in range(TB):
                last = mark(dve.scalar_tensor_tensor(combine[:, t, 0:E], hot[:, 1, t, :], gates[:, 2, t:t + 1],
                                                     combine[:, t, 0:E], ALU.mult, ALU.add))
            dve.wait_ge(rank_done, 1)
            rank = bank[4][:, 0:TB * E].rearrange("p (t e) -> p t e", t=TB)
            step(dve.scalar_tensor_tensor(place[:, :, 0:E], rank, 1.0, routed[:, :, :], ALU.add, ALU.mult))
            step(dve.tensor_scalar(place[:, :, 0:E], place[:, :, 0:E], -1.0, None, ALU.add))

            def overflow():
                step(dve.tensor_scalar(over[:, 0, :], bank[4][:, 2 * E:3 * E], float(P), None, ALU.is_gt))
                step(dve.tensor_tensor_scan(over[:, 1, :], ones[:, 0:E], over[:, 0, :], 0.0, ALU.mult, ALU.add))
                step(dve.tensor_copy(item_f[:, 1:1 + E], iota_row[:, 0:E]))
                for k in range(ITEMS - E):
                    step(dve.scalar_tensor_tensor(over_sel[:, :], over[:, 1, :], float(k + 1), over[:, 0, :],
                                                  ALU.is_equal, ALU.mult))
                    sel = over_sel[:, :].unsqueeze(1).to_broadcast((P, TB, E))
                    step(dve.tensor_tensor(over_tmp[:, :, :], combine[:, :, 0:E], sel, ALU.mult))
                    step(dve.reduce_sum(combine[:, :, E + k:E + k + 1], over_tmp[:, :, :], axis=AX))
                    step(dve.scalar_tensor_tensor(over_tmp[:, :, :], place[:, :, 0:E], 1.0 - P, sel, ALU.add, ALU.mult))
                    step(dve.reduce_sum(place[:, :, E + k:E + k + 1], over_tmp[:, :, :], axis=AX))
                    step(dve.tensor_scalar(place[:, :, E + k:E + k + 1], place[:, :, E + k:E + k + 1], -1.0, None, ALU.add))
                    step(dve.tensor_tensor(over_tmp[:, 0, :], iota_row[:, 0:E], over_sel[:, :], ALU.mult))
                    step(dve.reduce_sum(item_f[:, 1 + E + k:2 + E + k], over_tmp[:, 0, :], axis=AX))
                step(dve.tensor_scalar(item_f[:, 0:1], over[:, 1, E - 1:E], float(E - 1), None, ALU.add))
                dve.tensor_copy(item_i[:, :], item_f[:, :]).then_inc(items_done, 1)

            def hidden(n):
                dve.wait_ge(m_silu, n)
                dve.tensor_tensor(hid[:, :], hid_sig[:, :], bank[1][:, :], ALU.mult).then_inc(m_h, 1)

            def turned(n):
                dve.wait_ge(m_T_hi, n)
                dve.tensor_tensor(mixT_lo[:, 0:512], bank[2][:, :], mixT_hi[:, 0:512].bitcast(f32),
                                  ALU.subtract).then_inc(m_T_lo, 1)

            def choose(i):
                for t in range(TB):
                    dve.tensor_scalar(pick[:, t, :], iota_row[:, :], place[:, t, bass.ds(i, 1)], None, ALU.is_equal)
                dve.tensor_copy(gate_tok[:, :], combine[:, :, bass.ds(i, 1)].rearrange(
                    "p t a -> p (t a)")).then_inc(m_pick, 1)

            def gathered(n):
                for k in range(2):
                    s = slice(k * 512, (k + 1) * 512)
                    dve.wait_ge(m_xg_hi, 2 * n + k - 1)
                    dve.tensor_tensor(actT_lo[:, s], bank[6 + k][:, :], actT_hi[:, s].bitcast(f32),
                                      ALU.subtract).then_inc(m_xg_lo, 1)

            def output(n):
                dve.wait_ge(m_y_hi, n)
                for k in range(2):
                    s = slice(k * 512, (k + 1) * 512)
                    last = dve.scalar_tensor_tensor(y_lo[:, s], bank[4 + k][:, :], gate_slot[:, :],
                                                    y_hi[:, s].bitcast(f32), ALU.mult, ALU.subtract)
                last.then_inc(m_y_lo, 1)

            def accumulate(i):
                for t in range(TB):
                    for h in range(2):
                        q = 2 * t + h
                        dve.wait_ge(m_back, 4 * i + q + 1)
                        dve.wait_ge(m_acc, 4 * i + q + 1)
                        s = xres[:, t, h * 512:(h + 1) * 512]
                        dve.tensor_tensor(s, s, bank[4 + q][:, :], ALU.add).then_inc(m_acc, 1)

            def start_item(i):
                lo(ITEM0 + 2, FB * i)
                turned(FB * i + 1)
                lo(ITEM0 + 3, FB * i)
                lo(ITEM0 + 4, FB * i)
                hidden(FB * i + 2)

            def middle(c, n, turns):
                for k in range(1, 5):
                    lo(c + k, turns)
                turned(n)
                lo(c + 5, turns)
                lo(c + 6, turns)
                hidden(n + 1)

            choose(0)
            dve.wait_ge(xs_done, TB)
            dve.tensor_scalar(xres[:, :, :], xres[:, :, :], ALPHA, None, ALU.mult).then_inc(m_acc, 4)
            overflow()
            gathered(1)
            for k in range(2, 7):
                lo(MOE0 + k)
            hidden(1)
            lo(MOE0 + 7)
            dve.wait_ge(items_done, 1)
            last_item = dve.value_load(item_i[0:1, 0:1], min_val=E - 1, max_val=ITEMS - 1)
            with dve.Fori(0, last_item) as i:
                start_item(i)
                choose(i + 1)
                with dve.Fori(2, FB - 1) as fb:
                    middle(ITEM0 + 4, FB * i + fb, FB * i + fb - 2)
                middle(SEAM0 - 6, FB * i + FB - 1, FB * i)
                gathered(i + 2)
                for k in range(1, 5):
                    lo(SEAM0 + k, FB * i)
                turned(FB * i + FB)
                lo(SEAM0 + 5, FB * i)
                lo(SEAM0 + 6, FB * i)
                hidden(FB * i + FB + 1)
                lo(SEAM0 + 7, FB * i)
                output(i + 1)
                lo(SEAM0 + 8, FB * i)
                lo(SEAM0 + 9, FB * i)
                accumulate(i)
            i = last_item
            start_item(i)
            with dve.Fori(2, FB) as fb:
                middle(ITEM0 + 4, FB * i + fb, FB * i + fb - 2)
            lo(SEAM0 + 1, FB * i)
            turned(FB * i + FB)
            output(i + 1)
            accumulate(i)
            dve.wait_ge(m_acc, 4 * last_item + 8)
            for t in range(TB):
                norm_statistics(3, t)
            for t in range(TB):
                norm_apply(3, t)


_INS = ["x", "w_in", "w_out", "hg_lb_logits", "hg_norm_g", "lru_conv_w", "lru_conv_b", "lru_wa", "lru_ba",
        "lru_wx", "lru_bx", "lru_lambda", "da_lq1", "da_lk1", "da_lq2", "da_lk2", "da_norm_g",
        "ln1_g", "ln1_b", "ln2_g", "ln2_b", "ffn_wg", "ffn_wu", "ffn_wd", "router_w", "moe_wg", "moe_wu", "moe_wd"]


def kernel(**inputs):
    import numpy as np
    import concourse.bacc as bacc
    from concourse.bass_utils import run_bass_kernel_spmd

    nc = bacc.Bacc("TRN2", target_bir_lowering=False, num_devices=1)
    arrays, args = {}, []
    for name in _INS:
        a = np.ascontiguousarray(inputs[name])
        arrays[f"in_{name}"] = a
        args.append(nc.dram_tensor(f"in_{name}", a.shape, mybir.dt.from_np(a.dtype), kind="ExternalInput").ap())
    args.append(nc.dram_tensor("out_x", inputs["x"].shape, mybir.dt.float32, kind="ExternalOutput").ap())
    decoder_trunk(nc, *args)
    r = run_bass_kernel_spmd(nc, [arrays], core_ids=[0])
    return r.results[0]["out_x"]
```
